# Optimizing a Trainium2 kernel written in Bass

```python
import math
import jax, jax.numpy as jnp
from jax import lax
import numpy as np
import jax
import jax.numpy as jnp

D_MODEL = 1024
BATCH = 1
SEQ = 512
DEPTH = 2

MIX_WIDTH = D_MODEL
M_HEADS = 4
M_HEAD_DIM = (MIX_WIDTH // 2) // M_HEADS
M_WIDTH = M_HEADS * M_HEAD_DIM
A_HEADS = 8
A_HEAD_DIM = (MIX_WIDTH - M_WIDTH) // A_HEADS
A_WIDTH = A_HEADS * A_HEAD_DIM
D_FF = 4 * D_MODEL
CONV_WIDTH = 5
M_CHUNK = 64
DILATED_PATTERNS = ((128, 1), (512, 4), (2048, 16))
BAND_BLOCK = 64
ROPE_THETA = 10000.0
NORM_EPS = 1e-6
NEG_INF = -1e30
IN_SPLITS = (M_WIDTH, M_WIDTH, M_WIDTH, M_WIDTH, 2 * M_HEADS, 2 * M_HEADS, A_WIDTH, A_WIDTH, A_WIDTH)
IN_WIDTH = 4 * M_WIDTH + 4 * M_HEADS + 3 * A_WIDTH


def rms_norm(x, g):
    xf = x.astype(jnp.float32)
    y = xf * lax.rsqrt(jnp.mean(xf * xf, axis=-1, keepdims=True) + NORM_EPS)
    return (y * g.astype(jnp.float32)).astype(x.dtype)

def rope(t):
    S, D = t.shape[1], t.shape[-1]
    half = D // 2
    inv_freq = ROPE_THETA ** (-jnp.arange(half, dtype=jnp.float32) / half)
    ang = jnp.arange(S, dtype=jnp.float32)[:, None] * inv_freq[None, :]
    cos = jnp.cos(ang)[None, :, None, :]
    sin = jnp.sin(ang)[None, :, None, :]
    tf = t.astype(jnp.float32)
    t1, t2 = tf[..., :half], tf[..., half:]
    return jnp.concatenate([t1 * cos - t2 * sin, t1 * sin + t2 * cos], axis=-1)

def centred_depthwise_conv(x, w):
    K, C = w.shape
    return lax.conv_general_dilated(
        x, w[:, None, :], window_strides=(1,), padding=[(K // 2, K // 2)],
        dimension_numbers=("NWC", "WIO", "NWC"), feature_group_count=C)

def mlstm_chunkwise(q, k, v, li, lf):
    B, H, S, D = q.shape
    L = M_CHUNK
    NC = S // L
    q = q.reshape(B, H, NC, L, D)
    k = k.reshape(B, H, NC, L, D)
    v = v.reshape(B, H, NC, L, D)
    li = li.reshape(B, H, NC, L)
    lf = lf.reshape(B, H, NC, L)
    b = jnp.cumsum(lf, axis=-1)
    b_last = b[..., -1]
    g = b_last[..., None] - b + li
    g_max = jnp.max(g, axis=-1)

    def step(carry, inp):
        C, n, m = carry
        k_c, v_c, g_c, gmax_c, bl_c = inp
        m_new = jnp.maximum(bl_c + m, gmax_c)
        decay = jnp.exp(bl_c + m - m_new)
        w = jnp.exp(g_c - m_new[..., None])
        C_new = decay[..., None, None] * C + jnp.einsum("bhs,bhsk,bhsv->bhkv", w, k_c, v_c)
        n_new = decay[..., None] * n + jnp.einsum("bhs,bhsk->bhk", w, k_c)
        return (C_new, n_new, m_new), (C, n, m)

    init = (jnp.zeros((B, H, D, D), jnp.float32), jnp.zeros((B, H, D), jnp.float32),
            jnp.full((B, H), NEG_INF, jnp.float32))
    xs = (jnp.moveaxis(k, 2, 0), jnp.moveaxis(v, 2, 0), jnp.moveaxis(g, 2, 0),
          jnp.moveaxis(g_max, 2, 0), jnp.moveaxis(b_last, 2, 0))
    _, (C_prev, n_prev, m_prev) = lax.scan(step, init, xs)
    C_prev = jnp.moveaxis(C_prev, 0, 2)
    n_prev = jnp.moveaxis(n_prev, 0, 2)
    m_prev = jnp.moveaxis(m_prev, 0, 2)

    a = b + m_prev[..., None]
    lower = jnp.tril(jnp.ones((L, L), dtype=bool))
    dmat = jnp.where(lower, b[..., :, None] - b[..., None, :] + li[..., None, :], NEG_INF)
    m_t = jnp.maximum(a, jnp.max(dmat, axis=-1))
    s = jnp.einsum("bhnqd,bhnkd->bhnqk", q, k) * jnp.exp(dmat - m_t[..., None])
    inter = jnp.exp(a - m_t)
    num = (jnp.einsum("bhnqk,bhnkd->bhnqd", s, v)
           + inter[..., None] * jnp.einsum("bhnqk,bhnkv->bhnqv", q, C_prev))
    den = jnp.sum(s, axis=-1) + inter * jnp.einsum("bhnqk,bhnk->bhnq", q, n_prev)
    h = num / jnp.maximum(jnp.abs(den), jnp.exp(-m_t))[..., None]
    return h.reshape(B, H, S, D)

def strided_band_attention(q, k, v, dilation, half):
    B, H, S, D = q.shape
    L = S // dilation
    qb_len = math.gcd(L, BAND_BLOCK)
    nb = L // qb_len
    span = qb_len + 2 * half

    def to_strided(t):
        return t.reshape(B, H, L, dilation, D).transpose(0, 1, 3, 2, 4)

    qs = to_strided(q).reshape(B, H, dilation, nb, qb_len, D)
    pad = ((0, 0), (0, 0), (0, 0), (half, half), (0, 0))
    kp = jnp.pad(to_strided(k), pad)
    vp = jnp.pad(to_strided(v), pad)
    idx = (jnp.arange(nb) * qb_len)[:, None] + jnp.arange(span)[None, :]
    kb = kp[:, :, :, idx, :]
    vb = vp[:, :, :, idx, :]
    qpos = (jnp.arange(nb) * qb_len)[:, None, None] + jnp.arange(qb_len)[None, :, None]
    kpos = idx[:, None, :] - half
    valid = (jnp.abs(kpos - qpos) <= half) & (kpos >= 0) & (kpos < L)
    s = jnp.einsum("bhrnqd,bhrnkd->bhrnqk", qs, kb) * (1.0 / math.sqrt(D))
    s = jnp.where(valid, s, NEG_INF)
    m = jnp.max(s, axis=-1)
    p = jnp.exp(s - m[..., None])
    l = jnp.sum(p, axis=-1)
    o = jnp.einsum("bhrnqk,bhrnkd->bhrnqd", p, vb) / l[..., None]

    def from_strided(t):
        tail = t.shape[5:]
        t = jnp.moveaxis(t.reshape((B, H, dilation, L) + tail), 2, 3)
        return t.reshape((B, H, S) + tail)

    return from_strided(o), from_strided(m), from_strided(l)

def dilated_attention(q, k, v):
    outs = [strided_band_attention(q, k, v, d, w // (2 * d)) for (w, d) in DILATED_PATTERNS]
    m_all = jnp.max(jnp.stack([m for (_, m, _) in outs]), axis=0)
    weights = [l * jnp.exp(m - m_all) for (_, m, l) in outs]
    num = sum(w[..., None] * o for w, (o, _, _) in zip(weights, outs))
    return num / sum(weights)[..., None]

def hybrid_layer(x, norm1_g, w_in, conv_w, gate_i_b, gate_f_b, head_norm_g, w_out,
                 norm2_g, w_up, w_down):
    B, S, _ = x.shape
    h = rms_norm(x, norm1_g)
    proj = h @ w_in
    mq, mk, mv, mo, mi, mf, aq, ak, av = jnp.split(
        proj, list(np.cumsum(IN_SPLITS)[:-1]), axis=-1)

    qk = jax.nn.silu(centred_depthwise_conv(jnp.concatenate([mq, mk], axis=-1), conv_w))
    mq, mk = qk[..., :M_WIDTH], qk[..., M_WIDTH:]

    def m_heads(t):
        return t.reshape(B, S, M_HEADS, M_HEAD_DIM).transpose(0, 2, 1, 3).astype(jnp.float32)

    q_m = m_heads(mq)
    k_m = m_heads(mk) * (1.0 / math.sqrt(M_HEAD_DIM))
    v_m = m_heads(mv)
    gi = (mi + gate_i_b).astype(jnp.float32).reshape(B, S, 2, M_HEADS).transpose(2, 0, 3, 1)
    gf = jax.nn.log_sigmoid((mf + gate_f_b).astype(jnp.float32)).reshape(
        B, S, 2, M_HEADS).transpose(2, 0, 3, 1)
    h_fwd = mlstm_chunkwise(q_m, k_m, v_m, gi[0], gf[0])
    flip = lambda t: jnp.flip(t, axis=2)
    h_bwd = flip(mlstm_chunkwise(flip(q_m), flip(k_m), flip(v_m), flip(gi[1]), flip(gf[1])))
    hm = h_fwd + h_bwd
    hm = hm * lax.rsqrt(jnp.mean(hm * hm, axis=-1, keepdims=True) + NORM_EPS)
    hm = hm.transpose(0, 2, 1, 3).reshape(B, S, M_WIDTH) * head_norm_g.astype(jnp.float32)
    y_m = (hm * jax.nn.sigmoid(mo.astype(jnp.float32))).astype(x.dtype)

    def a_heads(t, rotate):
        t = t.reshape(B, S, A_HEADS, A_HEAD_DIM)
        t = rope(t) if rotate else t.astype(jnp.float32)
        return t.transpose(0, 2, 1, 3)

    o_a = dilated_attention(a_heads(aq, True), a_heads(ak, True), a_heads(av, False))
    y_a = o_a.transpose(0, 2, 1, 3).reshape(B, S, A_WIDTH).astype(x.dtype)

    x = x + jnp.concatenate([y_m, y_a], axis=-1) @ w_out

    u = jax.nn.relu(rms_norm(x, norm2_g) @ w_up)
    return x + (u * u) @ w_down

def first_inputs(seed: int = 0) -> dict:
    key = jax.random.key(seed)
    ks = jax.random.split(key, 13)
    f32 = jnp.float32
    nrm = lambda k, shape: jax.random.normal(k, shape, f32)
    x = nrm(ks[0], (BATCH, SEQ, D_MODEL))
    norm1_g = 1.0 + 0.02 * nrm(ks[1], (DEPTH, D_MODEL))
    w_in = nrm(ks[2], (DEPTH, D_MODEL, IN_WIDTH)) * D_MODEL ** -0.5
    conv_w = nrm(ks[3], (DEPTH, CONV_WIDTH, 2 * M_WIDTH)) * CONV_WIDTH ** -0.5
    gate_i_b = 0.1 * nrm(ks[4], (DEPTH, 2 * M_HEADS))
    gate_f_b = (jnp.tile(jnp.linspace(3.0, 6.0, M_HEADS, dtype=f32), 2)[None, :]
                + 0.1 * nrm(ks[5], (DEPTH, 2 * M_HEADS)))
    head_norm_g = 1.0 + 0.02 * nrm(ks[6], (DEPTH, M_WIDTH))
    w_out = nrm(ks[7], (DEPTH, MIX_WIDTH, D_MODEL)) * MIX_WIDTH ** -0.5
    norm2_g = 1.0 + 0.02 * nrm(ks[8], (DEPTH, D_MODEL))
    w_up = nrm(ks[9], (DEPTH, D_MODEL, D_FF)) * D_MODEL ** -0.5
    w_down = nrm(ks[10], (DEPTH, D_FF, D_MODEL)) * D_FF ** -0.5
    final_g = 1.0 + 0.02 * nrm(ks[11], (D_MODEL,))
    return {"x": x, "norm1_g": norm1_g, "w_in": w_in, "conv_w": conv_w,
            "gate_i_b": gate_i_b, "gate_f_b": gate_f_b, "head_norm_g": head_norm_g,
            "w_out": w_out, "norm2_g": norm2_g, "w_up": w_up, "w_down": w_down,
            "final_g": final_g}

def first_block(x, norm1_g, w_in, conv_w, gate_i_b, gate_f_b, head_norm_g, w_out,
              norm2_g, w_up, w_down, final_g):
    for layer in range(DEPTH):
        x = hybrid_layer(x, norm1_g[layer], w_in[layer], conv_w[layer], gate_i_b[layer],
                         gate_f_b[layer], head_norm_g[layer], w_out[layer], norm2_g[layer],
                         w_up[layer], w_down[layer])
    return rms_norm(x, final_g)


DEPTH_2 = 1

CTX_LEN = 256
GRID_W = 64
N_MOD = 6
EPS = 1e-6
DA_HEADS = 8
DA_QK = 64
DA_V = 2 * DA_QK
DA_QK_COLS = DA_HEADS * 2 * DA_QK
DA_WIDTH = DA_HEADS * DA_V
ROPE_FREQS = DA_QK // 4
Q_BLOCK = 128
RW_HEADS = 16
RW_HEAD = 64
RW_WIDTH = RW_HEADS * RW_HEAD
RW_W_LORA = 64
RW_A_LORA = 64
RW_G_LORA = 128
RW_SHIFT_CH = 3 * RW_WIDTH + RW_W_LORA + RW_A_LORA + RW_G_LORA
RW_LN_EPS = 64e-5
L2_EPS = 1e-12
RW_SPLIT_IDX = (RW_WIDTH, 2 * RW_WIDTH, 3 * RW_WIDTH, 3 * RW_WIDTH + RW_W_LORA, 3 * RW_WIDTH + RW_W_LORA + RW_A_LORA)
N_BRANCH = 2
IN_SPLIT_IDX = (DA_QK_COLS, 2 * DA_QK_COLS, 2 * DA_QK_COLS + DA_WIDTH, 2 * DA_QK_COLS + DA_WIDTH + RW_SHIFT_CH)
IN_WIDTH_2 = 2 * DA_QK_COLS + DA_WIDTH + RW_SHIFT_CH + N_BRANCH * D_MODEL
PEER_HEADS = 8
N_KEYS = 128
N_EXPERTS = N_KEYS * N_KEYS
PEER_TOPK = 16
PEER_QDIM = 256
PEER_CHUNK = 128


def rmsnorm(x, g):
    xf = x.astype(jnp.float32)
    y = xf * lax.rsqrt(jnp.mean(xf * xf, axis=-1, keepdims=True) + EPS)
    return (y * g.astype(jnp.float32)).astype(x.dtype)

def modulate(h, shift, scale):
    return h * (1 + scale) + shift

def axial_angles(n_tokens):
    rows = n_tokens // GRID_W
    row = jnp.repeat(jnp.arange(rows, dtype=jnp.float32), GRID_W)
    col = jnp.tile(jnp.arange(GRID_W, dtype=jnp.float32), rows)
    inv = ROPE_THETA ** (-jnp.arange(ROPE_FREQS, dtype=jnp.float32) / ROPE_FREQS)
    return jnp.stack([row[:, None] * inv, col[:, None] * inv], axis=1)

def apply_axial_rope(x, ang):
    xs = x.reshape(x.shape[:-1] + (2, 2, ROPE_FREQS))
    cos = jnp.cos(ang)[:, None, None, :, None, :].astype(x.dtype)
    sin = jnp.sin(ang)[:, None, None, :, None, :].astype(x.dtype)
    x1, x2 = xs[..., 0:1, :], xs[..., 1:2, :]
    out = jnp.concatenate([x1 * cos - x2 * sin, x2 * cos + x1 * sin], axis=-2)
    return out.reshape(x.shape)

def diff_heads(q, k, v, q_g, k_g, ang):
    B, T, _ = q.shape
    q = rmsnorm(q.reshape(B, T, DA_HEADS, 2, DA_QK), q_g)
    k = rmsnorm(k.reshape(B, T, DA_HEADS, 2, DA_QK), k_g)
    if ang is not None:
        q = apply_axial_rope(q, ang)
        k = apply_axial_rope(k, ang)
    q = q.transpose(0, 3, 2, 1, 4)
    k = k.transpose(0, 3, 2, 1, 4)
    v = v.reshape(B, T, DA_HEADS, DA_V).transpose(0, 2, 1, 3)
    return q, k, v

def diff_attention(q, k, v, lam):
    B, _, H, T, d = q.shape
    nb = T // Q_BLOCK
    qb = q.reshape(B, 2, H, nb, Q_BLOCK, d).transpose(3, 0, 1, 2, 4, 5)
    scale = d ** -0.5

    def one_block(q_blk):
        s = jnp.einsum('bmhqd,bmhkd->bmhqk', q_blk, k).astype(jnp.float32) * scale
        p = jax.nn.softmax(s, axis=-1)
        pd = (p[:, 0] - lam * p[:, 1]).astype(v.dtype)
        return jnp.einsum('bhqk,bhkd->bhqd', pd, v)

    o = lax.map(one_block, qb)
    return o.transpose(1, 0, 3, 2, 4).reshape(B, T, H * v.shape[-1])

def diff_post(o, out_g, lam_init):
    B, T, _ = o.shape
    o = rmsnorm(o.reshape(B, T, DA_HEADS, DA_V), out_g) * (1 - lam_init)
    return o.reshape(B, T, DA_WIDTH)

def centred_shift(z, w):
    zp = jnp.pad(z, ((0, 0), (1, 1), (0, 0)))
    return w[0] * zp[:, :-2] + w[1] * zp[:, 1:-1] + w[2] * zp[:, 2:]

def head_l2norm(t):
    th = t.reshape(t.shape[:-1] + (RW_HEADS, RW_HEAD)).astype(jnp.float32)
    th = th * lax.rsqrt(jnp.sum(th * th, axis=-1, keepdims=True) + L2_EPS)
    return th.reshape(t.shape).astype(t.dtype)

def dual(t):
    return jnp.stack([t, t])

def to_scan(t):
    t = jnp.stack([t[0], t[1][:, ::-1]]).astype(jnp.float32)
    return t.reshape(t.shape[:3] + (RW_HEADS, RW_HEAD)).transpose(2, 0, 1, 3, 4)

def from_scan(y):
    y = y.transpose(1, 2, 0, 3, 4)
    return y[0] + y[1][:, ::-1]

def rwkv_prepare(z, shift_w, w0, w_up, a0, a_up, k_k, k_a):
    z = centred_shift(z, shift_w)
    r, k, v, wd, ad, gd = jnp.split(z, RW_SPLIT_IDX, axis=-1)
    w_log = -jax.nn.softplus(-(w0[:, None, None, :] + jnp.einsum('btr,drc->dbtc', jnp.tanh(wd), w_up))) - 0.5
    decay = jnp.exp(-jnp.exp(w_log.astype(jnp.float32)))
    a = jax.nn.sigmoid(a0[:, None, None, :] + jnp.einsum('btr,drc->dbtc', ad, a_up))
    kk = head_l2norm(k * k_k)
    k_eff = k[None] * (1 + (a - 1) * k_a)
    scan_in = (to_scan(decay), to_scan(dual(kk)), to_scan(a), to_scan(k_eff), to_scan(dual(v)), to_scan(dual(r)))
    return scan_in, (r, k, v, gd)

def wkv_scan(s0, scan_in):
    def step(s, inp):
        w, kk, a, k, v, r = inp
        sa = jnp.einsum('dbhij,dbhj->dbhi', s, kk)
        s = s * w[..., None, :] - sa[..., :, None] * (kk * a)[..., None, :] + v[..., :, None] * k[..., None, :]
        return s, jnp.einsum('dbhij,dbhj->dbhi', s, r)
    return lax.scan(step, s0, scan_in)

def rwkv_post(y, r, k, v, gd, g_up, r_k, ln_g, ln_b):
    B, T, C = r.shape
    mu = jnp.mean(y, axis=-1, keepdims=True)
    var = jnp.mean(jnp.square(y - mu), axis=-1, keepdims=True)
    yn = ((y - mu) * lax.rsqrt(var + RW_LN_EPS)).reshape(B, T, C) * ln_g + ln_b
    hs = lambda t: t.reshape(B, T, RW_HEADS, RW_HEAD)
    bonus = jnp.sum(hs(r) * hs(k) * r_k, axis=-1, keepdims=True) * hs(v)
    g = jax.nn.sigmoid(gd) @ g_up
    return (yn.astype(r.dtype) + bonus.reshape(B, T, C)) * g

def merge_branches(o_a, o_b, z_gate, w_branch_a, w_branch_b, w_out):
    g_a, g_b = jnp.split(jax.nn.sigmoid(z_gate), N_BRANCH, axis=-1)
    return (g_a * (o_a @ w_branch_a) + g_b * (o_b @ w_branch_b)) @ w_out

def peer_ffn(h, peer_wq, peer_keys, peer_u, peer_v):
    B, T, D = h.shape
    tok = h.reshape(-1, PEER_CHUNK, D)

    def one_chunk(xc):
        q = (xc @ peer_wq).reshape(PEER_CHUNK, PEER_HEADS, 2, PEER_QDIM // 2)
        s = jnp.einsum('chpd,hpkd->chpk', q, peer_keys).astype(jnp.float32)
        sv, si = lax.top_k(s, PEER_TOPK)
        cand = (sv[..., 0, :, None] + sv[..., 1, None, :]).reshape(PEER_CHUNK, PEER_HEADS, PEER_TOPK * PEER_TOPK)
        cidx = (si[..., 0, :, None] * N_KEYS + si[..., 1, None, :]).reshape(PEER_CHUNK, PEER_HEADS, PEER_TOPK * PEER_TOPK)
        top_s, pos = lax.top_k(cand, PEER_TOPK)
        eidx = jnp.take_along_axis(cidx, pos, axis=-1)
        gate = jax.nn.softmax(top_s, axis=-1)
        act = jax.nn.gelu(jnp.einsum('chkd,cd->chk', peer_u[eidx], xc))
        return jnp.einsum('chk,chkd->cd', (gate * act).astype(xc.dtype), peer_v[eidx])

    return lax.map(one_chunk, tok).reshape(B, T, D)

def hybrid_layer_2(x, ctx, c, c_ctx, w_mod, b_mod, norm1_g, w_in, q_norm_g, k_norm_g, diff_lambda, diff_out_g,
                 rw_shift, rw_w0, rw_w_up, rw_a0, rw_a_up, rw_g_up, rw_k_k, rw_k_a, rw_r_k, rw_ln_g, rw_ln_b,
                 w_branch_a, w_branch_b, w_out, norm2_g, peer_wq, peer_keys, peer_u, peer_v, layer_idx, update_ctx):
    B, S, _ = x.shape
    lam_init = 0.8 - 0.6 * math.exp(-0.3 * layer_idx)
    mod_x = jnp.split((jax.nn.silu(c) @ w_mod + b_mod)[:, None, :], N_MOD, axis=-1)
    mod_c = jnp.split((jax.nn.silu(c_ctx) @ w_mod + b_mod)[None, None, :], N_MOD, axis=-1)
    zx = jnp.split(modulate(rmsnorm(x, norm1_g), mod_x[0], mod_x[1]) @ w_in, IN_SPLIT_IDX, axis=-1)
    zc = jnp.split(modulate(rmsnorm(ctx, norm1_g), mod_c[0], mod_c[1]) @ w_in, IN_SPLIT_IDX, axis=-1)

    qx, kx, vx = diff_heads(zx[0], zx[1], zx[2], q_norm_g, k_norm_g, axial_angles(S))
    qc, kc, vc = diff_heads(zc[0], zc[1], zc[2], q_norm_g, k_norm_g, None)
    lam = jnp.exp(jnp.sum(diff_lambda[0] * diff_lambda[1])) - jnp.exp(jnp.sum(diff_lambda[2] * diff_lambda[3])) + lam_init
    k_all = jnp.concatenate([kc, kx], axis=3)
    v_all = jnp.concatenate([vc, vx], axis=2)
    o_ax = diff_post(diff_attention(qx, k_all, v_all, lam), diff_out_g, lam_init)

    scan_c, aux_c = rwkv_prepare(zc[3], rw_shift, rw_w0, rw_w_up, rw_a0, rw_a_up, rw_k_k, rw_k_a)
    scan_x, aux_x = rwkv_prepare(zx[3], rw_shift, rw_w0, rw_w_up, rw_a0, rw_a_up, rw_k_k, rw_k_a)
    s0 = jnp.zeros((2, B, RW_HEADS, RW_HEAD, RW_HEAD), jnp.float32)
    s_ctx, y_c = wkv_scan(s0, scan_c)
    _, y_x = wkv_scan(s_ctx, scan_x)
    o_bx = rwkv_post(from_scan(y_x), *aux_x, rw_g_up, rw_r_k, rw_ln_g, rw_ln_b)

    x = x + mod_x[2] * merge_branches(o_ax, o_bx, zx[4], w_branch_a, w_branch_b, w_out)
    x = x + mod_x[5] * peer_ffn(modulate(rmsnorm(x, norm2_g), mod_x[3], mod_x[4]), peer_wq, peer_keys, peer_u, peer_v)

    if update_ctx:
        o_ac = diff_post(diff_attention(qc, kc, vc, lam), diff_out_g, lam_init)
        o_bc = rwkv_post(from_scan(y_c), *aux_c, rw_g_up, rw_r_k, rw_ln_g, rw_ln_b)
        ctx = ctx + mod_c[2] * merge_branches(o_ac, o_bc, zc[4], w_branch_a, w_branch_b, w_out)
        ctx = ctx + mod_c[5] * peer_ffn(modulate(rmsnorm(ctx, norm2_g), mod_c[3], mod_c[4]), peer_wq, peer_keys, peer_u, peer_v)
    return x, ctx

def second_inputs(seed: int = 0) -> dict:
    key = jax.random.key(seed)
    ks = iter(jax.random.split(key, 40))
    nrm = lambda shape, s: jax.random.normal(next(ks), shape, jnp.float32) * s
    L, D = DEPTH_2, D_MODEL
    return {
        'x': nrm((BATCH, SEQ, D), 1.0),
        'c': nrm((BATCH, D), 1.0),
        'ctx': nrm((BATCH, CTX_LEN, D), 1.0),
        'c_ctx': nrm((D,), 1.0),
        'w_mod': nrm((L, D, N_MOD * D), D ** -0.5),
        'b_mod': nrm((L, N_MOD * D), 0.01),
        'norm1_g': 1.0 + nrm((L, D), 0.02),
        'w_in': nrm((L, D, IN_WIDTH_2), D ** -0.5),
        'q_norm_g': 1.0 + nrm((L, DA_QK), 0.02),
        'k_norm_g': 1.0 + nrm((L, DA_QK), 0.02),
        'diff_lambda': nrm((L, 4, DA_QK), 0.1),
        'diff_out_g': 1.0 + nrm((L, DA_V), 0.02),
        'rw_shift': jnp.array([0.25, 0.5, 0.25], jnp.float32)[None, :, None] + nrm((L, 3, RW_SHIFT_CH), 0.1),
        'rw_w0': -6.0 + 5.0 * jax.random.uniform(next(ks), (L, 2, RW_WIDTH), jnp.float32),
        'rw_w_up': nrm((L, 2, RW_W_LORA, RW_WIDTH), 0.1 * RW_W_LORA ** -0.5),
        'rw_a0': nrm((L, 2, RW_WIDTH), 0.5),
        'rw_a_up': nrm((L, 2, RW_A_LORA, RW_WIDTH), 0.1 * RW_A_LORA ** -0.5),
        'rw_g_up': nrm((L, RW_G_LORA, RW_WIDTH), RW_G_LORA ** -0.5),
        'rw_k_k': 0.85 + nrm((L, RW_WIDTH), 0.1),
        'rw_k_a': 1.0 + nrm((L, RW_WIDTH), 0.05),
        'rw_r_k': nrm((L, RW_HEADS, RW_HEAD), 0.1),
        'rw_ln_g': 1.0 + nrm((L, RW_WIDTH), 0.02),
        'rw_ln_b': nrm((L, RW_WIDTH), 0.01),
        'w_branch_a': nrm((L, DA_WIDTH, D), DA_WIDTH ** -0.5),
        'w_branch_b': nrm((L, RW_WIDTH, D), RW_WIDTH ** -0.5),
        'w_out': nrm((L, D, D), D ** -0.5),
        'norm2_g': 1.0 + nrm((L, D), 0.02),
        'peer_wq': nrm((L, D, PEER_HEADS * PEER_QDIM), D ** -0.5),
        'peer_keys': nrm((L, PEER_HEADS, 2, N_KEYS, PEER_QDIM // 2), (PEER_QDIM // 2) ** -0.5),
        'peer_u': nrm((L, N_EXPERTS, D), D ** -0.5),
        'peer_v': nrm((L, N_EXPERTS, D), PEER_HEADS ** -0.5),
    }

def second_block(x, c, ctx, c_ctx, w_mod, b_mod, norm1_g, w_in, q_norm_g, k_norm_g, diff_lambda, diff_out_g,
              rw_shift, rw_w0, rw_w_up, rw_a0, rw_a_up, rw_g_up, rw_k_k, rw_k_a, rw_r_k, rw_ln_g, rw_ln_b,
              w_branch_a, w_branch_b, w_out, norm2_g, peer_wq, peer_keys, peer_u, peer_v):
    for l in range(DEPTH_2):
        x, ctx = hybrid_layer_2(
            x, ctx, c, c_ctx, w_mod[l], b_mod[l], norm1_g[l], w_in[l], q_norm_g[l], k_norm_g[l], diff_lambda[l],
            diff_out_g[l], rw_shift[l], rw_w0[l], rw_w_up[l], rw_a0[l], rw_a_up[l], rw_g_up[l], rw_k_k[l], rw_k_a[l],
            rw_r_k[l], rw_ln_g[l], rw_ln_b[l], w_branch_a[l], w_branch_b[l], w_out[l], norm2_g[l], peer_wq[l],
            peer_keys[l], peer_u[l], peer_v[l], layer_idx=l, update_ctx=l < DEPTH_2 - 1)
    return x


def setup_inputs(seed=0):
    out = dict(first_inputs(seed))
    for name, value in second_inputs(seed + 1).items():
        if name != "x":
            out[name + "_2"] = value
    return out


def reference(
    x, norm1_g, w_in, conv_w, gate_i_b, gate_f_b, head_norm_g, w_out, norm2_g, w_up, w_down,
    final_g, c_2, ctx_2, c_ctx_2, w_mod_2, b_mod_2, norm1_g_2, w_in_2, q_norm_g_2, k_norm_g_2,
    diff_lambda_2, diff_out_g_2, rw_shift_2, rw_w0_2, rw_w_up_2, rw_a0_2, rw_a_up_2, rw_g_up_2,
    rw_k_k_2, rw_k_a_2, rw_r_k_2, rw_ln_g_2, rw_ln_b_2, w_branch_a_2, w_branch_b_2, w_out_2,
    norm2_g_2, peer_wq_2, peer_keys_2, peer_u_2, peer_v_2,
):
    x = first_block(
        x, norm1_g, w_in, conv_w, gate_i_b, gate_f_b, head_norm_g, w_out, norm2_g, w_up, w_down,
        final_g,
    )
    return second_block(
        x, c_2, ctx_2, c_ctx_2, w_mod_2, b_mod_2, norm1_g_2, w_in_2, q_norm_g_2, k_norm_g_2,
        diff_lambda_2, diff_out_g_2, rw_shift_2, rw_w0_2, rw_w_up_2, rw_a0_2, rw_a_up_2,
        rw_g_up_2, rw_k_k_2, rw_k_a_2, rw_r_k_2, rw_ln_g_2, rw_ln_b_2, w_branch_a_2,
        w_branch_b_2, w_out_2, norm2_g_2, peer_wq_2, peer_keys_2, peer_u_2, peer_v_2,
    )


_drawn_inputs = setup_inputs


def setup_inputs(seed=0):
    import zlib

    import numpy as np

    out = dict(_drawn_inputs(seed))
    spreads = {}
    factors = {'gate_i_b': 8.0,
     'head_norm_g': 3.387,
     'b_mod_2': 3.077,
     'norm1_g_2': 3.926,
     'q_norm_g_2': 25.964,
     'k_norm_g_2': 25.741,
     'diff_out_g_2': 39.896,
     'rw_w_up_2': 5.708,
     'rw_a_up_2': 4.034,
     'rw_ln_g_2': 54.44,
     'rw_ln_b_2': 64.0,
     'norm2_g_2': 24.112,
     'diff_lambda_2': 3.581,
     'rw_a0_2': 2.791}
    for name, (base, spread) in spreads.items():
        noise = np.random.default_rng([zlib.crc32(name.encode()), seed]).standard_normal(out[name].shape)
        drawn = base * np.exp(spread * noise) if base else spread * noise
        out[name] = jnp.asarray(drawn.astype(out[name].dtype))
    for name, factor in factors.items():
        out[name] = (out[name] * factor).astype(out[name].dtype)
    return out
```

```python
from contextlib import ExitStack

import concourse.bass as bass
from concourse import mybir

F32 = mybir.dt.float32
U32 = mybir.dt.uint32
I32 = mybir.dt.int32
ALU = mybir.AluOpType
ACT = mybir.ActivationFunctionType
AX = mybir.AxisListType

P = 128
D = 1024
DC = D // P
S = 512
ST = S // P
DEPTH = 2
EPS = 1e-6
NEG = -1e30
BANKS = 8
M_HEADS, M_DIM = 4, 128
A_HEADS, A_DIM = 8, 64
FF = 4 * D
NB = 512


class Chain:

    def __init__(self, eng, sem, base=0):
        self.eng, self.sem, self.base, self.n = eng, sem, base, 0

    def after(self, ins):
        self.n += 1
        ins.then_inc(self.sem, 1)
        self.eng.wait_ge(self.sem, self.base + self.n)


class Phase:

    count = 0

    def __init__(self, nc, names):
        self.nc, self.names = nc, names

    def __enter__(self):
        Phase.count += 1
        self.sems = [self.nc.alloc_semaphore(f"{n}_{Phase.count}") for n in self.names]
        self.block = ExitStack()
        block = self.block.enter_context(self.nc.Block())
        return [block] + self.sems

    def __exit__(self, *exc):
        if exc[0] is not None:
            return False
        self.block.close()
        self.nc.clear_and_free_semaphores(self.sems)
        self.nc.all_engine_barrier()
        return False


def load_phase(nc, loads):
    with Phase(nc, ["small_loaded"]) as (block, small_loaded):
        @block.sync
        def _(sp):
            for dst, src in loads:
                sp.dma_start(dst, src).then_inc(small_loaded, 16)
            sp.wait_ge(small_loaded, 16 * len(loads))


def norm_phase(nc, psum, ident, x, tiles, scratch, stats, finish, write_back=None):
    with Phase(nc, ["squares_summed", "root_taken", "rows_scaled", "transposed", "vec_step", "act_step"]) as (
            block, squares_summed, root_taken, rows_scaled, transposed, vec_step, act_step):
        sq, xn = scratch

        @block.scalar
        def _(act):
            chain = Chain(act, act_step)
            for t in range(tiles):
                chain.after(nc.scalar.activation(sq[:, t % 2, :], x[:, t, :], ACT.Square, accum_out=stats[:, 0, t:t + 1]))
            squares = nc.scalar.activation(stats[:, 3, 0:tiles], stats[:, 0, 0:tiles], ACT.Copy, scale=1.0 / D)
            squares.then_inc(squares_summed, 1)
            act.wait_ge(vec_step, 1)
            nc.scalar.activation(stats[:, 1, 0:tiles], stats[:, 0, 0:tiles], ACT.Sqrt).then_inc(root_taken, 1)

        @block.vector
        def _(dve):
            chain = Chain(dve, vec_step)
            dve.wait_ge(squares_summed, 1)
            chain.after(nc.vector.tensor_scalar(stats[:, 0, 0:tiles], stats[:, 3, 0:tiles], EPS, None, ALU.add))
            dve.wait_ge(root_taken, 1)
            chain.after(nc.vector.reciprocal(stats[:, 2, 0:tiles], stats[:, 1, 0:tiles]))
            for t in range(tiles):
                if write_back is None:
                    nc.vector.tensor_scalar(xn[:, t, :], x[:, t, :], stats[:, 2, t:t + 1], None,
                                            ALU.mult).then_inc(rows_scaled, 1)
                else:
                    chain.after(nc.vector.scalar_tensor_tensor(x[:, t, :], x[:, t, :], stats[:, 2, t:t + 1],
                                                               write_back, ALU.mult, ALU.mult))
            if write_back is None:
                for c in range(DC):
                    dve.wait_ge(transposed, c + 1)
                    finish(c, psum[:, c, 0:tiles * P])

        @block.tensor
        def _(pe):
            if write_back is None:
                pe.wait_ge(rows_scaled, tiles)
                for c in range(DC):
                    for t in range(tiles):
                        last = nc.tensor.transpose(psum[:, c, t * P:(t + 1) * P], xn[:, t, c * P:(c + 1) * P], ident[:])
                    last.then_inc(transposed, 1)


def gemm_phase(nc, psum, wbuf, blocks):
    slots = wbuf.shape[1]
    flat = []
    for b, (src, groups) in enumerate(blocks):
        n = src.shape[2]
        for g in groups(wbuf[:, b % slots, :].rearrange("p (c n) -> p c n", c=DC)[:, :, 0:n] if n == NB else
                        wbuf[:, b % slots, 0:DC * n].rearrange("p (c n) -> p c n", c=DC)):
            flat.append((b,) + tuple(g))
    done = {"v": 0, "a": 0}
    order = []
    for g in flat:
        done[g[5]] += 1
        order.append(done[g[5]])
    names = [f"weights_loaded{i}" for i in range(slots)] + ["block_used", "sum_ready", "vec_emptied", "act_emptied",
                                                           "vec_step", "act_step"]
    with Phase(nc, names) as (block, *sems):
        weights_loaded = sems[:slots]
        block_used, sum_ready, vec_emptied, act_emptied, vec_step, act_step = sems[slots:]
        emptied = {"v": vec_emptied, "a": act_emptied}

        @block.sync
        def _(sp):
            for b, (src, _g) in enumerate(blocks):
                if b >= slots:
                    sp.wait_ge(block_used, b - slots + 1)
                n = src.shape[2]
                sp.dma_start(wbuf[:, b % slots, 0:DC * n].rearrange("p (c n) -> p c n", c=DC), src).then_inc(
                    weights_loaded[b % slots], 16)

        @block.tensor
        def _(pe):
            for i, (b, rows, cols, pairs, evac, eng) in enumerate(flat):
                if i == 0 or flat[i - 1][0] != b:
                    pe.wait_ge(weights_loaded[b % slots], 16 * (b // slots + 1))
                if i >= BANKS:
                    pe.wait_ge(emptied[flat[i - BANKS][5]], order[i - BANKS])
                for j, (lhsT, rhs) in enumerate(pairs):
                    last = nc.tensor.matmul(psum[0:rows, i % BANKS, 0:cols], lhsT, rhs, start=(j == 0),
                                            stop=(j == len(pairs) - 1))
                last.then_inc(sum_ready, 1)
                if i + 1 == len(flat) or flat[i + 1][0] != b:
                    pe.wait_ge(sum_ready, i + 1)
                    pe.sem_inc(block_used, 1)

        def empty(which, eng, chain):
            n = 0
            for i, (b, rows, cols, pairs, evac, e) in enumerate(flat):
                if e == which:
                    eng.wait_ge(sum_ready, i + 1)
                    if n:
                        eng.wait_ge(emptied[e], n)
                    n += 1
                    evac(chain, psum[0:rows, i % BANKS, 0:cols]).then_inc(emptied[e], 1)

        @block.vector
        def _(dve):
            empty("v", dve, Chain(dve, vec_step))

        @block.scalar
        def _(act):
            empty("a", act, Chain(act, act_step))


def hybrid_layer(nc, l, T):
    psum, ident, x, wbuf, hT = T["psum"], T["ident"], T["x"], T["wbuf"], T["hT"]
    cols, stats = T["cols"], T["stats"]
    I = T["in"]
    scratch = (T["big"][:, 0:2 * D].rearrange("p (t d) -> p t d", t=2),
               T["big"][:, 2 * D:2 * D + ST * D].rearrange("p (t d) -> p t d", t=ST))

    load_phase(nc, [(cols[:, 0:DC], I["norm1_g"][l]), (cols[:, 8:16], I["norm2_g"][l]),
                    (T["taps"][:], I["conv_w"][l]), (T["gate_b"][:], I["gate_b"][l]),
                    (T["hng"][:], I["head_norm_g"][l].to_broadcast([P, 512]))])

    def scale_chunk(first):
        def finish(c, acc):
            return nc.vector.tensor_scalar(hT[:, c, :], acc, cols[:, first + c:first + c + 1], None, ALU.mult)
        return finish

    norm_phase(nc, psum, ident, x, ST, scratch, stats, scale_chunk(0))
    with ExitStack() as ctx:
        def sb(name, shape, dt=F32):
            return ctx.enter_context(nc.sbuf_tensor(name, shape, dt))
        qkpad = sb("qkpad", [P, 8, S + 4])
        v_ext = sb("v_ext", [P, ST, M_HEADS, M_DIM + 1])
        mo = sb("mo", [P, ST, 512])
        aqk = sb("aqk", [P, 8, S])
        av = sb("av", [P, ST, 512])
        gates = sb("gates", [4, 4, S])
        y = sb("y", [P, ST, D])

        def channel_major(dst):
            def groups(w):
                def evac_v(j):
                    return lambda ch, acc: nc.vector.tensor_copy(dst(j), acc)

                def evac_a(j):
                    return lambda ch, acc: nc.scalar.copy(dst(j), acc)
                return [(P, S, [(w[:, c, j * P:(j + 1) * P], hT[:, c, :]) for c in range(DC)],
                         (evac_v if j % 2 == 0 else evac_a)(j), "va"[j % 2]) for j in range(4)]
            return groups

        def token_major(evac_v, evac_a):
            def groups(w):
                return [(P, NB, [(hT[:, c, t * P:(t + 1) * P], w[:, c, :]) for c in range(DC)],
                         (lambda ch, acc, t=t: evac_v(t, acc)) if t % 2 == 0 else
                         (lambda ch, acc, t=t: evac_a(t, acc)), "va"[t % 2]) for t in range(ST)]
            return groups

        def v_dst(t):
            return v_ext[:, t, :, 0:M_DIM]

        def heads(acc):
            return acc.rearrange("p (h d) -> p h d", h=M_HEADS)

        def gate_groups(w):
            def evac(s_):
                return lambda ch, acc: nc.vector.tensor_scalar(gates[:, s_, :], acc, T["gate_b"][:, s_:s_ + 1], None,
                                                               ALU.add)
            return [(4, S, [(w[:, c, 4 * s_:4 * s_ + 4], hT[:, c, :]) for c in range(DC)], evac(s_), "v")
                    for s_ in range(4)]

        W = I["w_in"]
        blocks = [
            (W[l, 0], channel_major(lambda j: qkpad[:, j, 2:2 + S])),
            (W[l, 1], channel_major(lambda j: qkpad[:, 4 + j, 2:2 + S])),
            (I["w_gates"][l], gate_groups),
            (W[l, 2], token_major(lambda t, acc: nc.vector.tensor_copy(v_dst(t), heads(acc)),
                                  lambda t, acc: nc.scalar.copy(v_dst(t), heads(acc)))),
            (W[l, 3], token_major(lambda t, acc: nc.vector.tensor_copy(mo[:, t, :], acc),
                                  lambda t, acc: nc.scalar.copy(mo[:, t, :], acc))),
            (W[l, 4], channel_major(lambda j: aqk[:, j, :])),
            (W[l, 5], channel_major(lambda j: aqk[:, 4 + j, :])),
            (W[l, 6], token_major(lambda t, acc: nc.vector.tensor_copy(av[:, t, :], acc),
                                  lambda t, acc: nc.scalar.copy(av[:, t, :], acc))),
        ]
        gemm_phase(nc, psum, wbuf, blocks)
        mlstm_phase(nc, T, qkpad, v_ext, mo, gates, y)
        attention_phase(nc, T, aqk, av, y)
        yT = T["hT2"]
        transpose_phase(nc, psum, ident, y, yT)

    def out_groups(half, src, dst):
        def groups(w):
            return [(P, NB, [(src[:, c, t * P:(t + 1) * P], w[:, c, :]) for c in range(DC)],
                     lambda ch, acc, t=t: nc.vector.tensor_tensor(dst[:, t, half * NB:(half + 1) * NB], acc,
                                                                  dst[:, t, half * NB:(half + 1) * NB], ALU.add), "v")
                    for t in range(ST)]
        return groups

    gemm_phase(nc, psum, wbuf, [(I["w_out"][l, n], out_groups(n, yT, x)) for n in range(2)])
    norm_phase(nc, psum, ident, x, ST, scratch, stats, scale_chunk(8))
    with nc.sbuf_tensor("uT", [P, FF // P, S], F32) as uT, nc.sbuf_tensor("relu", [P, 2, S], F32) as relu:
        def up_groups(b):
            def groups(w):
                def evac(j):
                    def f(ch, acc):
                        ch.after(nc.scalar.activation(relu[:, j % 2, :], acc, ACT.Relu))
                        return nc.scalar.activation(uT[:, 4 * b + j, :], relu[:, j % 2, :], ACT.Square)
                    return f
                return [(P, S, [(w[:, c, j * P:(j + 1) * P], hT[:, c, :]) for c in range(DC)], evac(j), "a")
                        for j in range(4)]
            return groups
        gemm_phase(nc, psum, wbuf, [(I["w_up"][l, b], up_groups(b)) for b in range(FF // NB)])
        mlp_down_phase(nc, psum, wbuf, I["w_down"][l], uT, x)


def transpose_phase(nc, psum, ident, src, dst):
    with Phase(nc, ["chunk_transposed"]) as (block, chunk_transposed):
        @block.tensor
        def _(pe):
            for c in range(DC):
                for t in range(ST):
                    last = nc.tensor.transpose(psum[:, c, t * P:(t + 1) * P], src[:, t, c * P:(c + 1) * P], ident[:])
                last.then_inc(chunk_transposed, 1)

        @block.vector
        def _(dve):
            for c in range(0, DC, 2):
                dve.wait_ge(chunk_transposed, c + 1)
                nc.vector.tensor_copy(dst[:, c, :], psum[:, c, :])

        @block.scalar
        def _(act):
            for c in range(1, DC, 2):
                act.wait_ge(chunk_transposed, c + 1)
                nc.scalar.copy(dst[:, c, :], psum[:, c, :])


def mlp_down_phase(nc, psum, wbuf, w_down, uT, x):
    slots = wbuf.shape[1]
    KB = FF // P // DC
    with Phase(nc, [f"weights_loaded{i}" for i in range(slots)] + ["block_used", "sum_ready"]) as (block, *sems):
        weights_loaded, (block_used, sum_ready) = sems[:slots], sems[slots:]

        @block.sync
        def _(sp):
            for b in range(2 * KB):
                if b >= slots:
                    sp.wait_ge(block_used, b - slots + 1)
                sp.dma_start(wbuf[:, b % slots, :].rearrange("p (c n) -> p c n", c=DC),
                             w_down[b // KB, b % KB]).then_inc(weights_loaded[b % slots], 16)

        @block.tensor
        def _(pe):
            for b in range(2 * KB):
                half, kb = divmod(b, KB)
                w = wbuf[:, b % slots, :].rearrange("p (c n) -> p c n", c=DC)
                pe.wait_ge(weights_loaded[b % slots], 16 * (b // slots + 1))
                for t in range(ST):
                    for c in range(DC):
                        last = nc.tensor.matmul(psum[:, half * ST + t, :], uT[:, kb * DC + c, t * P:(t + 1) * P],
                                                w[:, c, :], start=(kb == 0 and c == 0),
                                                stop=(kb == KB - 1 and c == DC - 1))
                    if kb == KB - 1 and t < ST - 1:
                        last.then_inc(sum_ready, 1)
                if kb == KB - 1:
                    last.then_inc(sum_ready, 1)
                    pe.wait_ge(sum_ready, ST * (half + 1))
                    pe.sem_inc(block_used, 1)
                else:
                    last.then_inc(block_used, 1)

        @block.vector
        def _(dve):
            for half in range(2):
                for t in range(ST):
                    dve.wait_ge(sum_ready, half * ST + t + 1)
                    dst = x[:, t, half * NB:(half + 1) * NB]
                    nc.vector.tensor_tensor(dst, psum[:, half * ST + t, :], dst, ALU.add)


def mlstm_phase(nc, T, qkpad, v_ext, mo, gates, y):
    psum, ident = T["psum"], T["ident"]
    taps, hng, maskF, maskB, selneg = T["taps"], T["hng"], T["maskF"], T["maskB"], T["selneg"]
    SCALE = M_DIM ** -0.5
    with ExitStack() as ctx:
        def sb(name, shape, dt=F32):
            return ctx.enter_context(nc.sbuf_tensor(name, shape, dt))
        qk = T["big"][:, 0:8 * S].rearrange("p (j s) -> p j s", j=8)
        conv = sb("conv", [P, 2, S])
        lse = sb("lse", [4, 2, S])
        G = sb("G", [4, 2, S])
        F = sb("F", [4, 2, S])
        M = sb("M", [4, 2, S])
        E = sb("E", [4, 2, S])
        gcol = sb("gcol", [P, 2, 2, ST, 4])
        wt = sb("wt", [P, 2, S])
        we = sb("we", [P, 2, S])
        prod = T["big"][:, 8 * S:16 * S].rearrange("p (b j s) -> p b j s", b=2, j=ST)
        den = sb("den", [P, 2, ST])
        hm = sb("hm", [P, ST, M_DIM])
        junk = sb("junk", [P, M_DIM])
        ss = sb("ss", [P, 3, ST])
        names = ["pads_zero", "convolved", "activated", "logs_taken", "floor_taken", "gates_ready", "cols_transposed",
                 "cols_copied", "scores_ready", "scores_used", "maxima_ready", "exponents_ready", "weights_ready",
                 "prod_ready", "values_ready", "values_used", "squares_ready", "root_taken", "gate_opened",
                 "vec_step", "act_step"]
        with Phase(nc, names) as (block, pads_zero, convolved, activated, logs_taken, floor_taken, gates_ready,
                                  cols_transposed, cols_copied, scores_ready, scores_used, maxima_ready,
                                  exponents_ready, weights_ready, prod_ready, values_ready, values_used,
                                  squares_ready, root_taken, gate_opened, vec_step, act_step):

            @block.gpsimd
            def _(pool):
                nc.gpsimd.memset(qkpad[:, :, 0:2], 0.0).then_inc(pads_zero, 1)
                nc.gpsimd.memset(qkpad[:, :, S + 2:S + 4], 0.0).then_inc(pads_zero, 1)
                nc.gpsimd.memset(v_ext[:, :, :, M_DIM:M_DIM + 1], 1.0).then_inc(pads_zero, 1)

            @block.vector
            def _(dve):
                chain = Chain(dve, vec_step)
                dve.wait_ge(logs_taken, 1)
                chain.after(nc.vector.scalar_tensor_tensor(lse[:], gates[:, 2:4, :], 0.0, lse[:], ALU.min, ALU.subtract))
                ones = wt[0:4, 0, :]
                chain.after(nc.vector.memset(ones, 1.0))
                for d in range(2):
                    def run(ap):
                        return ap if d == 0 else ap[:, ::-1]
                    chain.after(nc.vector.tensor_tensor_scan(run(F[:, d, :]), ones, run(lse[:, d, :]), 0.0, ALU.mult,
                                                             ALU.add))
                    chain.after(nc.vector.tensor_tensor(G[:, d, :], gates[:, d, :], F[:, d, :], ALU.subtract))
                    chain.after(nc.vector.tensor_tensor_scan(run(M[:, d, :]), ones, run(G[:, d, :]), -3e38, ALU.mult,
                                                             ALU.max))
                    chain.after(nc.vector.tensor_tensor(E[:, d, :], F[:, d, :], M[:, d, :], ALU.add))
                dve.sem_inc(gates_ready, 1)
                dve.wait_ge(pads_zero, 3)
                for j in range(8):
                    c = conv[:, j % 2, :]
                    if j >= 2:
                        dve.wait_ge(activated, j - 1)
                    chain.after(nc.vector.tensor_scalar(c, qkpad[:, j, 0:S], taps[:, 8 * 0 + j:8 * 0 + j + 1], None,
                                                        ALU.mult))
                    for k in range(1, 5):
                        ins = nc.vector.scalar_tensor_tensor(c, qkpad[:, j, k:k + S], taps[:, 8 * k + j:8 * k + j + 1],
                                                             c, ALU.mult, ALU.add)
                        if k < 4:
                            chain.after(ins)
                    ins.then_inc(convolved, 1)
                dve.wait_ge(cols_transposed, 1)
                nc.vector.tensor_copy(gcol[:], psum[:, 7, 0:64].rearrange("p (a d t h) -> p a d t h", a=2, d=2, t=ST)
                                      ).then_inc(cols_copied, 1)
                dve.wait_ge(cols_copied, 1)
                dve.wait_ge(gate_opened, 1)
                for t in range(ST):
                    chain.after(nc.vector.tensor_tensor(mo[:, t, :], mo[:, t, :], hng[:], ALU.mult))
                u = 0
                for h in range(M_HEADS):
                    for d in range(2):
                        n = 2 * h + d
                        dve.wait_ge(maxima_ready, n + 1)
                        for j in range(ST):
                            lo, hi = (j * P, S) if d == 0 else (0, (j + 1) * P)
                            mask = maskF[:, 0:S - j * P] if d == 0 else maskB[:, S - (j + 1) * P:S]
                            if u >= 2:
                                dve.wait_ge(weights_ready, u - 1)
                            nc.vector.scalar_tensor_tensor(wt[:, u % 2, lo:hi], psum[:, 4, lo:hi],
                                                           gcol[:, 0, d, j, h:h + 1], mask, ALU.add, ALU.add
                                                           ).then_inc(exponents_ready, 1)
                            u += 1
                            dve.wait_ge(weights_ready, u)
                            if j == 0:
                                dve.wait_ge(scores_ready, h + 1)
                                if n >= 2:
                                    dve.wait_ge(values_ready, n - 1)
                            nc.vector.scalar_tensor_tensor(prod[:, n % 2, j, lo:hi], psum[:, j, lo:hi], SCALE,
                                                           we[:, (u - 1) % 2, lo:hi], ALU.mult, ALU.mult
                                                           ).then_inc(prod_ready, 1)
                        dve.wait_ge(values_ready, n + 1)
                        O = psum[:, 5:7, :].rearrange("p b (i c) -> p b i c", i=2)
                        dn = den[:, 0, :].rearrange("p (b i) -> p b i", b=2)
                        neg = den[:, 1, :].rearrange("p (b i) -> p b i", b=2)
                        chain.after(nc.vector.tensor_scalar(neg, O[:, :, :, M_DIM], -1.0, None, ALU.mult))
                        chain.after(nc.vector.tensor_tensor(dn, O[:, :, :, M_DIM], neg, ALU.max))
                        chain.after(nc.vector.tensor_tensor(den[:, 0, :], den[:, 0, :], gcol[:, 1, d, :, h], ALU.max))
                        chain.after(nc.vector.reciprocal(den[:, 1, :], den[:, 0, :]))
                        for t in range(ST):
                            o = O[:, t // 2, t % 2, 0:M_DIM]
                            if d == 0:
                                chain.after(nc.vector.tensor_scalar(hm[:, t, :], o, den[:, 1, t:t + 1], None, ALU.mult))
                            else:
                                chain.after(nc.vector.scalar_tensor_tensor(hm[:, t, :], o, den[:, 1, t:t + 1],
                                                                           hm[:, t, :], ALU.mult, ALU.add))
                        dve.sem_inc(values_used, 1)
                    for t in range(ST):
                        chain.after(nc.vector.tensor_tensor(junk[:], hm[:, t, :], hm[:, t, :], ALU.mult))
                        chain.after(nc.vector.reduce_sum(ss[:, 0, t:t + 1], junk[:], AX.X))
                    nc.vector.tensor_scalar(ss[:, 1, :], ss[:, 0, :], 1.0 / M_DIM, EPS, ALU.mult, ALU.add
                                            ).then_inc(squares_ready, 1)
                    dve.wait_ge(root_taken, h + 1)
                    chain.after(nc.vector.reciprocal(ss[:, 0, :], ss[:, 2, :]))
                    for t in range(ST):
                        ins = nc.vector.scalar_tensor_tensor(y[:, t, h * M_DIM:(h + 1) * M_DIM], hm[:, t, :],
                                                             ss[:, 0, t:t + 1], mo[:, t, h * M_DIM:(h + 1) * M_DIM],
                                                             ALU.mult, ALU.mult)
                    chain.after(ins)

            @block.scalar
            def _(act):
                chain = Chain(act, act_step)
                z = gates[:, 2:4, :]
                chain.after(nc.scalar.activation(lse[:], z, ACT.Abs))
                chain.after(nc.scalar.activation(lse[:], lse[:], ACT.Exp, scale=-1.0))
                nc.scalar.activation(lse[:], lse[:], ACT.Ln, bias=T["one"][0:4, :]).then_inc(logs_taken, 1)
                act.wait_ge(gates_ready, 1)
                nc.scalar.activation(E[:], E[:], ACT.Exp, scale=-1.0).then_inc(floor_taken, 1)
                nc.scalar.activation(mo[:], mo[:], ACT.Sigmoid).then_inc(gate_opened, 1)
                for j in range(8):
                    act.wait_ge(convolved, j + 1)
                    nc.scalar.activation(qk[:, j, :], conv[:, j % 2, :], ACT.Silu).then_inc(activated, 1)
                u = 0
                for h in range(M_HEADS):
                    for d in range(2):
                        for j in range(ST):
                            lo, hi = (j * P, S) if d == 0 else (0, (j + 1) * P)
                            act.wait_ge(exponents_ready, u + 1)
                            if u >= 2:
                                act.wait_ge(prod_ready, u - 1)
                            nc.scalar.activation(we[:, u % 2, lo:hi], wt[:, u % 2, lo:hi], ACT.Exp
                                                 ).then_inc(weights_ready, 1)
                            u += 1
                    act.wait_ge(squares_ready, h + 1)
                    nc.scalar.activation(ss[:, 2, :], ss[:, 1, :], ACT.Sqrt).then_inc(root_taken, 1)

            @block.tensor
            def _(pe):
                pe.wait_ge(floor_taken, 1)
                for a, src in enumerate((G, E)):
                    for d in range(2):
                        for t in range(ST):
                            k = ((a * 2 + d) * ST + t) * 4
                            last = nc.tensor.transpose(psum[:, 7, k:k + 4], src[:, d, t * P:(t + 1) * P],
                                                       ident[0:4, 0:4])
                last.then_inc(cols_transposed, 1)
                pe.wait_ge(activated, 8)
                for h in range(M_HEADS):
                    if h >= 1:
                        pe.wait_ge(prod_ready, 8 * h)
                    for j in range(ST):
                        last = nc.tensor.matmul(psum[:, j, :], qk[:, 4 + h, j * P:(j + 1) * P], qk[:, h, :],
                                                start=True, stop=True)
                    last.then_inc(scores_ready, 1)
                    for d in range(2):
                        n = 2 * h + d
                        if n >= 1:
                            pe.wait_ge(exponents_ready, 4 * n)
                        nc.tensor.matmul(psum[:, 4, :], selneg[:, h, :], M[:, d, :], start=True, stop=True
                                         ).then_inc(maxima_ready, 1)
                        pe.wait_ge(prod_ready, 4 * (n + 1))
                        if n >= 1:
                            pe.wait_ge(values_used, n)
                        for t in range(ST):
                            src = list(range(0, t + 1)) if d == 0 else list(range(t, ST))
                            for k, j in enumerate(src):
                                last = nc.tensor.matmul(psum[:, 5 + t // 2, (t % 2) * 256:(t % 2) * 256 + M_DIM + 1],
                                                        prod[:, n % 2, j, t * P:(t + 1) * P], v_ext[:, j, h, :],
                                                        start=(k == 0), stop=(k == len(src) - 1))
                        last.then_inc(values_ready, 1)


def attention_phase(nc, T, aqk, av, y):
    psum, ident, rot, cosT, sinT, amask = T["psum"], T["ident"], T["rot"], T["cosT"], T["sinT"], T["amask"]
    SCALE = A_DIM ** -0.5
    UNITS = A_HEADS * ST
    with ExitStack() as ctx:
        def sb(name, shape, dt=F32):
            return ctx.enter_context(nc.sbuf_tensor(name, shape, dt))
        turned = sb("turned", [P, 8, S])
        part = sb("part", [P, 2, S])
        sc = sb("sc", [P, 2, S])
        pr = sb("pr", [P, 2, S])
        pT = sb("pT", [P, 2, S])
        st = sb("st", [P, 4, UNITS])
        names = ["rotated", "turned_ready", "scores_ready", "scores_masked", "probs_ready", "probs_turned",
                 "turned_copied", "values_ready", "out_ready", "vec_step"]
        with Phase(nc, names) as (block, rotated, turned_ready, scores_ready, scores_masked, probs_ready,
                                  probs_turned, turned_copied, values_ready, out_ready, vec_step):
            @block.tensor
            def _(pe):
                for j in range(8):
                    nc.tensor.matmul(psum[:, j, :], rot[:], aqk[:, j, :], start=True, stop=True).then_inc(rotated, 1)
                pe.wait_ge(turned_ready, 8)

                def scores(u):
                    h, i = divmod(u, ST)
                    lo = 64 * (h % 2)
                    if u >= 2:
                        pe.wait_ge(scores_masked, u - 1)
                    nc.tensor.matmul(psum[:, u % 2, :], turned[lo:lo + 64, h // 2, i * P:(i + 1) * P],
                                     turned[lo:lo + 64, 4 + h // 2, :], start=True, stop=True).then_inc(scores_ready, 1)

                def turn(u):
                    pe.wait_ge(probs_ready, u + 1)
                    if u >= 2:
                        pe.wait_ge(turned_copied, u - 1)
                    for k in range(ST):
                        last = nc.tensor.transpose(psum[:, 2 + u % 2, k * P:(k + 1) * P],
                                                   pr[:, u % 2, k * P:(k + 1) * P], ident[:])
                    last.then_inc(probs_turned, 1)

                def values(u):
                    h, i = divmod(u, ST)
                    pe.wait_ge(turned_copied, u + 1)
                    if u >= 2:
                        pe.wait_ge(out_ready, u - 1)
                    for k in range(ST):
                        last = nc.tensor.matmul(psum[:, 4 + u % 2, 0:A_DIM], pT[:, u % 2, k * P:(k + 1) * P],
                                                av[:, k, h * A_DIM:(h + 1) * A_DIM], start=(k == 0), stop=(k == ST - 1))
                    last.then_inc(values_ready, 1)

                scores(0)
                for u in range(UNITS + 1):
                    if u + 1 < UNITS:
                        scores(u + 1)
                    if u < UNITS:
                        turn(u)
                    if u >= 1:
                        values(u - 1)

            @block.vector
            def _(dve):
                chain = Chain(dve, vec_step)
                for j in range(8):
                    dve.wait_ge(rotated, j + 1)
                    if j >= 1:
                        dve.wait_ge(turned_ready, j)
                    chain.after(nc.vector.tensor_tensor(part[:, 0, :], psum[:, j, :], sinT[:], ALU.mult))
                    chain.after(nc.vector.tensor_tensor(part[:, 1, :], aqk[:, j, :], cosT[:], ALU.mult))
                    nc.vector.tensor_tensor(turned[:, j, :], part[:, 0, :], part[:, 1, :], ALU.add
                                            ).then_inc(turned_ready, 1)

                def mask(u):
                    dve.wait_ge(scores_ready, u + 1)
                    if u >= 2:
                        dve.wait_ge(probs_ready, u - 1)
                    chain.after(nc.vector.scalar_tensor_tensor(sc[:, u % 2, :], psum[:, u % 2, :], SCALE,
                                                               amask[:, u % ST, :], ALU.mult, ALU.add))
                    nc.vector.tensor_reduce(st[:, 0, u:u + 1], sc[:, u % 2, :], AX.X, ALU.max, negate=True
                                            ).then_inc(scores_masked, 1)

                def out(u):
                    h, i = divmod(u, ST)
                    chain.after(nc.vector.reciprocal(st[:, 2, u:u + 1], st[:, 1, u:u + 1]))
                    dve.wait_ge(values_ready, u + 1)
                    nc.vector.tensor_scalar(y[:, i, 512 + h * A_DIM:512 + (h + 1) * A_DIM], psum[:, 4 + u % 2, 0:A_DIM],
                                            st[:, 2, u:u + 1], None, ALU.mult).then_inc(out_ready, 1)

                mask(0)
                for u in range(UNITS + 1):
                    if u + 1 < UNITS:
                        mask(u + 1)
                    if u >= 1:
                        out(u - 1)

            @block.scalar
            def _(act):
                def probs(u):
                    act.wait_ge(scores_masked, u + 1)
                    if u >= 2:
                        act.wait_ge(probs_turned, u - 1)
                    nc.scalar.activation(pr[:, u % 2, :], sc[:, u % 2, :], ACT.Exp, bias=st[:, 0, u:u + 1],
                                         accum_out=st[:, 1, u:u + 1]).then_inc(probs_ready, 1)

                def copy(u):
                    act.wait_ge(probs_turned, u + 1)
                    if u >= 2:
                        act.wait_ge(values_ready, u - 1)
                    nc.scalar.copy(pT[:, u % 2, :], psum[:, 2 + u % 2, :]).then_inc(turned_copied, 1)

                probs(0)
                for u in range(UNITS):
                    if u + 1 < UNITS:
                        probs(u + 1)
                    copy(u)


def constants():
    import numpy as np
    f = np.float32
    out = {"ident": np.eye(P, dtype=f)}
    p, q = np.arange(P)[:, None], np.arange(S)[None, :]
    out["maskF"] = np.where((q < P) & (q < p), NEG, 0.0).astype(f)
    out["maskB"] = np.where((q >= S - P) & (q - (S - P) > p), NEG, 0.0).astype(f)
    sel = np.zeros((4, 4, P), f)
    for h in range(4):
        sel[h, h, :] = -1.0
    out["selneg"] = sel
    rot = np.zeros((P, P), f)
    for m in range(P):
        if m % 64 < 32:
            rot[m + 32, m] = -1.0
        else:
            rot[m - 32, m] = 1.0
    out["rot"] = rot
    inv = (f(10000.0) ** (-np.arange(32, dtype=f) / f(32))).astype(f)
    ang = np.arange(S, dtype=f)[None, :] * inv[np.arange(P) % 32][:, None]
    out["cosT"], out["sinT"] = np.cos(ang).astype(f), np.sin(ang).astype(f)
    qq, kk = np.arange(S)[:, None], np.arange(S)[None, :]
    dd = np.abs(qq - kk)
    cnt = (dd <= 64).astype(int) + ((dd % 4 == 0) & (dd <= 256)) + (dd % 16 == 0)
    m = np.where(cnt > 0, np.log(np.maximum(cnt, 1)), NEG).astype(f)
    out["amask"] = np.ascontiguousarray(m.reshape(ST, P, S).transpose(1, 0, 2))
    return out


CTX = 256
CT = CTX // P
N_ALL = CTX + S
AT = N_ALL // P
DA_HEADS, DA_QK = 8, 64
L_CH = 64
NCH = N_ALL // L_CH
CCH = CTX // L_CH
XCH = NCH - CCH
LEVELS = 5
RW_LN_EPS = 64e-5
DECAY = 0.6065306597126334
LAM_INIT = 0.2
PEER_HEADS, N_KEYS, TOPK = 8, 128, 16
SLOTS = PEER_HEADS * TOPK
RING = 6


def modulation_phases(nc, T, wbuf):
    I, psum = T["in"], T["psum"]
    with nc.sbuf_tensor("csil", [P, DC, 2], F32) as csil, nc.sbuf_tensor("cwide", [P, DC, P], F32) as cwide, \
            nc.sbuf_tensor("bcol", [P, 6, DC], F32) as bcol, nc.sbuf_tensor("gn", [P, 2, DC], F32) as gn, \
            nc.sbuf_tensor("modc", [P, 6, DC, 2], F32) as modc:
        load_phase(nc, [(csil[:], I["c"]), (bcol[:], I["b_mod"]), (gn[:, 0, :], I["norm1_g_2"]),
                        (gn[:, 1, :], I["norm2_g_2"])] +
                   [(T["gate_rows"][:, k, :], I["b_mod_rows"][:, m * D:(m + 1) * D].to_broadcast([P, D]))
                    for k, m in enumerate((2, 5))])
        with Phase(nc, ["silu_taken", "widened"]) as (block, silu_taken, widened):
            @block.scalar
            def _(act):
                nc.scalar.activation(csil[:], csil[:], ACT.Silu).then_inc(silu_taken, 1)

            @block.vector
            def _(dve):
                dve.wait_ge(silu_taken, 1)
                nc.vector.tensor_copy(cwide[:], csil[:, :, 0:1].to_broadcast([P, DC, P])).then_inc(widened, 1)

        def column_groups(m, half):
            def groups(w):
                def evac(j):
                    k = half * 4 + j
                    return lambda ch, acc: nc.vector.tensor_scalar(modc[:, m, k, :], acc, bcol[:, m, k:k + 1], None,
                                                                   ALU.add)
                return [(P, 2, [(w[:, c, j * P:(j + 1) * P], csil[:, c, :]) for c in range(DC)], evac(j), "v")
                        for j in range(4)]
            return groups

        def row_groups(k, half):
            def groups(w):
                dst = T["gate_rows"][:, k, half * NB:(half + 1) * NB]
                return [(P, NB, [(cwide[:, c, :], w[:, c, :]) for c in range(DC)],
                         lambda ch, acc: nc.vector.tensor_tensor(dst, acc, dst, ALU.add), "v")]
            return groups
        blocks = []
        for m in range(6):
            for half in range(2):
                g = row_groups(m // 3, half) if m in (2, 5) else column_groups(m, half)
                blocks.append((I["w_mod"][2 * m + half], g))
        gemm_phase(nc, psum, wbuf, blocks)
        with Phase(nc, ["vec_step"]) as (block, vec_step):
            @block.vector
            def _(dve):
                chain = Chain(dve, vec_step)
                for k, (m, col, g) in enumerate(((0, 0, 0), (0, 1, 0), (3, 0, 1))):
                    chain.after(nc.vector.scalar_tensor_tensor(T["affine"][:, k, 0, :], modc[:, m + 1, :, col], 1.0,
                                                               gn[:, g, :], ALU.add, ALU.mult))
                    chain.after(nc.vector.tensor_copy(T["affine"][:, k, 1, :], modc[:, m, :, col]))


def modulated_norm(nc, T, x, tiles, which, dst, at, scratch):
    A = T["affine"]

    def finish(c, acc):
        return nc.vector.tensor_scalar(dst[:, c, at:at + tiles * P], acc, A[:, which, 0, c:c + 1],
                                       A[:, which, 1, c:c + 1], ALU.mult, ALU.add)
    norm_phase(nc, T["psum"], T["ident"], x, tiles, scratch, T["stats"], finish)


def head_norm_rope_phase(nc, T, q, k, ropeC, ropeS, gq, gk, qT, kT):
    psum, ident = T["psum"], T["ident"]
    with ExitStack() as ctx:
        def sb(name, shape, dt=F32):
            return ctx.enter_context(nc.sbuf_tensor(name, shape, dt))
        tabs = sb("tabs", [P, 2, 2, AT, 64])
        tmp = sb("hn_tmp", [P, 2, D])
        ss = sb("hn_ss", [P, 2, 16])
        jobs = [(q, t, t + CT, 0, qT) for t in range(ST)] + [(k, t, t, 1, kT) for t in range(AT)]
        n_banks = 2
        with Phase(nc, ["sums_ready", "root_taken", "rows_ready", "transposed", "copied", "vec_step"]) as (
                block, sums_ready, root_taken, rows_ready, transposed, copied, vec_step):
            @block.vector
            def _(dve):
                chain = Chain(dve, vec_step)
                for w, g in enumerate((gq, gk)):
                    chain.after(nc.vector.tensor_tensor(tabs[:, w, 0], ropeC, g[:, 0:1, :].to_broadcast([P, AT, 64]),
                                                        ALU.mult))
                    chain.after(nc.vector.tensor_tensor(tabs[:, w, 1], ropeS, g[:, 1:2, :].to_broadcast([P, AT, 64]),
                                                        ALU.mult))
                for n, (src, t, pos, w, dst) in enumerate(jobs):
                    row = src[:, t, :]
                    g3 = row.rearrange("p (g e) -> p g e", e=64)
                    t0 = tmp[:, 0, :].rearrange("p (g e) -> p g e", e=64)
                    t1 = tmp[:, 1, :].rearrange("p (g e) -> p g e", e=64)
                    chain.after(nc.vector.tensor_tensor(tmp[:, 0, :], row, row, ALU.mult))
                    chain.after(nc.vector.reduce_sum(ss[:, 0, :], t0, AX.X))
                    nc.vector.tensor_scalar(ss[:, 0, :], ss[:, 0, :], 1.0 / 64, EPS, ALU.mult, ALU.add
                                            ).then_inc(sums_ready, 1)
                    dve.wait_ge(root_taken, n + 1)
                    chain.after(nc.vector.reciprocal(ss[:, 0, :], ss[:, 1, :]))
                    chain.after(nc.vector.tensor_tensor(g3, g3, ss[:, 0, :].rearrange("p (g o) -> p g o", o=1)
                                                        .to_broadcast([P, 16, 64]), ALU.mult))
                    C = tabs[:, w, 0, pos:pos + 1, :].to_broadcast([P, 16, 64])
                    chain.after(nc.vector.tensor_tensor(t0, g3, C, ALU.mult))
                    for half in range(2):
                        o4 = tmp[:, 1, :].rearrange("p (g a h f) -> p g a h f", g=16, a=2, h=2)[:, :, :, half, :]
                        i4 = row.rearrange("p (g a h f) -> p g a h f", g=16, a=2, h=2)[:, :, :, 1 - half, :]
                        S4 = tabs[:, w, 1, pos, :].rearrange("p (o a h f) -> p o a h f", o=1, a=2, h=2)[
                            :, :, :, half, :].to_broadcast([P, 16, 2, 16])
                        chain.after(nc.vector.tensor_tensor(o4, i4, S4, ALU.mult))
                    nc.vector.tensor_tensor(row, tmp[:, 0, :], tmp[:, 1, :], ALU.add).then_inc(rows_ready, 1)
                    dve.wait_ge(rows_ready, n + 1)

            def copy_out(act, n):
                src, t, pos, w, dst = jobs[n]
                act.wait_ge(transposed, n + 1)
                nc.scalar.copy(dst[:, :, t * P:(t + 1) * P],
                               psum[:, 2 * (n % n_banks):2 * (n % n_banks) + 2, :].rearrange("p b (c t) -> p (b c) t", c=4)
                               ).then_inc(copied, 1)

            @block.scalar
            def _(act):
                for n, (src, t, pos, w, dst) in enumerate(jobs):
                    act.wait_ge(sums_ready, n + 1)
                    nc.scalar.activation(ss[:, 1, :], ss[:, 0, :], ACT.Sqrt).then_inc(root_taken, 1)
                    if n >= 1:
                        copy_out(act, n - 1)
                copy_out(act, len(jobs) - 1)

            @block.tensor
            def _(pe):
                for n, (src, t, pos, w, dst) in enumerate(jobs):
                    pe.wait_ge(rows_ready, n + 1)
                    if n >= n_banks:
                        pe.wait_ge(copied, n - n_banks + 1)
                    for c in range(DC):
                        last = nc.tensor.transpose(psum[:, 2 * (n % n_banks) + c // 4, (c % 4) * P:(c % 4 + 1) * P],
                                                   src[:, t, c * P:(c + 1) * P], ident[:])
                    last.then_inc(transposed, 1)


def diff_attention_phase(nc, T, qT, kT, v, lam, og, oaT):
    psum, ident = T["psum"], T["ident"]
    SCALE = DA_QK ** -0.5
    UNITS = DA_HEADS * ST
    with ExitStack() as ctx:
        def sb(name, shape, dt=F32):
            return ctx.enter_context(nc.sbuf_tensor(name, shape, dt))
        pr = sb("da_pr", [P, 2, 2, N_ALL])
        pT = sb("da_pT", [P, 2, N_ALL])
        nm = sb("da_nm", [P, 2, UNITS])
        ls = sb("da_ls", [P, 2, UNITS])
        ri = sb("da_ri", [P, 3, 2])
        oa = sb("oa", [P, ST, D])
        junk = sb("da_junk", [P, P])
        sq = sb("da_sq", [P, 3, UNITS])
        with Phase(nc, ["lam_sums", "lam_exps", "vec_step"]) as (block, lam_sums, lam_exps, vec_step):
            @block.vector
            def _(dve):
                chain = Chain(dve, vec_step)
                l4 = lam["rows"][:].rearrange("p (a b e) -> p a b e", a=2, b=2)
                pr4 = lam["prod"][:].rearrange("p (a e) -> p a e", a=2)
                chain.after(nc.vector.tensor_tensor(pr4, l4[:, :, 0, :], l4[:, :, 1, :], ALU.mult))
                nc.vector.reduce_sum(lam["two"][:, 0, :], pr4, AX.X).then_inc(lam_sums, 1)
                dve.wait_ge(lam_exps, 1)
                chain.after(nc.vector.tensor_tensor(lam["neg"][:], lam["two"][:, 1, 1:2], lam["two"][:, 1, 0:1],
                                                    ALU.subtract))
                chain.after(nc.vector.tensor_scalar(lam["neg"][:], lam["neg"][:], -LAM_INIT, None, ALU.add))

            @block.scalar
            def _(act):
                act.wait_ge(lam_sums, 1)
                nc.scalar.activation(lam["two"][:, 1, :], lam["two"][:, 0, :], ACT.Exp).then_inc(lam_exps, 1)

        names = ["scores_ready", "max_taken", "probs_ready", "diff_ready", "turned_ready", "turned_copied",
                 "values_ready", "out_taken", "vec_step"]
        with Phase(nc, names) as (block, scores_ready, max_taken, probs_ready, diff_ready, turned_ready,
                                  turned_copied, values_ready, out_taken, vec_step):
            def S_of(m):
                return psum[:, 2 * m:2 * m + 2, :].rearrange("p b n -> p (b n)")[:, 0:N_ALL]
            turned = psum[:, 4:6, :].rearrange("p b n -> p (b n)")[:, 0:N_ALL]

            @block.tensor
            def _(pe):
                def scores(u):
                    h, i = divmod(u, ST)
                    for m in range(2):
                        if u >= 1:
                            pe.wait_ge(probs_ready, 2 * (u - 1) + m + 1)
                        lo = 64 * m
                        for a, b in ((0, 512), (512, N_ALL)):
                            last = nc.tensor.matmul(S_of(m)[:, a:b], qT[lo:lo + 64, h, i * P:(i + 1) * P],
                                                    kT[lo:lo + 64, h, a:b], start=True, stop=True)
                        last.then_inc(scores_ready, 1)

                def turn(u):
                    pe.wait_ge(diff_ready, u + 1)
                    if u >= 1:
                        pe.wait_ge(turned_copied, u)
                    for k in range(AT):
                        last = nc.tensor.transpose(turned[:, k * P:(k + 1) * P], pr[:, u % 2, 0, k * P:(k + 1) * P],
                                                   ident[:])
                    last.then_inc(turned_ready, 1)

                def values(u):
                    h, i = divmod(u, ST)
                    pe.wait_ge(turned_copied, u + 1)
                    if u >= 2:
                        pe.wait_ge(out_taken, u - 1)
                    for k in range(AT):
                        last = nc.tensor.matmul(psum[:, 6 + u % 2, 0:P], pT[:, u % 2, k * P:(k + 1) * P],
                                                v[:, k, h * P:(h + 1) * P], start=(k == 0), stop=(k == AT - 1))
                    last.then_inc(values_ready, 1)

                scores(0)
                for u in range(UNITS + 1):
                    if u + 1 < UNITS:
                        scores(u + 1)
                    if u < UNITS:
                        turn(u)
                    if u >= 1:
                        values(u - 1)

            @block.vector
            def _(dve):
                chain = Chain(dve, vec_step)

                def maxima(u):
                    for m in range(2):
                        dve.wait_ge(scores_ready, 2 * u + m + 1)
                        chain.after(nc.vector.tensor_reduce(nm[:, m, u:u + 1], S_of(m), AX.X, ALU.max, negate=True))
                    nc.vector.tensor_scalar(nm[:, :, u:u + 1], nm[:, :, u:u + 1], SCALE, None, ALU.mult
                                            ).then_inc(max_taken, 1)

                def difference(u):
                    dve.wait_ge(probs_ready, 2 * u + 2)
                    chain.after(nc.vector.reciprocal(ri[:, 0:2, u % 2:u % 2 + 1], ls[:, :, u:u + 1]))
                    chain.after(nc.vector.tensor_tensor(ri[:, 2, u % 2:u % 2 + 1], ri[:, 1, u % 2:u % 2 + 1],
                                                        lam["neg"][:], ALU.mult))
                    p = pr[:, u % 2]
                    chain.after(nc.vector.tensor_scalar(p[:, 1, :], p[:, 1, :], ri[:, 2, u % 2:u % 2 + 1], None,
                                                        ALU.mult))
                    nc.vector.scalar_tensor_tensor(p[:, 0, :], p[:, 0, :], ri[:, 0, u % 2:u % 2 + 1], p[:, 1, :],
                                                   ALU.mult, ALU.add).then_inc(diff_ready, 1)

                def out(u):
                    h, i = divmod(u, ST)
                    dve.wait_ge(values_ready, u + 1)
                    o = oa[:, i, h * P:(h + 1) * P]
                    nc.vector.tensor_copy(o, psum[:, 6 + u % 2, 0:P]).then_inc(out_taken, 1)
                    dve.wait_ge(out_taken, u + 1)
                    chain.after(nc.vector.tensor_tensor(junk[:], o, o, ALU.mult))
                    chain.after(nc.vector.reduce_sum(sq[:, 0, u:u + 1], junk[:], AX.X))

                maxima(0)
                for u in range(UNITS + 1):
                    if u < UNITS:
                        difference(u)
                    if u + 1 < UNITS:
                        maxima(u + 1)
                    if u >= 1:
                        out(u - 1)

            @block.scalar
            def _(act):
                def probs(u):
                    act.wait_ge(max_taken, u + 1)
                    if u >= 2:
                        act.wait_ge(turned_ready, u - 1)
                    for m in range(2):
                        nc.scalar.activation(pr[:, u % 2, m, :], S_of(m), ACT.Exp, bias=nm[:, m, u:u + 1], scale=SCALE,
                                             accum_out=ls[:, m, u:u + 1]).then_inc(probs_ready, 1)

                def copy(u):
                    act.wait_ge(turned_ready, u + 1)
                    if u >= 2:
                        act.wait_ge(values_ready, u - 1)
                    nc.scalar.copy(pT[:, u % 2, :], turned).then_inc(turned_copied, 1)

                probs(0)
                for u in range(UNITS):
                    if u + 1 < UNITS:
                        probs(u + 1)
                    copy(u)

        with Phase(nc, ["mean_ready", "root_taken", "rows_ready", "transposed", "vec_step"]) as (
                block, mean_ready, root_taken, rows_ready, transposed, vec_step):
            @block.vector
            def _(dve):
                chain = Chain(dve, vec_step)
                nc.vector.tensor_scalar(sq[:, 1, :], sq[:, 0, :], 1.0 / P, EPS, ALU.mult, ALU.add
                                        ).then_inc(mean_ready, 1)
                dve.wait_ge(root_taken, 1)
                chain.after(nc.vector.reciprocal(sq[:, 0, :], sq[:, 2, :]))
                for u in range(UNITS):
                    h, i = divmod(u, ST)
                    o = oa[:, i, h * P:(h + 1) * P]
                    ins = nc.vector.tensor_scalar(o, o, sq[:, 0, u:u + 1], None, ALU.mult)
                    if i == ST - 1:
                        ins.then_inc(rows_ready, 1)
                for h in range(DA_HEADS):
                    dve.wait_ge(transposed, h + 1)
                    nc.vector.tensor_scalar(oaT[:, h, :], psum[:, h, :], og[:], 1.0 - LAM_INIT, ALU.mult, ALU.mult)

            @block.scalar
            def _(act):
                act.wait_ge(mean_ready, 1)
                nc.scalar.activation(sq[:, 2, :], sq[:, 1, :], ACT.Sqrt).then_inc(root_taken, 1)

            @block.tensor
            def _(pe):
                for h in range(DA_HEADS):
                    pe.wait_ge(rows_ready, h + 1)
                    for i in range(ST):
                        last = nc.tensor.transpose(psum[:, h, i * P:(i + 1) * P], oa[:, i, h * P:(h + 1) * P], ident[:])
                    last.then_inc(transposed, 1)


def rwkv_tile(nc, T, g, R, lora, obT):
    psum, ident, K = T["psum"], T["ident"], T["rwc"]
    z, area, cst = R["z"], R["area"], R["cst"]
    prm, up, gup = R["prm"], R["up"], R["gup"]
    C768 = N_ALL

    def cells(ap):
        return ap.rearrange("p (c t) -> p c t", t=L_CH)

    def wide(ap, n):
        return ap.rearrange("p c (o t) -> p c o t", o=1).to_broadcast([P, n, 2, L_CH])

    def bd(n):
        return cst["bd"][:].rearrange("p (c h t) -> p c h t", c=1, h=2).to_broadcast([P, n, 2, L_CH])

    def mask(ap, n):
        return ap.rearrange("p (c t) -> p c t", c=1).to_broadcast([P, n, L_CH])

    r, k, v = z[:, 0, 0:S], z[:, 1, :], z[:, 2, :]
    qr = R["qr"]
    bt, kt = R["bt"], R["kt"]
    wq, wb, wk, wv = R["wq"], R["wb"], R["wk"], R["wv"]
    wBT, wAT, wXT, wbt, wkt = R["wBT"], R["wAT"], R["wXT"], R["wbt"], R["wkt"]
    Cc, Dd, wV = R["C"], R["D"], R["wV"]
    tmp = R["tmp"]
    pl = R["pl"]

    names = ["tile_loaded", "lora_up", "opened", "kr_ready", "squares_ready", "norms_summed", "root_taken",
             "sums_ready", "exps_ready", "stacked_ready", "widened", "vec_step", "pool_step", "act_step"]
    with Phase(nc, names) as (block, tile_loaded, lora_up, opened, kr_ready, squares_ready, norms_summed, root_taken,
                              sums_ready, exps_ready, stacked_ready, widened, vec_step, pool_step, act_step):
        sig = [tmp[:, 0], tmp[:, 1]]
        a = [tmp[:, 2], tmp[:, 3]]
        kr, kk, Lc, Lm = tmp[:, 4], tmp[:, 5], tmp[:, 6], tmp[:, 7]
        eQ, eR, eK = R["eQ"], R["eR"], R["eK"]

        @block.sync
        def _(sp):
            sp.dma_start(z[:, 0, 0:S], R["zr_d"][g]).then_inc(tile_loaded, 16)
            sp.dma_start(z[:, 1, :], R["zk_d"][g]).then_inc(tile_loaded, 16)
            sp.dma_start(z[:, 2, :], R["zv_d"][g]).then_inc(tile_loaded, 16)
            sp.dma_start(prm[:, 0:9], T["in"]["rw_cols"][g]).then_inc(tile_loaded, 16)
            sp.dma_start(up[:], T["in"]["rw_up"][g]).then_inc(tile_loaded, 16)
            sp.dma_start(gup[:], T["in"]["rw_gup"][g]).then_inc(tile_loaded, 16)

        @block.tensor
        def _(pe):
            pe.wait_ge(tile_loaded, 96)
            for d in range(2):
                for w in range(2):
                    for lo, hi in ((0, 512), (512, C768)):
                        last = nc.tensor.matmul(psum[:, 4 * d + 2 * w + lo // 512, 0:hi - lo],
                                                up[64 * w:64 * w + 64, d, :], lora[64 * w:64 * w + 64, lo:hi],
                                                start=True, stop=True)
                    last.then_inc(lora_up, 1)
            pe.wait_ge(opened, 1)
            pe.wait_ge(squares_ready, 1)
            for lo, hi in ((0, 512), (512, C768)):
                last = nc.tensor.matmul(psum[:, lo // 512, 0:hi - lo], cst["ones"][:], kk[:, lo:hi],
                                        start=True, stop=True)
            last.then_inc(norms_summed, 1)

        def two_banks(b):
            return psum[:, b:b + 2, :].rearrange("p b n -> p (b n)")[:, 0:C768]

        @block.scalar
        def _(act):
            for d in range(2):
                for w, dst in ((0, sig[d]), (1, a[d])):
                    act.wait_ge(lora_up, 2 * d + w + 1)
                    nc.scalar.activation(dst, two_banks(4 * d + 2 * w), ACT.Sigmoid,
                                         bias=prm[:, 2 * w + d:2 * w + d + 1]).then_inc(opened, 1)
            act.wait_ge(kr_ready, 1)
            nc.scalar.activation(kk, kr, ACT.Square).then_inc(squares_ready, 1)
            act.wait_ge(norms_summed, 1)
            nc.scalar.activation(Lc, two_banks(0), ACT.Sqrt, bias=cst["tiny"][:]).then_inc(root_taken, 1)
            for d in range(2):
                act.wait_ge(sums_ready, d + 1)
                if d:
                    act.wait_ge(stacked_ready, 4)
                nc.scalar.activation(eQ, Lm, ACT.Exp, scale=-DECAY).then_inc(exps_ready, 1)
                nc.scalar.activation(eR, Lc, ACT.Exp, scale=-DECAY).then_inc(exps_ready, 1)
                nc.scalar.activation(eK, Lc, ACT.Exp, scale=DECAY).then_inc(exps_ready, 1)

        @block.vector
        def _(dve):
            chain = Chain(dve, vec_step)
            dve.wait_ge(tile_loaded, 96)
            nc.vector.tensor_scalar(kr, k, prm[:, 4:5], None, ALU.mult).then_inc(kr_ready, 1)
            chain.after(nc.vector.tensor_scalar(prm[:, 9:10], prm[:, 5:6], -1.0, 1.0, ALU.mult, ALU.add))
            dve.wait_ge(root_taken, 1)
            chain.after(nc.vector.reciprocal(Lc, Lc))
            chain.after(nc.vector.tensor_tensor(kk, kr, Lc, ALU.mult))
            dve.wait_ge(opened, 4)
            for d in range(2):
                if d:
                    dve.wait_ge(exps_ready, 3)

                def run(ap):
                    return ap if d == 0 else ap[:, ::-1]
                chain.after(nc.vector.tensor_tensor_scan(run(Lc), run(cst["reset"][:, d, :]), run(sig[d]), 0.0,
                                                         ALU.mult, ALU.add))
                nc.vector.tensor_tensor(Lm, Lc, sig[d], ALU.subtract).then_inc(sums_ready, 1)
                chain.after(nc.vector.tensor_tensor(bt[:, d], kk, a[d], ALU.mult))
                chain.after(nc.vector.tensor_scalar(a[d], a[d], prm[:, 5:6], prm[:, 9:10], ALU.mult, ALU.add))
                chain.after(nc.vector.tensor_tensor(kt[:, d], k, a[d], ALU.mult))
                dve.wait_ge(exps_ready, 3 * d + 3)
                nc.vector.tensor_tensor(qr[:, d, :, 0, :], cells(kk), cells(eQ), ALU.mult).then_inc(stacked_ready, 1)
                nc.vector.tensor_tensor(qr[:, d, CCH:, 1, :], cells(r), cells(eR)[:, CCH:, :], ALU.mult
                                        ).then_inc(stacked_ready, 1)
                nc.vector.tensor_tensor(bt[:, d], bt[:, d], eK, ALU.mult).then_inc(stacked_ready, 1)
                chain.after(nc.vector.tensor_copy(pl[:, d, :], cells(eR)[:, :, (L_CH - 1) * (1 - d)]))
                nc.vector.tensor_tensor(kt[:, d], kt[:, d], eK, ALU.mult).then_inc(stacked_ready, 1)
                dve.wait_ge(stacked_ready, 4 * d + 4)
                chain.after(nc.vector.tensor_tensor(wk[:, d], wide(cells(kt[:, d]), NCH), bd(NCH), ALU.mult))
            nc.vector.tensor_tensor(wv[:], wide(cells(v), NCH), bd(NCH), ALU.mult)

        @block.gpsimd
        def _(pool):
            for d in range(2):
                pool.wait_ge(stacked_ready, 4 * d + 3)
                nc.gpsimd.tensor_tensor(wq[:, d], wide(qr[:, d, :, 0, :], NCH), bd(NCH), ALU.mult)
                nc.gpsimd.tensor_tensor(wb[:, d], wide(cells(bt[:, d]), NCH), bd(NCH), ALU.mult)

    wX, wU, zt = R["wX"], R["wU"], R["zt"]

    def flat(ap):
        return ap.rearrange("p h t -> p (h t)")

    def flat4(ap):
        return ap.rearrange("p c h t -> p (c h t)")

    names = ["grams_ready", "grams_read", "turned_ready", "turned_read", "v_ready", "v_read", "vec_step"]
    with Phase(nc, names) as (block, grams_ready, grams_read, turned_ready, turned_read, v_ready, v_read, vec_step):
        batches = [(d, c0) for d in range(2) for c0 in range(0, NCH, 4)]

        @block.tensor
        def _(pe):
            for n, (d, c0) in enumerate(batches):
                if n >= 2:
                    pe.wait_ge(grams_read, n - 1)
                for i in range(4):
                    c = c0 + i
                    rhs = qr[:, d, c].rearrange("p a t -> p (a t)")
                    nc.tensor.matmul(psum[:, n % 2, i * P:(i + 1) * P], flat(wb[:, d, c]), rhs, start=True, stop=True)
                    nc.tensor.matmul(psum[:, 2 + n % 2, i * P:(i + 1) * P], flat(wk[:, d, c]), rhs,
                                     start=True, stop=True)
                    last = nc.tensor.matmul(psum[:, 4 + n % 2, i * P:(i + 1) * P], flat(wq[:, d, c]),
                                            flat(wb[:, d, c]), start=True, stop=True)
                last.then_inc(grams_ready, 1)
                if n >= 1:
                    pe.wait_ge(turned_read, 2 * n)
                for i in range(4):
                    c = c0 + i
                    nc.tensor.transpose(psum[:, 6, i * P:(i + 1) * P], flat(wb[:, d, c]), ident[:])
                    last = nc.tensor.transpose(psum[:, 7, i * P:(i + 1) * P], flat(wk[:, d, c]), ident[:])
                last.then_inc(turned_ready, 1)
            pe.wait_ge(turned_read, 2 * len(batches))
            for n in range(3):
                if n == 2:
                    pe.wait_ge(v_read, 1)
                for i in range(4):
                    last = nc.tensor.transpose(psum[:, 6 + n % 2, i * P:(i + 1) * P], flat(wv[:, 4 * n + i]), ident[:])
                last.then_inc(v_ready, 1)

        @block.vector
        def _(dve):
            chain = Chain(dve, vec_step)
            for n, (d, c0) in enumerate(batches):
                dve.wait_ge(grams_ready, n + 1)
                g1 = psum[:, n % 2, :].rearrange("p (c a t) -> p c a t", a=2, t=L_CH)
                g2 = psum[:, 2 + n % 2, :].rearrange("p (c a t) -> p c a t", a=2, t=L_CH)
                am = psum[:, 4 + n % 2, :].rearrange("p (c m) -> p c m", m=P)
                strict = cst["strict_wide"][:, d, :].rearrange("p (c h t) -> p c h t", c=1, h=2).to_broadcast(
                    [P, 4, 2, L_CH])
                x4 = wX[:, d, c0:c0 + 4].rearrange("p c h t -> p c (h t)")
                chain.after(nc.vector.tensor_tensor(x4, am, cst["level"][:, d, 0:1, :].to_broadcast([P, 4, P]),
                                                    ALU.mult))
                nc.vector.tensor_tensor(wAT[:, d, c0:c0 + 4], wide(g1[:, :, 0, :], 4), strict, ALU.mult)
                nc.vector.tensor_tensor(wBT[:, d, c0:c0 + 4], wide(g2[:, :, 0, :], 4), strict, ALU.mult)
                if c0 >= CCH:
                    incl = mask(cst["incl"][:, d, :], 4)
                    nc.vector.tensor_tensor(Dd[:, d, c0 - CCH:c0 - CCH + 4], g1[:, :, 1, :], incl, ALU.mult)
                    nc.vector.tensor_tensor(Cc[:, d, c0 - CCH:c0 - CCH + 4], g2[:, :, 1, :], incl, ALU.mult)
                nc.vector.tensor_tensor(x4, x4, ident[:].rearrange("p (c m) -> p c m", c=1).to_broadcast([P, 4, P]),
                                        ALU.add).then_inc(grams_read, 1)

        @block.scalar
        def _(act):
            for n, (d, c0) in enumerate(batches):
                act.wait_ge(turned_ready, n + 1)
                nc.scalar.copy(flat4(wbt[:, d, c0:c0 + 4]), psum[:, 6, :]).then_inc(turned_read, 1)
                nc.scalar.copy(flat4(wkt[:, d, c0:c0 + 4]), psum[:, 7, :]).then_inc(turned_read, 1)
            for n in range(3):
                act.wait_ge(v_ready, n + 1)
                nc.scalar.copy(flat4(wV[:, 4 * n:4 * n + 4]), psum[:, 6 + n % 2, :]).then_inc(v_read, 1)

    BQ = [(d, c0) for d in range(2) for c0 in range(0, NCH, 4)]
    NQ = len(BQ)
    names = ["x_turned", "xt_ready", "u_ready", "u_copied", "z_ready", "z_masked", "x_ready0", "x_ready1"]
    with Phase(nc, names) as (block, x_turned, xt_ready, u_ready, u_copied, z_ready, z_masked, x_ready0, x_ready1):
        x_ready = (x_ready0, x_ready1)

        @block.tensor
        def _(pe):
            for lv in range(LEVELS + 1):
                for q, (d, c0) in enumerate(BQ):
                    n = lv * NQ + q
                    if lv:
                        pe.wait_ge(x_ready[d], 3 * (lv - 1) + q % 3 + 1)
                    if n >= 2:
                        pe.wait_ge(xt_ready, n - 1)
                    for i in range(4):
                        last = nc.tensor.transpose(psum[:, 6 + q % 2, i * P:(i + 1) * P], flat(wX[:, d, c0 + i]),
                                                   ident[:])
                    last.then_inc(x_turned, 1)
                    if lv < LEVELS:
                        for i in range(4):
                            last = nc.tensor.matmul(psum[:, q, i * P:(i + 1) * P], flat(wAT[:, d, c0 + i]),
                                                    flat(wX[:, d, c0 + i]), start=True, stop=True)
                        last.then_inc(u_ready, 1)
                if lv < LEVELS:
                    for q, (d, c0) in enumerate(BQ):
                        n = lv * NQ + q
                        pe.wait_ge(u_copied, n + 1)
                        pe.wait_ge(xt_ready, n + 1)
                        for i in range(4):
                            last = nc.tensor.matmul(psum[:, q, i * P:(i + 1) * P], flat(wXT[:, d, c0 + i]),
                                                    flat(wU[:, d, c0 + i]), start=True, stop=True)
                        last.then_inc(z_ready, 1)

        @block.scalar
        def _(act):
            for lv in range(LEVELS + 1):
                for q, (d, c0) in enumerate(BQ):
                    n = lv * NQ + q
                    act.wait_ge(x_turned, n + 1)
                    if lv:
                        act.wait_ge(z_ready, n - NQ + 1)
                    nc.scalar.copy(flat4(wXT[:, d, c0:c0 + 4]), psum[:, 6 + q % 2, :]).then_inc(xt_ready, 1)
                    if lv < LEVELS:
                        act.wait_ge(u_ready, n + 1)
                        nc.scalar.copy(flat4(wU[:, d, c0:c0 + 4]), psum[:, q, :]).then_inc(u_copied, 1)

        @block.vector
        def _(dve):
            for lv in range(LEVELS):
                for q, (d, c0) in enumerate(BQ):
                    n = lv * NQ + q
                    t_ = zt[:, d, c0:c0 + 4].rearrange("p c h t -> p c (h t)")
                    dve.wait_ge(z_ready, n + 1)
                    if lv and d:
                        dve.wait_ge(x_ready1, 3 * (lv - 1) + q % 3 + 1)
                    nc.vector.tensor_tensor(t_, psum[:, q, :].rearrange("p (c m) -> p c m", m=P),
                                            cst["level"][:, d, lv + 1:lv + 2, :].to_broadcast([P, 4, P]), ALU.mult
                                            ).then_inc(z_masked, 1)
                    if d == 0:
                        dve.wait_ge(z_masked, n + 1)
                        x4 = flat4(wX[:, d, c0:c0 + 4])
                        nc.vector.tensor_tensor(x4, x4, flat4(zt[:, d, c0:c0 + 4]), ALU.add).then_inc(x_ready0, 1)

        @block.gpsimd
        def _(pool):
            for lv in range(LEVELS):
                for q, (d, c0) in enumerate(BQ):
                    if d:
                        pool.wait_ge(z_masked, lv * NQ + q + 1)
                        x4 = flat4(wX[:, d, c0:c0 + 4])
                        nc.gpsimd.tensor_tensor(x4, x4, flat4(zt[:, d, c0:c0 + 4]), ALU.add).then_inc(x_ready1, 1)

    orders = [list(range(NCH)), list(range(CCH - 1, -1, -1)) + list(range(NCH - 1, CCH - 1, -1))]
    wS, wW, wN = R["wS"], R["wW"], R["wN"]
    names = ["w_ready", "w_copied", "n_ready", "n_copied", "s_ready", "s_copied", "y_done"]
    with Phase(nc, [n + s for n in names for s in ("0", "1")] + ["state_zero"]) as (block, *sems):
        w_ready, w_copied, n_ready, n_copied, s_ready, s_copied, y_done = [
            (sems[2 * i], sems[2 * i + 1]) for i in range(7)]
        state_zero = sems[-1]

        def room(d, k):
            bank = 6 + d if k == 2 else 4 + d
            return psum[:, bank, k * P:(k + 1) * P]

        @block.tensor
        def _(pe):
            pe.wait_ge(state_zero, 1)

            def outputs(n, d):
                c = orders[d][n] - CCH
                yy = psum[0:L_CH, 2 * d + c // 4, (c % 4) * P:(c % 4 + 1) * P]
                nc.tensor.matmul(yy, qr[:, d, CCH + c, 1, :], wS[:, d], start=True, stop=False)
                nc.tensor.matmul(yy, Cc[:, d, c], flat(wV[:, CCH + c]), start=False, stop=False)
                nc.tensor.matmul(yy, Dd[:, d, c], wN[:, d], start=False, stop=True).then_inc(y_done[d], 1)

            for n in range(NCH):
                for d in range(2):
                    c = orders[d][n]
                    if n >= 1:
                        pe.wait_ge(s_copied[d], n)
                    nc.tensor.matmul(room(d, 0), flat(wq[:, d, c]), wS[:, d], start=True, stop=False)
                    nc.tensor.matmul(room(d, 0), flat(wBT[:, d, c]), flat(wV[:, c]), start=False, stop=True
                                     ).then_inc(w_ready[d], 1)
                for d in range(2):
                    c = orders[d][n]
                    pe.wait_ge(w_copied[d], n + 1)
                    nc.tensor.matmul(room(d, 1), flat(wXT[:, d, c]), wW[:, d], start=True, stop=True
                                     ).then_inc(n_ready[d], 1)
                for d in range(2):
                    c = orders[d][n]
                    if n < NCH - 1:
                        nc.tensor.matmul(room(d, 2), ident[:], wS[:, d], start=True, stop=False)
                        nc.tensor.matmul(room(d, 2), flat(wkt[:, d, c]), flat(wV[:, c]), start=False, stop=False)
                        pe.wait_ge(n_copied[d], n + 1)
                        nc.tensor.matmul(room(d, 2), flat(wbt[:, d, c]), wN[:, d], start=False, stop=True
                                         ).then_inc(s_ready[d], 1)
                    else:
                        pe.wait_ge(n_copied[d], n + 1)
                    if n >= CCH:
                        outputs(n, d)

        def copies(d, eng, copy_w, copy_n, copy_s):
            for n in range(NCH):
                c = orders[d][n]
                eng.wait_ge(w_ready[d], n + 1)
                copy_w(wW[:, d], room(d, 0)).then_inc(w_copied[d], 1)
                eng.wait_ge(n_ready[d], n + 1)
                if n >= 1:
                    if n > CCH:
                        eng.wait_ge(y_done[d], n - CCH)
                    else:
                        eng.wait_ge(s_ready[d], n)
                copy_n(wN[:, d], room(d, 1)).then_inc(n_copied[d], 1)
                if n < NCH - 1:
                    eng.wait_ge(s_ready[d], n + 1)
                    if n >= CCH:
                        eng.wait_ge(y_done[d], n - CCH + 1)
                    copy_s(wS[:, d], room(d, 2), pl[:, d, c:c + 1]).then_inc(s_copied[d], 1)

        @block.vector
        def _(dve):
            nc.vector.memset(wS[:], 0.0).then_inc(state_zero, 1)
            copies(0, dve, nc.vector.tensor_copy, lambda o, i: nc.vector.tensor_scalar(o, i, -1.0, None, ALU.mult),
                   lambda o, i, s: nc.vector.tensor_scalar(o, i, s, None, ALU.mult))

        @block.scalar
        def _(act):
            copies(1, act, nc.scalar.copy, lambda o, i: nc.scalar.activation(o, i, ACT.Copy, scale=-1.0),
                   lambda o, i, s: nc.scalar.activation(o, i, ACT.Copy, scale=s))

    names = ["y_added", "y_turned", "y_summed", "mean_ready", "squares_ready", "var_ready", "root_taken", "rk_ready",
             "bonus_ready", "gate_ready", "vec_step"]
    with Phase(nc, names) as (block, y_added, y_turned, y_summed, mean_ready, squares_ready, var_ready, root_taken,
                              rk_ready, bonus_ready, gate_ready, vec_step):
        yb, sqb, rk, rt = (R["fin"][:, i] for i in range(4))
        rows = R["y_rows"]

        @block.tensor
        def _(pe):
            nc.tensor.matmul(psum[:, 5, :], gup[:], R["gd"], start=True, stop=True).then_inc(gate_ready, 1)
            pe.wait_ge(rk_ready, 1)
            nc.tensor.matmul(psum[:, 6, :], cst["ones"][:], rk, start=True, stop=True).then_inc(bonus_ready, 1)
            pe.wait_ge(y_added, 1)
            for c in range(XCH):
                last = nc.tensor.transpose(psum[:, 4, c * L_CH:(c + 1) * L_CH], rows[:, c * P:(c + 1) * P],
                                           ident[0:L_CH, 0:L_CH])
            last.then_inc(y_turned, 1)
            pe.wait_ge(y_summed, 1)
            nc.tensor.matmul(psum[:, 7, :], cst["ones"][:], yb, start=True, stop=True).then_inc(mean_ready, 1)
            pe.wait_ge(squares_ready, 1)
            nc.tensor.matmul(psum[:, 4, :], cst["ones"][:], sqb, start=True, stop=True).then_inc(var_ready, 1)

        @block.scalar
        def _(act):
            act.wait_ge(var_ready, 1)
            nc.scalar.activation(rt, psum[:, 4, :], ACT.Sqrt, bias=cst["ln_eps"][:], scale=1.0 / 64
                                 ).then_inc(root_taken, 1)

        @block.vector
        def _(dve):
            chain = Chain(dve, vec_step)
            both = [psum[0:L_CH, 2 * d:2 * d + 2, :].rearrange("p b n -> p (b n)") for d in range(2)]
            chain.after(nc.vector.tensor_copy(rows, both[0]))
            nc.vector.tensor_tensor(rows, rows, both[1], ALU.add).then_inc(y_added, 1)
            nc.vector.scalar_tensor_tensor(rk, r, prm[:, 6:7], k[:, CTX:], ALU.mult, ALU.mult).then_inc(rk_ready, 1)
            dve.wait_ge(y_turned, 1)
            nc.vector.tensor_copy(yb, psum[:, 4, :]).then_inc(y_summed, 1)
            dve.wait_ge(mean_ready, 1)
            chain.after(nc.vector.scalar_tensor_tensor(yb, psum[:, 7, :], -1.0 / 64, yb, ALU.mult, ALU.add))
            nc.vector.tensor_tensor(sqb, yb, yb, ALU.mult).then_inc(squares_ready, 1)
            dve.wait_ge(bonus_ready, 1)
            chain.after(nc.vector.tensor_tensor(rk, psum[:, 6, :], v[:, CTX:], ALU.mult))
            dve.wait_ge(root_taken, 1)
            chain.after(nc.vector.reciprocal(rt, rt))
            chain.after(nc.vector.tensor_tensor(yb, yb, rt, ALU.mult))
            chain.after(nc.vector.tensor_scalar(yb, yb, prm[:, 7:8], prm[:, 8:9], ALU.mult, ALU.add))
            chain.after(nc.vector.tensor_tensor(yb, yb, rk, ALU.add))
            dve.wait_ge(gate_ready, 1)
            chain.after(nc.vector.tensor_tensor(obT[:, g, :], yb, psum[:, 5, :], ALU.mult))


def rwkv_constants():
    import numpy as np
    f = np.float32
    p = np.arange(P)
    t = np.arange(L_CH)
    out = {"ones": (p[:, None] // 64 == p[None, :] // 64).astype(f)}
    out["bd"] = out["ones"].copy()
    row, col = p[:, None] % 64, t[None, :]
    strict = [(row < col), (row > col)]
    incl = [(row <= col), (row >= col)]
    out["strict_wide"] = np.stack([np.tile(m, (1, 2)) * out["ones"] for m in strict], 1).astype(f)
    out["incl"] = np.stack(incl, 1).astype(f)
    lev = np.zeros((P, 2, LEVELS + 1, L_CH), f)
    for i in range(LEVELS + 1):
        m = 2 ** i
        same = row // (2 * m) == col // (2 * m)
        lev[:, 0, i] = -1.0 * (same & ((row // m) % 2 == 1) & ((col // m) % 2 == 0))
        lev[:, 1, i] = -1.0 * (same & ((row // m) % 2 == 0) & ((col // m) % 2 == 1))
    out["level"] = np.tile(lev, (1, 1, 1, 2)) * out["bd"][:, None, None, :]
    tt = np.arange(N_ALL)
    out["reset"] = np.broadcast_to(np.stack([tt % L_CH != 0, tt % L_CH != L_CH - 1]).astype(f), (P, 2, N_ALL)).copy()
    out["tiny"] = np.full((P, 1), 1e-12, f)
    out["ln_eps"] = np.full((P, 1), RW_LN_EPS, f)
    return out


def rope_constants():
    import numpy as np
    f = np.float32
    inv = (f(10000.0) ** (-np.arange(16, dtype=f) / f(16))).astype(f)
    tok = np.arange(S)
    C = np.ones((N_ALL, 2, 2, 16), f)
    Sn = np.zeros((N_ALL, 2, 2, 16), f)
    for a, pos in enumerate((tok // 64, tok % 64)):
        ang = pos.astype(f)[:, None] * inv
        C[CTX:, a, :, :] = np.cos(ang)[:, None, :]
        Sn[CTX:, a, 0, :] = -np.sin(ang)
        Sn[CTX:, a, 1, :] = np.sin(ang)
    lay = lambda x: np.ascontiguousarray(x.reshape(AT, P, 64).transpose(1, 0, 2))
    return {"ropeC": lay(C), "ropeS": lay(Sn)}


def peer_phases(nc, T, x, out):
    I, psum, ident = T["in"], T["psum"], T["ident"]
    with ExitStack() as ctx:
        def sb(name, shape, dt=F32):
            return ctx.enter_context(nc.sbuf_tensor(name, shape, dt))
        h = sb("h_rows", [P, ST, D])
        sel = sb("sel_idx", [P, ST, SLOTS], I32)
        gate = sb("sel_gate", [P, ST, SLOTS])
        with ExitStack() as inner:
            def sbi(name, shape, dt=F32):
                return inner.enter_context(nc.sbuf_tensor(name, shape, dt))
            hT = sbi("hT_p", [P, DC, S])
            qT = sbi("qT_p", [P, 2 * PEER_HEADS, S])
            with nc.sbuf_tensor("p_scr", [P, 6 * D], F32) as scr:
                sc2 = scr[:].rearrange("p (t d) -> p t d", d=D)
                modulated_norm(nc, T, x, ST, 2, hT, 0, (sc2[:, 0:2], sc2[:, 2:6]))
            with Phase(nc, ["turned_back", "copied"]) as (block, turned_back, copied):
                @block.tensor
                def _(pe):
                    for t in range(ST):
                        for c in range(DC):
                            last = nc.tensor.transpose(psum[:, 2 * t + c // 4, (c % 4) * P:(c % 4 + 1) * P],
                                                       hT[:, c, t * P:(t + 1) * P], ident[:])
                        last.then_inc(turned_back, 1)

                @block.vector
                def _(dve):
                    for t in range(ST):
                        dve.wait_ge(turned_back, t + 1)
                        nc.vector.tensor_copy(h[:, t, :], psum[:, 2 * t:2 * t + 2, :].rearrange("p b n -> p (b n)"))
            with nc.sbuf_tensor("wbuf_p", [P, 2, DC * NB], F32) as wbuf:
                def q_groups(b):
                    def groups(w):
                        res = []
                        for j in range(4):
                            dst = qT[:, 4 * b + j, :]
                            ev = (lambda ch, acc, dst=dst: nc.vector.tensor_copy(dst, acc)) if j % 2 == 0 else \
                                (lambda ch, acc, dst=dst: nc.scalar.copy(dst, acc))
                            res.append((P, S, [(w[:, c, j * P:(j + 1) * P], hT[:, c, :]) for c in range(DC)], ev,
                                        "va"[j % 2]))
                        return res
                    return groups
                gemm_phase(nc, psum, wbuf, [(I["peer_wq"][b], q_groups(b)) for b in range(4)])
            search_phase(nc, T, qT, sel, gate, sbi)
        expert_phase(nc, T, x, h, sel, gate, out, sb)


def search_phase(nc, T, qT, sel, gate, sb):
    I, psum = T["in"], T["psum"]
    HP = 2 * PEER_HEADS
    keys = sb("keys", [P, HP, N_KEYS])
    iota = sb("iota16", [P, TOPK])
    load_phase(nc, [(keys[:], I["peer_keys"]), (iota[:], I["iota16"])])
    sc = sb("key_scores", [P, HP, N_KEYS])
    top = sb("top_val", [P, HP, TOPK])
    topi = sb("top_pos", [P, HP, TOPK], U32)
    topf = sb("top_posf", [P, HP, TOPK])
    cand = sb("cand", [P, TOPK * TOPK])
    best = sb("best", [P, PEER_HEADS, TOPK])
    besti = sb("best_pos", [P, PEER_HEADS, TOPK], U32)
    hi = sb("pos_hi", [P, 2, PEER_HEADS * TOPK], U32)
    hif = sb("pos_hif", [P, 2, PEER_HEADS * TOPK])
    pick = sb("pick", [P, PEER_HEADS, TOPK, TOPK])
    found = sb("found", [P, 2, PEER_HEADS * TOPK])
    den = sb("gate_den", [P, 2, PEER_HEADS])
    with Phase(nc, ["scores_ready", "scores_copied", "shifted", "exps_ready", "vec_step"]) as (
            block, scores_ready, scores_copied, shifted, exps_ready, vec_step):
        @block.tensor
        def _(pe):
            for t in range(ST):
                for hp in range(HP):
                    if hp == 0 and t >= 2:
                        pe.wait_ge(scores_copied, t - 1)
                    last = nc.tensor.matmul(psum[:, 4 * (t % 2) + hp // 4, (hp % 4) * P:(hp % 4 + 1) * P],
                                            qT[:, hp, t * P:(t + 1) * P], keys[:, hp, :], start=True, stop=True)
                last.then_inc(scores_ready, 1)

        @block.scalar
        def _(act):
            for t in range(ST):
                act.wait_ge(shifted, t + 1)
                nc.scalar.activation(best[:], best[:], ACT.Exp).then_inc(exps_ready, 1)

        @block.vector
        def _(dve):
            chain = Chain(dve, vec_step)

            def top16(vals, v16, i16):
                chain.after(nc.vector.max(v16[:, 0:8], vals))
                chain.after(nc.vector.max_index(i16[:, 0:8], v16[:, 0:8], vals))
                chain.after(nc.vector.match_replace(vals, v16[:, 0:8], vals, -3e38))
                chain.after(nc.vector.max(v16[:, 8:16], vals))
                chain.after(nc.vector.max_index(i16[:, 8:16], v16[:, 8:16], vals))

            for t in range(ST):
                dve.wait_ge(scores_ready, t + 1)
                nc.vector.tensor_copy(sc[:].rearrange("p h k -> p (h k)"),
                                      psum[:, 4 * (t % 2):4 * (t % 2) + 4, :].rearrange("p b n -> p (b n)")
                                      ).then_inc(scores_copied, 1)
                dve.wait_ge(scores_copied, t + 1)
                for hp in range(HP):
                    top16(sc[:, hp, :], top[:, hp, :], topi[:, hp, :])
                chain.after(nc.vector.tensor_copy(topf[:], topi[:]))
                for hd in range(PEER_HEADS):
                    first = top[:, 2 * hd, :].rearrange("p (a o) -> p a o", o=1).to_broadcast([P, TOPK, TOPK])
                    second = top[:, 2 * hd + 1:2 * hd + 2, :].to_broadcast([P, TOPK, TOPK])
                    chain.after(nc.vector.tensor_tensor(cand[:].rearrange("p (a b) -> p a b", a=TOPK), first, second,
                                                        ALU.add))
                    top16(cand[:], best[:, hd, :], besti[:, hd, :])
                flat = besti[:].rearrange("p h k -> p (h k)")
                chain.after(nc.vector.tensor_scalar(hi[:, 0, :], flat, 4, None, ALU.logical_shift_right))
                chain.after(nc.vector.tensor_scalar(hi[:, 1, :], flat, 15, None, ALU.bitwise_and))
                chain.after(nc.vector.tensor_copy(hif[:], hi[:]))
                for w in range(2):
                    rank = hif[:, w, :].rearrange("p (n o) -> p n o", o=1).to_broadcast([P, SLOTS, TOPK])
                    io = iota[:].rearrange("p (o a) -> p o a", o=1).to_broadcast([P, SLOTS, TOPK])
                    pk = pick[:].rearrange("p h k a -> p (h k) a")
                    chain.after(nc.vector.tensor_tensor(pk, rank, io, ALU.is_equal))
                    names_ = topf[:, w::2, :].rearrange("p h (o a) -> p h o a", o=1).to_broadcast(
                        [P, PEER_HEADS, TOPK, TOPK])
                    chain.after(nc.vector.tensor_tensor(pick[:], pick[:], names_, ALU.mult))
                    chain.after(nc.vector.reduce_sum(found[:, w, :], pk, AX.X))
                chain.after(nc.vector.scalar_tensor_tensor(found[:, 0, :], found[:, 0, :], float(N_KEYS),
                                                           found[:, 1, :], ALU.mult, ALU.add))
                chain.after(nc.vector.tensor_copy(sel[:, t, :], found[:, 0, :]))
                chain.after(nc.vector.tensor_copy(den[:, 0, :], best[:, :, 0]))
                big = den[:, 0, :].rearrange("p (h o) -> p h o", o=1).to_broadcast([P, PEER_HEADS, TOPK])
                nc.vector.tensor_tensor(best[:], best[:], big, ALU.subtract).then_inc(shifted, 1)
                dve.wait_ge(exps_ready, t + 1)
                chain.after(nc.vector.reduce_sum(den[:, 0, :], best[:], AX.X))
                chain.after(nc.vector.reciprocal(den[:, 1, :], den[:, 0, :]))
                inv = den[:, 1, :].rearrange("p (h o) -> p h o", o=1).to_broadcast([P, PEER_HEADS, TOPK])
                chain.after(nc.vector.tensor_tensor(gate[:, t, :].rearrange("p (h k) -> p h k", k=TOPK), best[:], inv,
                                                    ALU.mult))


def expert_phase(nc, T, x, h, sel, gate, out, sb):
    I, psum, ident = T["in"], T["psum"], T["ident"]
    BATCH = 4
    RB = 2 * BATCH + 2
    NBT = SLOTS // BATCH
    rows = sb("rows", [P, RB, 2 * D])
    prod = sb("uh", [P, D])
    dots = sb("dots", [P, 2, BATCH])
    g1 = sb("g1", [P, 2, BATCH])
    g2 = sb("g2", [P, 2, BATCH])
    diag = sb("diag", [P, 2 * BATCH, P])
    UN = ST * SLOTS
    with Phase(nc, [f"row_landed{i}" for i in range(RB)] +
               ["dot_taken", "inner_ready", "tanh_ready", "weights_ready", "diag_ready", "row_used", "tile_ready",
                "tile_taken", "out_written", "vec_step"]) as (block, *sems):
        row_landed = sems[:RB]
        (dot_taken, inner_ready, tanh_ready, weights_ready, diag_ready, row_used, tile_ready, tile_taken, out_written,
         vec_step) = sems[RB:]

        @block.gpsimd
        def _(pool):
            for n in range(UN):
                t, s = divmod(n, SLOTS)
                if n >= RB:
                    pool.wait_ge(row_used, n - RB + 1)
                nc.gpsimd.indirect_dma_start(out=rows[:, n % RB, :], out_offset=None, in_=I["peer_uv"],
                                             in_offset=bass.IndirectOffsetOnAxis(ap=sel[:, t, s:s + 1], axis=0)
                                             ).then_inc(row_landed[n % RB], 16)

        @block.vector
        def _(dve):
            chain = Chain(dve, vec_step)

            def dot(n):
                t, s = divmod(n, SLOTS)
                dve.wait_ge(row_landed[n % RB], 16 * (n // RB + 1))
                if n >= 1:
                    dve.wait_ge(dot_taken, n)
                if s % BATCH == 0 and n >= 2 * BATCH:
                    dve.wait_ge(weights_ready, n // BATCH - 1)
                nc.vector.scalar_tensor_tensor(prod[:], rows[:, n % RB, 0:D], 1.0, h[:, t, :], ALU.mult, ALU.mult,
                                               accum_out=dots[:, (n // BATCH) % 2, s % BATCH:s % BATCH + 1]
                                               ).then_inc(dot_taken, 1)

            def gelu(b):
                zz, u1, u2 = dots[:, b % 2, :], g1[:, b % 2, :], g2[:, b % 2, :]
                t, s = divmod(b * BATCH, SLOTS)
                dve.wait_ge(dot_taken, (b + 1) * BATCH)
                chain.after(nc.vector.tensor_tensor(u1, zz, zz, ALU.mult))
                chain.after(nc.vector.tensor_scalar(u1, u1, 0.044715, 1.0, ALU.mult, ALU.add))
                nc.vector.tensor_tensor(u1, u1, zz, ALU.mult).then_inc(inner_ready, 1)
                chain.after(nc.vector.scalar_tensor_tensor(u2, zz, 0.5, gate[:, t, s:s + BATCH], ALU.mult, ALU.mult))
                dve.wait_ge(tanh_ready, b + 1)
                if b >= 2:
                    dve.wait_ge(diag_ready, (b - 1) * BATCH)
                nc.vector.scalar_tensor_tensor(u2, u1, 1.0, u2, ALU.add, ALU.mult).then_inc(weights_ready, 1)

            for b in range(ST * NBT):
                for i in range(BATCH):
                    dot(b * BATCH + i)
                gelu(b)
                if (b + 1) % NBT == 0:
                    t = b // NBT
                    dve.wait_ge(tile_ready, t + 1)
                    acc = psum[:, 2 * (t % 2):2 * (t % 2) + 2, :].rearrange("p b n -> p (b n)")
                    chain.after(nc.vector.tensor_tensor(prod[:], acc, T["gate_rows"][:, 1, :], ALU.mult))
                    nc.vector.tensor_tensor(x[:, t, :], x[:, t, :], prod[:], ALU.add).then_inc(tile_taken, 1)
                    dve.wait_ge(tile_taken, t + 1)

        @block.scalar
        def _(act):
            for b in range(ST * NBT):
                act.wait_ge(inner_ready, b + 1)
                nc.scalar.activation(g1[:, b % 2, :], g1[:, b % 2, :], ACT.Tanh, scale=0.7978845608028654
                                     ).then_inc(tanh_ready, 1)
                act.wait_ge(weights_ready, b + 1)
                for i in range(BATCH):
                    n = b * BATCH + i
                    if n >= 2 * BATCH:
                        act.wait_ge(row_used, n - 2 * BATCH + 1)
                    nc.scalar.activation(diag[:, n % (2 * BATCH), :], ident[:], ACT.Copy,
                                         scale=g2[:, b % 2, i:i + 1]).then_inc(diag_ready, 1)

        @block.tensor
        def _(pe):
            for n in range(UN):
                t, s = divmod(n, SLOTS)
                pe.wait_ge(row_landed[n % RB], 16 * (n // RB + 1))
                pe.wait_ge(diag_ready, n + 1)
                if s == 0 and t >= 2:
                    pe.wait_ge(tile_taken, t - 1)
                for half in range(2):
                    last = nc.tensor.matmul(psum[:, 2 * (t % 2) + half, :], diag[:, n % (2 * BATCH), :],
                                            rows[:, n % RB, D + half * NB:D + (half + 1) * NB],
                                            start=(s == 0), stop=(s == SLOTS - 1))
                last.then_inc(row_used, 1)
                if s == SLOTS - 1:
                    pe.wait_ge(row_used, n + 1)
                    pe.sem_inc(tile_ready, 1)

        @block.sync
        def _(sp):
            for t in range(ST):
                sp.wait_ge(tile_taken, t + 1)
                sp.dma_start(out[:, t, :], x[:, t, :]).then_inc(out_written, 16)
            sp.wait_ge(out_written, 16 * ST)


def second_block_program(nc, T, out):
    I, psum, ident, x = T["in"], T["psum"], T["ident"], T["x"]
    hT_d, oaT_d = (nc.dram_tensor(n, [P, DC, w], F32, kind="Internal").ap() for n, w in (("hT_spill", N_ALL),
                                                                                        ("oaT_spill", S)))
    z_d = {n: nc.dram_tensor(f"z{n}_spill", [DC, P, w], F32, kind="Internal").ap()
           for n, w in (("r", S), ("k", N_ALL), ("v", N_ALL))}

    def scope():
        s = ExitStack()

        def sb(name, shape, dt=F32):
            return s.enter_context(nc.sbuf_tensor(name, shape, dt))
        return s, sb

    def move_phase(moves):
        with Phase(nc, ["moved"]) as (block, moved):
            @block.sync
            def _(sp):
                for dst, src in moves:
                    sp.dma_start(dst, src).then_inc(moved, 16)
                sp.wait_ge(moved, 16 * len(moves))

    with nc.sbuf_tensor("wbuf_mod", [P, 2, DC * NB], F32) as wbuf:
        modulation_phases(nc, T, wbuf)

    top, sbt = scope()
    lora = sbt("lora", [P, N_ALL])
    gd = sbt("gd", [P, S])
    with ExitStack() as stage:
        def sb(name, shape, dt=F32):
            return stage.enter_context(nc.sbuf_tensor(name, shape, dt))
        hT = sb("hT_all", [P, DC, N_ALL])
        oaT = sb("oaT", [P, DC, S])
        with nc.sbuf_tensor("ctx_rows", [P, CT, D], F32) as ctx_rows, nc.sbuf_tensor("nscr", [P, 6 * D], F32) as scr:
            load_phase(nc, [(ctx_rows[:], I["ctx"])])
            sc2 = scr[:].rearrange("p (t d) -> p t d", d=D)
            modulated_norm(nc, T, ctx_rows, CT, 1, hT, 0, (sc2[:, 0:2], sc2[:, 2:6]))
            modulated_norm(nc, T, x, ST, 0, hT, CTX, (sc2[:, 0:2], sc2[:, 2:6]))

        def rows_of(dst, half, first_tile, tiles):
            def groups(w):
                res = []
                for t in range(tiles):
                    o = dst[:, t, half * NB:(half + 1) * NB]
                    ev = (lambda ch, acc, o=o: nc.vector.tensor_copy(o, acc)) if t % 2 == 0 else \
                        (lambda ch, acc, o=o: nc.scalar.copy(o, acc))
                    at = (first_tile + t) * P
                    res.append((P, NB, [(hT[:, c, at:at + P], w[:, c, :]) for c in range(DC)], ev, "va"[t % 2]))
                return res
            return groups

        W = I["w_in_2"]
        with ExitStack() as att:
            def sba(name, shape, dt=F32):
                return att.enter_context(nc.sbuf_tensor(name, shape, dt))
            v = sba("v_all", [P, AT, D])
            qT = sba("qT", [P, DC, S])
            kT = sba("kT", [P, DC, N_ALL])
            with nc.sbuf_tensor("q_rows", [P, ST, D], F32) as q, nc.sbuf_tensor("k_rows", [P, AT, D], F32) as k:
                with nc.sbuf_tensor("wbuf_qkv", [P, 2, DC * NB], F32) as wbuf:
                    gemm_phase(nc, psum, wbuf, [(W[0], rows_of(q, 0, CT, ST)), (W[1], rows_of(q, 1, CT, ST)),
                                                (W[2], rows_of(k, 0, 0, AT)), (W[3], rows_of(k, 1, 0, AT)),
                                                (W[4], rows_of(v, 0, 0, AT)), (W[5], rows_of(v, 1, 0, AT))])
                with nc.sbuf_tensor("ropeC_sb", [P, AT, 64], F32) as rc, nc.sbuf_tensor("ropeS_sb", [P, AT, 64], F32) \
                        as rs, nc.sbuf_tensor("gq", [P, 2, 64], F32) as gq, nc.sbuf_tensor("gk", [P, 2, 64], F32) as gk:
                    load_phase(nc, [(rc[:], I["ropeC"]), (rs[:], I["ropeS"]),
                                    (gq[:], I["q_gain"].to_broadcast([P, 2, 64])),
                                    (gk[:], I["k_gain"].to_broadcast([P, 2, 64]))])
                    head_norm_rope_phase(nc, T, q, k, rc[:], rs[:], gq, gk, qT, kT)
            with nc.sbuf_tensor("lam_rows", [P, 256], F32) as lr, nc.sbuf_tensor("lam_prod", [P, 128], F32) as lp, \
                    nc.sbuf_tensor("lam_two", [P, 2, 2], F32) as l2, nc.sbuf_tensor("lam_neg", [P, 1], F32) as ln, \
                    nc.sbuf_tensor("og", [P, 1], F32) as og:
                load_phase(nc, [(lr[:], I["diff_lambda"].to_broadcast([P, 256])), (og[:], I["diff_out_g"])])
                diff_attention_phase(nc, T, qT, kT, v, {"rows": lr, "prod": lp, "two": l2, "neg": ln}, og, oaT)

        with ExitStack() as proj:
            def sbp(name, shape, dt=F32):
                return proj.enter_context(nc.sbuf_tensor(name, shape, dt))
            zr, zk, zv = sbp("zr", [P, DC, S]), sbp("zk", [P, DC, N_ALL]), sbp("zv", [P, DC, N_ALL])
            shift = sbp("shift", [P, 26, 3])
            lo2 = sbp("lo2", [P, 2, N_ALL])
            wbuf = sbp("wbuf_rw", [P, 2, DC * NB])
            load_phase(nc, [(shift[:], I["rw_shift"])])

            def shifted(j, dst):
                def evac(ch, acc):
                    n = dst.shape[1]
                    ch.after(nc.vector.tensor_scalar(dst, acc, shift[:, j, 1:2], None, ALU.mult))
                    ch.after(nc.vector.scalar_tensor_tensor(dst[:, 1:n], acc[:, 0:n - 1], shift[:, j, 0:1], dst[:, 1:n],
                                                            ALU.mult, ALU.add))
                    return nc.vector.scalar_tensor_tensor(dst[:, 0:n - 1], acc[:, 1:n], shift[:, j, 2:3],
                                                          dst[:, 0:n - 1], ALU.mult, ALU.add)
                return evac

            def channels(first, dst, tiles, with_ctx):
                def groups(w):
                    res = []
                    for i in range(tiles):
                        j = first + i
                        o = dst(i)
                        spans = ([(0, CTX)] if with_ctx else []) + [(CTX, N_ALL)]
                        for lo, hi in spans:
                            at = lo if with_ctx else lo - CTX
                            res.append((P, hi - lo, [(w[:, c, i * P:(i + 1) * P], hT[:, c, lo:hi]) for c in range(DC)],
                                        shifted(j, o[:, at:at + hi - lo]), "v"))
                    return res
                return groups
            blocks = [(W[6 + b], channels(4 * b, lambda i, b=b: zr[:, 4 * b + i], 4, False)) for b in range(2)]
            blocks += [(W[8 + b], channels(8 + 4 * b, lambda i, b=b: zk[:, 4 * b + i], 4, True)) for b in range(2)]
            blocks += [(W[10 + b], channels(16 + 4 * b, lambda i, b=b: zv[:, 4 * b + i], 4, True)) for b in range(2)]
            blocks += [(I["w_lora"], channels(24, lambda i: lo2[:, i], 2, True))]
            gemm_phase(nc, psum, wbuf, blocks)
            with Phase(nc, ["spilled"]) as (block, spilled):
                @block.sync
                def _(sp):
                    for dst, src in ((z_d["r"], zr), (z_d["k"], zk), (z_d["v"], zv)):
                        sp.dma_start(dst.rearrange("c p n -> p c n"), src[:]).then_inc(spilled, 16)
                    sp.dma_start(hT_d, hT[:]).then_inc(spilled, 16)
                    sp.dma_start(oaT_d, oaT[:]).then_inc(spilled, 16)
                    sp.wait_ge(spilled, 80)

                @block.scalar
                def _(act):
                    nc.scalar.activation(lora[0:64, :], lo2[0:64, 0, :], ACT.Tanh)
                    nc.scalar.copy(lora[64:P, :], lo2[64:P, 0, :])
                    nc.scalar.activation(gd[:], lo2[:, 1, CTX:], ACT.Sigmoid)

    obT = sbt("obT", [P, DC, S])
    with ExitStack() as rw:
        def sb(name, shape, dt=F32):
            return rw.enter_context(nc.sbuf_tensor(name, shape, dt))
        cst = {n: sb("rwc_" + n, list(I["rwc_" + n].shape)) for n in T["rwc_names"]}
        load_phase(nc, [(cst[n][:], I["rwc_" + n]) for n in cst])
        wide_shape = [P, 2, NCH, 2, L_CH]
        R = {"cst": cst, "z": sb("z", [P, 3, N_ALL]), "prm": sb("prm", [P, 10]), "up": sb("up", [P, 2, P]),
             "gup": sb("gup", [P, P]), "gd": gd[:], "area": None, "pl": sb("pl", [P, 2, NCH]),
             "zr_d": z_d["r"], "zk_d": z_d["k"], "zv_d": z_d["v"]}
        R["qr"] = sb("qr", [P, 2, NCH, 2, L_CH])[:]
        A1 = sb("room_bk", [P, 4 * N_ALL])
        R["bt"] = A1[:, 0:2 * N_ALL].rearrange("p (d n) -> p d n", d=2)
        R["kt"] = A1[:, 2 * N_ALL:].rearrange("p (d n) -> p d n", d=2)
        R["wXT"] = A1[:, :].rearrange("p (d c h t) -> p d c h t", d=2, c=NCH, h=2)
        A2 = sb("room_ab", [P, 8 * N_ALL])
        R["tmp"] = A2[:, :].rearrange("p (i n) -> p i n", i=8)
        R["wAT"] = A2[:, 0:4 * N_ALL].rearrange("p (d c h t) -> p d c h t", d=2, c=NCH, h=2)
        R["wBT"] = A2[:, 4 * N_ALL:].rearrange("p (d c h t) -> p d c h t", d=2, c=NCH, h=2)
        A3 = sb("room_turned", [P, 4 * N_ALL])
        R["eQ"], R["eR"], R["eK"] = (A3[:, i * N_ALL:(i + 1) * N_ALL] for i in range(3))
        R["wbt"] = A3[:, :].rearrange("p (d c h t) -> p d c h t", d=2, c=NCH, h=2)
        R["wkt"] = sb("wkt", wide_shape)[:]
        R["wq"] = sb("wq", wide_shape)[:]
        A4 = sb("room_wb", [P, 4 * N_ALL])
        R["wb"] = A4[:, :].rearrange("p (d c h t) -> p d c h t", d=2, c=NCH, h=2)
        R["wU"] = R["wb"]
        A5 = sb("room_wk", [P, 4 * N_ALL])
        R["wk"] = A5[:, :].rearrange("p (d c h t) -> p d c h t", d=2, c=NCH, h=2)
        R["zt"] = R["wk"]
        R["fin"] = A5[:, 0:4 * S].rearrange("p (i n) -> p i n", i=4)
        R["y_rows"] = A5[0:L_CH, 4 * S:6 * S]
        R["wX"] = sb("wX", wide_shape)[:]
        R["wv"] = A1[:, 2 * N_ALL:].rearrange("p (c h t) -> p c h t", c=NCH, h=2)
        R["C"], R["D"] = sb("Cc", [P, 2, XCH, L_CH])[:], sb("Dd", [P, 2, XCH, L_CH])[:]
        R["wV"] = sb("wV", [P, NCH, 2, L_CH])[:]
        R["wS"], R["wW"], R["wN"] = sb("wS", [P, 2, P])[:], *(
            A4[:, i * 2 * P:(i + 1) * 2 * P].rearrange("p (d m) -> p d m", d=2) for i in range(2))
        with Phase(nc, ["zeroed"]) as (block, zeroed):
            @block.vector
            def _(dve):
                nc.vector.memset(R["qr"][:, :, 0:CCH, 1, :], 0.0).then_inc(zeroed, 1)
        with nc.Fori(0, DC) as g:
            rwkv_tile(nc, T, g, R, lora, obT)

    with ExitStack() as mg:
        def sb(name, shape, dt=F32):
            return mg.enter_context(nc.sbuf_tensor(name, shape, dt))
        hT = sb("hT_again", [P, DC, N_ALL])
        oaT = sb("oaT_again", [P, DC, S])
        zg = sb("zg", [P, 2 * DC, S])
        m = sb("merged", [P, DC, S])
        mt = sb("merge_tmp", [P, 2, S])
        wbuf = sb("wbuf_mg", [P, 2, DC * NB])
        load_phase(nc, [(hT[:], hT_d), (oaT[:], oaT_d)])

        def open_gate(b):
            def groups(w):
                return [(P, S, [(w[:, c, j * P:(j + 1) * P], hT[:, c, CTX:]) for c in range(DC)],
                         lambda ch, acc, j=j: nc.scalar.activation(zg[:, 4 * b + j, :], acc, ACT.Sigmoid), "a")
                        for j in range(4)]
            return groups

        def branch(b, which, src):
            def groups(w):
                def evac(j):
                    k = 4 * b + j

                    def first(ch, acc):
                        return nc.vector.tensor_tensor(m[:, k, :], acc, zg[:, k, :], ALU.mult)

                    def second(ch, acc):
                        ch.after(nc.vector.tensor_tensor(mt[:, 0, :], acc, zg[:, DC + k, :], ALU.mult))
                        return nc.vector.tensor_tensor(m[:, k, :], m[:, k, :], mt[:, 0, :], ALU.add)
                    return second if which else first
                return [(P, S, [(w[:, c, j * P:(j + 1) * P], src[:, c, :]) for c in range(DC)], evac(j), "v")
                        for j in range(4)]
            return groups

        def project(half):
            def groups(w):
                def evac(t):
                    def f(ch, acc):
                        o = x[:, t, half * NB:(half + 1) * NB]
                        ch.after(nc.vector.tensor_tensor(mt[:, 1, :], acc,
                                                         T["gate_rows"][:, 0, half * NB:(half + 1) * NB], ALU.mult))
                        return nc.vector.tensor_tensor(o, o, mt[:, 1, :], ALU.add)
                    return f
                return [(P, NB, [(m[:, c, t * P:(t + 1) * P], w[:, c, :]) for c in range(DC)], evac(t), "v")
                        for t in range(ST)]
            return groups
        gemm_phase(nc, psum, wbuf, [(I["w_in_2"][12 + b], open_gate(b)) for b in range(4)])
        gemm_phase(nc, psum, wbuf, [(I["w_branch_a"][b], branch(b, 0, oaT)) for b in range(2)] +
                   [(I["w_branch_b"][b], branch(b, 1, obT)) for b in range(2)])
        gemm_phase(nc, psum, wbuf, [(I["w_out_2"][b], project(b)) for b in range(2)])
    top.close()
    peer_phases(nc, T, x, out)


def program(nc, I, consts, out):
    with ExitStack() as ctx:
        def sb(name, shape, dt=F32):
            return ctx.enter_context(nc.sbuf_tensor(name, shape, dt))
        T = {"in": I, "psum": ctx.enter_context(nc.psum_tensor("psum", [P, BANKS, 512], F32)),
             "rwc_names": [n[4:] for n in I if n.startswith("rwc_")]}
        T["x"] = sb("x", [P, ST, D])
        T["ident"] = sb("ident_sb", [P, P])
        T["stats"] = sb("stats", [P, 4, ST])
        T["one"] = sb("one", [P, 1])
        with ExitStack() as first:
            def sbf(name, shape, dt=F32):
                return first.enter_context(nc.sbuf_tensor(name, shape, dt))
            for name, a in consts.items():
                if name != "ident":
                    T[name] = sbf(name + "_sb", list(a.shape))
            T["hT"] = sbf("hT", [P, DC, S])
            T["hT2"] = T["hT"]
            T["wbuf"] = sbf("wbuf", [P, 2, DC * NB])
            T["cols"] = sbf("cols", [P, 16])
            T["taps"] = sbf("taps", [P, 40])
            T["gate_b"] = sbf("gate_b", [4, 4])
            T["hng"] = sbf("hng", [P, 512])
            T["big"] = T["wbuf"][:, :, :].rearrange("p s n -> p (s n)")
            load_phase(nc, [(T[n][:], a) for n, a in consts.items()] + [(T["x"][:], I["x"])])
            with Phase(nc, ["ones_set"]) as (block, ones_set):
                @block.vector
                def _(dve):
                    nc.vector.memset(T["one"][:], 1.0).then_inc(ones_set, 1)
            with nc.Fori(0, DEPTH) as l:
                hybrid_layer(nc, l, T)
            with nc.sbuf_tensor("fg", [P, D], F32) as fg:
                load_phase(nc, [(fg[:], I["final_g"].to_broadcast([P, D]))])
                norm_phase(nc, T["psum"], T["ident"], T["x"], ST,
                           (T["big"][:, 0:2 * D].rearrange("p (t d) -> p t d", t=2), None), T["stats"], None,
                           write_back=fg[:])
        T["gate_rows"] = sb("gate_rows", [P, 2, D])
        T["affine"] = sb("affine", [P, 3, 2, DC])
        T["rwc"] = None
        second_block_program(nc, T, out)


def lay_out(v):
    import numpy as np
    A = {k: np.asarray(a) for k, a in v.items()}
    c = np.ascontiguousarray
    L = DEPTH

    def blocks(w, nb):
        K, N = w.shape[1:]
        return c(w.reshape(w.shape[0], K // P, P, N // nb, nb).transpose(0, 3, 2, 1, 4))

    def cols(g):
        return c(g.reshape(g.shape[0], -1, P).transpose(0, 2, 1))
    w = A["w_in"]
    out = {
        "x": c(A["x"][0].reshape(ST, P, D).transpose(1, 0, 2)),
        "norm1_g": cols(A["norm1_g"]), "norm2_g": cols(A["norm2_g"]),
        "w_in": blocks(np.concatenate([w[:, :, 0:2048], w[:, :, 2064:]], axis=2), NB),
        "w_gates": c(blocks(w[:, :, 2048:2064], 16)[:, 0]),
        "conv_w": c(A["conv_w"].reshape(L, 5, 8, P).transpose(0, 3, 1, 2).reshape(L, P, 40)),
        "gate_b": c(np.concatenate([A["gate_i_b"].reshape(L, 2, 4), A["gate_f_b"].reshape(L, 2, 4)],
                                   axis=1).transpose(0, 2, 1)),
        "head_norm_g": A["head_norm_g"].reshape(L, 1, 512),
        "w_out": blocks(A["w_out"], NB),
        "w_up": blocks(A["w_up"], NB),
        "w_down": c(A["w_down"].reshape(L, 4, DC, P, 2, NB).transpose(0, 4, 1, 3, 2, 5)),
        "final_g": A["final_g"].reshape(1, D),
    }
    W = A["w_in_2"]
    order = np.concatenate([W[:, :, 0:6144], W[:, :, 6400:8448]], axis=2)
    out.update({
        "c": c(np.stack([A["c_2"][0], A["c_ctx_2"]], 1).reshape(DC, P, 2).transpose(1, 0, 2)),
        "ctx": c(A["ctx_2"][0].reshape(CT, P, D).transpose(1, 0, 2)),
        "w_mod": blocks(A["w_mod_2"], NB)[0],
        "b_mod": c(A["b_mod_2"][0].reshape(6, DC, P).transpose(2, 0, 1)),
        "b_mod_rows": A["b_mod_2"],
        "norm1_g_2": cols(A["norm1_g_2"])[0], "norm2_g_2": cols(A["norm2_g_2"])[0],
        "w_in_2": blocks(order, NB)[0],
        "w_lora": blocks(W[:, :, 6144:6400], 256)[0, 0],
        "diff_lambda": A["diff_lambda_2"].reshape(1, 256),
        "diff_out_g": A["diff_out_g_2"].reshape(P, 1),
        "rw_shift": c(A["rw_shift_2"][0].reshape(3, 26, P).transpose(2, 1, 0)),
        "rw_cols": c(np.stack([A["rw_w0_2"][0, 0], A["rw_w0_2"][0, 1], A["rw_a0_2"][0, 0], A["rw_a0_2"][0, 1],
                               A["rw_k_k_2"][0], A["rw_k_a_2"][0], A["rw_r_k_2"][0].reshape(-1), A["rw_ln_g_2"][0],
                               A["rw_ln_b_2"][0]], 1).reshape(DC, P, 9)),
        "rw_up": c(np.concatenate([A["rw_w_up_2"][0].transpose(1, 0, 2), A["rw_a_up_2"][0].transpose(1, 0, 2)], 0)
                   .reshape(P, 2, DC, P).transpose(2, 0, 1, 3)),
        "rw_gup": c(A["rw_g_up_2"][0].reshape(P, DC, P).transpose(1, 0, 2)),
        "w_branch_a": blocks(A["w_branch_a_2"], NB)[0], "w_branch_b": blocks(A["w_branch_b_2"], NB)[0],
        "w_out_2": blocks(A["w_out_2"], NB)[0],
        "peer_wq": blocks(A["peer_wq_2"], NB)[0],
        "peer_keys": c(A["peer_keys_2"][0].reshape(2 * PEER_HEADS, N_KEYS, P).transpose(2, 0, 1)),
        "peer_uv": c(np.concatenate([A["peer_u_2"][0], A["peer_v_2"][0]], axis=1)),
        "iota16": np.broadcast_to(np.arange(TOPK, dtype=np.float32), (P, TOPK)).copy(),
    })
    for n in ("q", "k"):
        g = A[f"{n}_norm_g_2"][0]
        swapped = g.reshape(2, 2, 16)[:, ::-1].reshape(64)
        out[n + "_gain"] = c(np.stack([g, swapped])[None])
    out.update(rope_constants())
    out.update({"rwc_" + n: a for n, a in rwkv_constants().items()})
    return out


def kernel(**v):
    import numpy as np
    import concourse.bacc as bacc
    from concourse import mybir as mb
    from concourse.bass_utils import run_bass_kernel_spmd as run
    nc = bacc.Bacc("TRN2", target_bir_lowering=False, num_devices=1)
    arrays, I, C = {}, {}, {}
    for group, dst in ((lay_out(v), I), (constants(), C)):
        for name, a in group.items():
            arrays["in_" + name] = np.ascontiguousarray(a)
            dst[name] = nc.dram_tensor("in_" + name, a.shape, mb.dt.from_np(a.dtype), kind="ExternalInput").ap()
    o = nc.dram_tensor("out_0", (P, ST, D), F32, kind="ExternalOutput").ap()
    program(nc, I, C, o)
    r = run(nc, [arrays], core_ids=[0]).results[0]["out_0"]
    return r.transpose(1, 0, 2).reshape(1, S, D)
```

```python
from contextlib import ExitStack

import concourse.bass as bass
from concourse import mybir

F32 = mybir.dt.float32
F32R = mybir.dt.float32r
U32 = mybir.dt.uint32
I32 = mybir.dt.int32
ALU = mybir.AluOpType
ACT = mybir.ActivationFunctionType
AX = mybir.AxisListType

P = 128
D = 1024
DC = D // P
S = 512
ST = S // P
DEPTH = 2
EPS = 1e-6
NEG = -1e30
BANKS = 8
M_HEADS, M_DIM = 4, 128
A_HEADS, A_DIM = 8, 64
FF = 4 * D
NB = 512
QC = 2
QUARTERS = DC // QC
RAW_RING, SPLIT_RING = 4, 6


class Split:

    def __init__(self, hi, lo):
        self.hi, self.lo = hi, lo

    def __getitem__(self, index):
        return Split(self.hi[index], self.lo[index])


class SplitBlock:

    def __init__(self, ring, b):
        self.ring, self.b = ring, b

    def __getitem__(self, index):
        rows, c, cols = index
        slot = (self.b * QUARTERS + c // QC) % SPLIT_RING
        return self.ring[rows, slot, c % QC, cols]


def parts(a, b):
    return [(a.hi, b.hi), (a.hi, b.lo), (a.lo, b.hi)]


def sbuf_split(ctx, nc, name, shape):
    return Split(ctx.enter_context(nc.sbuf_tensor(name + "_hi", shape, F32R)),
                 ctx.enter_context(nc.sbuf_tensor(name + "_lo", shape, F32R)))


class Chain:

    def __init__(self, eng, sem, base=0):
        self.eng, self.sem, self.base, self.n = eng, sem, base, 0

    def after(self, ins):
        self.n += 1
        ins.then_inc(self.sem, 1)
        self.eng.wait_ge(self.sem, self.base + self.n)


class Phase:

    count = 0

    def __init__(self, nc, names):
        self.nc, self.names = nc, names

    def __enter__(self):
        Phase.count += 1
        self.sems = [self.nc.alloc_semaphore(f"{n}_{Phase.count}") for n in self.names]
        self.block = ExitStack()
        block = self.block.enter_context(self.nc.Block())
        return [block] + self.sems

    def __exit__(self, *exc):
        if exc[0] is not None:
            return False
        self.block.close()
        self.nc.clear_and_free_semaphores(self.sems)
        self.nc.all_engine_barrier()
        return False


def load_phase(nc, loads):
    with Phase(nc, ["small_loaded"]) as (block, small_loaded):
        @block.sync
        def _(sp):
            for dst, src in loads:
                sp.dma_start(dst, src).then_inc(small_loaded, 16)
            sp.wait_ge(small_loaded, 16 * len(loads))


def norm_phase(nc, psum, ident, x, tiles, scratch, stats, finish, write_back=None):
    with Phase(nc, ["squares_summed", "root_taken", "rows_scaled", "transposed", "vec_step", "act_step"]) as (
            block, squares_summed, root_taken, rows_scaled, transposed, vec_step, act_step):
        sq, xn = scratch

        @block.scalar
        def _(act):
            chain = Chain(act, act_step)
            for t in range(tiles):
                chain.after(nc.scalar.activation(sq[:, t % 2, :], x[:, t, :], ACT.Square, accum_out=stats[:, 0, t:t + 1]))
            squares = nc.scalar.activation(stats[:, 3, 0:tiles], stats[:, 0, 0:tiles], ACT.Copy, scale=1.0 / D)
            squares.then_inc(squares_summed, 1)
            act.wait_ge(vec_step, 1)
            nc.scalar.activation(stats[:, 1, 0:tiles], stats[:, 0, 0:tiles], ACT.Sqrt).then_inc(root_taken, 1)

        @block.vector
        def _(dve):
            chain = Chain(dve, vec_step)
            dve.wait_ge(squares_summed, 1)
            chain.after(nc.vector.tensor_scalar(stats[:, 0, 0:tiles], stats[:, 3, 0:tiles], EPS, None, ALU.add))
            dve.wait_ge(root_taken, 1)
            chain.after(nc.vector.reciprocal(stats[:, 2, 0:tiles], stats[:, 1, 0:tiles]))
            for t in range(tiles):
                if write_back is None:
                    nc.vector.tensor_scalar(xn[:, t, :], x[:, t, :], stats[:, 2, t:t + 1], None,
                                            ALU.mult).then_inc(rows_scaled, 1)
                else:
                    chain.after(nc.vector.scalar_tensor_tensor(x[:, t, :], x[:, t, :], stats[:, 2, t:t + 1],
                                                               write_back, ALU.mult, ALU.mult))
            if write_back is None:
                for c in range(DC):
                    dve.wait_ge(transposed, c + 1)
                    finish(chain, c, psum[:, c, 0:tiles * P])

        @block.tensor
        def _(pe):
            if write_back is None:
                pe.wait_ge(rows_scaled, tiles)
                for c in range(DC):
                    for t in range(tiles):
                        last = nc.tensor.transpose(psum[:, c, t * P:(t + 1) * P], xn[:, t, c * P:(c + 1) * P], ident[:])
                    last.then_inc(transposed, 1)


def plain_gemm_phase(nc, psum, wbuf, blocks):
    slots = wbuf.shape[1]
    flat = []
    for b, (src, groups) in enumerate(blocks):
        n = src.shape[2]
        for g in groups(wbuf[:, b % slots, :].rearrange("p (c n) -> p c n", c=DC)[:, :, 0:n] if n == NB else
                        wbuf[:, b % slots, 0:DC * n].rearrange("p (c n) -> p c n", c=DC)):
            flat.append((b,) + tuple(g))
    done = {"v": 0, "a": 0}
    order = []
    for g in flat:
        done[g[5]] += 1
        order.append(done[g[5]])
    names = [f"weights_loaded{i}" for i in range(slots)] + ["block_used", "sum_ready", "vec_emptied", "act_emptied",
                                                           "vec_step", "act_step"]
    with Phase(nc, names) as (block, *sems):
        weights_loaded = sems[:slots]
        block_used, sum_ready, vec_emptied, act_emptied, vec_step, act_step = sems[slots:]
        emptied = {"v": vec_emptied, "a": act_emptied}

        @block.sync
        def _(sp):
            for b, (src, _g) in enumerate(blocks):
                if b >= slots:
                    sp.wait_ge(block_used, b - slots + 1)
                n = src.shape[2]
                sp.dma_start(wbuf[:, b % slots, 0:DC * n].rearrange("p (c n) -> p c n", c=DC), src).then_inc(
                    weights_loaded[b % slots], 16)

        @block.tensor
        def _(pe):
            for i, (b, rows, cols, pairs, evac, eng) in enumerate(flat):
                if i == 0 or flat[i - 1][0] != b:
                    pe.wait_ge(weights_loaded[b % slots], 16 * (b // slots + 1))
                if i >= BANKS:
                    pe.wait_ge(emptied[flat[i - BANKS][5]], order[i - BANKS])
                for j, (lhsT, rhs) in enumerate(pairs):
                    last = nc.tensor.matmul(psum[0:rows, i % BANKS, 0:cols], lhsT, rhs, start=(j == 0),
                                            stop=(j == len(pairs) - 1))
                last.then_inc(sum_ready, 1)
                if i + 1 == len(flat) or flat[i + 1][0] != b:
                    pe.wait_ge(sum_ready, i + 1)
                    pe.sem_inc(block_used, 1)

        def empty(which, eng, chain):
            n = 0
            for i, (b, rows, cols, pairs, evac, e) in enumerate(flat):
                if e == which:
                    eng.wait_ge(sum_ready, i + 1)
                    if n:
                        eng.wait_ge(emptied[e], n)
                    n += 1
                    evac(chain, psum[0:rows, i % BANKS, 0:cols]).then_inc(emptied[e], 1)

        @block.vector
        def _(dve):
            empty("v", dve, Chain(dve, vec_step))

        @block.scalar
        def _(act):
            empty("a", act, Chain(act, act_step))


def gemm_phase(nc, psum, blocks, tail=None, raw_ring=RAW_RING):
    with ExitStack() as ctx:
        raw = ctx.enter_context(nc.sbuf_tensor(f"w_raw{Phase.count}", [P, raw_ring, QC, NB], F32))
        ring = sbuf_split(ctx, nc, f"w_split{Phase.count}", [P, SPLIT_RING, QC, NB])
        flat, last_of_block, order, done = [], [], [], {"v": 0, "a": 0}
        for b, (src, groups) in enumerate(blocks):
            for g in groups(SplitBlock(ring, b)):
                g = tuple(g)
                bank, start, stop = g[5:8] if len(g) > 5 else (len(flat) % BANKS, True, True)
                flat.append((b,) + g[:5] + (bank, start, stop))
                if g[3] is not None:
                    done[g[4]] += 1
                order.append(done[g[4]])
            last_of_block.append(len(flat) - 1)
        names = [f"raw_loaded{i}" for i in range(raw_ring)] + ["hi_ready", "lo_ready", "quarter_used", "sum_ready",
                                                               "vec_emptied", "act_emptied", "tail_done", "vec_step",
                                                               "act_step"]
        with Phase(nc, names) as (block, *sems):
            raw_loaded = sems[:raw_ring]
            (hi_ready, lo_ready, quarter_used, sum_ready, vec_emptied, act_emptied, tail_done, vec_step,
             act_step) = sems[raw_ring:]
            emptied = {"v": vec_emptied, "a": act_emptied}
            quarters = len(blocks) * QUARTERS

            def width(q):
                return blocks[q // QUARTERS][0].shape[2]

            @block.sync
            def _(sp):
                for q in range(quarters):
                    b, k = divmod(q, QUARTERS)
                    if q >= raw_ring:
                        sp.wait_ge(lo_ready, q - raw_ring + 1)
                    sp.dma_start(raw[:, q % raw_ring, :, 0:width(q)], blocks[b][0][:, k * QC:(k + 1) * QC, :]
                                 ).then_inc(raw_loaded[q % raw_ring], 16)

            @block.tensor
            def _(pe):
                in_bank = {}
                for i, (b, rows, cols, pairs, evac, eng, bank, start, stop) in enumerate(flat):
                    if start and bank in in_bank:
                        before = in_bank[bank]
                        pe.wait_ge(emptied[flat[before][5]], order[before])
                    in_bank[bank] = i
                    for c, (lhsT, rhs) in enumerate(pairs):
                        if c % QC == 0 and (i == 0 or flat[i - 1][0] != b):
                            pe.wait_ge(lo_ready, b * QUARTERS + c // QC + 1)
                        three = parts(lhsT, rhs)
                        for j, (l_, r_) in enumerate(three):
                            last = nc.tensor.matmul(psum[0:rows, bank, 0:cols], l_, r_,
                                                    start=(start and c == 0 and j == 0),
                                                    stop=(stop and c == len(pairs) - 1 and j == len(three) - 1))
                        if i == last_of_block[b] and c % QC == QC - 1 and c < DC - 1:
                            last.then_inc(quarter_used, 1)
                    last.then_inc(sum_ready, 1)

            def each(eng, which, split, chain):
                n = 0

                def quarter(q):
                    if q < quarters:
                        split(q, width(q))
                for q in range(QUARTERS):
                    quarter(q)
                for b in range(len(blocks)):
                    groups = [i for i in range(len(flat)) if flat[i][0] == b]
                    for i in groups:
                        if i == groups[0]:
                            for q in range(SPLIT_RING - QUARTERS):
                                quarter((b + 1) * QUARTERS + q)
                        if i == groups[-1]:
                            for q in range(SPLIT_RING - QUARTERS, QUARTERS):
                                quarter((b + 1) * QUARTERS + q)
                        _b, rows, cols, pairs, evac, e, bank = flat[i][:7]
                        if e == which and evac is not None:
                            eng.wait_ge(sum_ready, i + 1)
                            if n:
                                eng.wait_ge(emptied[e], n)
                            if tail is not None and n >= 2:
                                eng.wait_ge(tail_done, n - 1)
                            n += 1
                            evac(chain, psum[0:rows, bank, 0:cols]).then_inc(emptied[e], 1)

            @block.scalar
            def _(act):
                def split(q, w):
                    act.wait_ge(raw_loaded[q % raw_ring], 16 * (q // raw_ring + 1))
                    if q >= SPLIT_RING:
                        b, k = divmod(q - SPLIT_RING, QUARTERS)
                        if k < QUARTERS - 1:
                            act.wait_ge(quarter_used, b * (QUARTERS - 1) + k + 1)
                        else:
                            act.wait_ge(sum_ready, last_of_block[b] + 1)
                    nc.scalar.copy(ring.hi[:, q % SPLIT_RING, :, 0:w], raw[:, q % raw_ring, :, 0:w]
                                   ).then_inc(hi_ready, 1)
                each(act, "a", split, Chain(act, act_step))

            @block.vector
            def _(dve):
                def split(q, w):
                    dve.wait_ge(hi_ready, q + 1)
                    nc.vector.tensor_tensor(ring.lo[:, q % SPLIT_RING, :, 0:w], raw[:, q % raw_ring, :, 0:w],
                                            ring.hi[:, q % SPLIT_RING, :, 0:w].bitcast(F32), ALU.subtract
                                            ).then_inc(lo_ready, 1)
                each(dve, "v", split, Chain(dve, vec_step))

            @block.gpsimd
            def _(pool):
                if tail is not None:
                    for n in range(done["a"]):
                        pool.wait_ge(act_emptied, n + 1)
                        tail(n).then_inc(tail_done, 1)


def split_phase(nc, src, dst, spill=None, source=None):
    with Phase(nc, ["hi_ready", "spilled"] + [f"chunk_loaded{c}" for c in range(DC)]) as (
            block, hi_ready, spilled, *chunk_loaded):
        @block.sync
        def _(sp):
            if spill is not None:
                sp.dma_start(*spill).then_inc(spilled, 16)
                sp.wait_ge(spilled, 16)
            if source is not None:
                for c in range(DC):
                    sp.dma_start(src[:, c, :], source[:, c, :]).then_inc(chunk_loaded[c], 16)

        @block.scalar
        def _(act):
            for c in range(DC):
                if source is not None:
                    act.wait_ge(chunk_loaded[c], 16)
                nc.scalar.copy(dst.hi[:, c, :], src[:, c, :]).then_inc(hi_ready, 1)

        @block.vector
        def _(dve):
            for c in range(DC):
                dve.wait_ge(hi_ready, c + 1)
                nc.vector.tensor_tensor(dst.lo[:, c, :], src[:, c, :], dst.hi[:, c, :].bitcast(F32), ALU.subtract)


def hybrid_layer(nc, l, T):
    psum, ident, x = T["psum"], T["ident"], T["x"]
    cols, stats = T["cols"], T["stats"]
    I = T["in"]
    load_phase(nc, [(cols[:, 0:DC], I["norm1_g"][l]), (cols[:, 8:16], I["norm2_g"][l]),
                    (T["taps"][:], I["conv_w"][l]), (T["gate_b"][:], I["gate_b"][l]),
                    (T["hng"][:], I["head_norm_g"][l].to_broadcast([P, 512]))])

    def scale_chunk(first, hT):
        def finish(chain, c, acc):
            g = cols[:, first + c:first + c + 1]
            chain.after(nc.vector.tensor_scalar(hT.hi[:, c, :], acc, g, None, ALU.mult))
            nc.vector.scalar_tensor_tensor(hT.lo[:, c, :], acc, g, hT.hi[:, c, :].bitcast(F32), ALU.mult, ALU.subtract)
        return finish

    def normalise(first, hT):
        with nc.sbuf_tensor(f"norm_scratch{first}", [P, 2 + ST, D], F32) as scr:
            norm_phase(nc, psum, ident, x, ST, (scr[:, 0:2], scr[:, 2:]), stats, scale_chunk(first, hT))

    mixing = ExitStack()
    y = mixing.enter_context(nc.sbuf_tensor("y", [P, ST, D], F32))
    with ExitStack() as ctx:
        def sb(name, shape, dt=F32):
            return ctx.enter_context(nc.sbuf_tensor(name, shape, dt))
        qkpad = sb("qkpad", [P, 8, S + 4])
        v_ext = sb("v_ext", [P, ST, M_HEADS, M_DIM + 1])
        mo = sb("mo", [P, ST, 512])
        aqk = sb("aqk", [P, 8, S])
        av = sb("av", [P, ST, 512])
        gates = sb("gates", [4, 4, S])
        normed = ExitStack()
        hT = sbuf_split(normed, nc, "hT", [P, DC, S])
        normalise(0, hT)

        def channel_major(dst):
            def groups(w):
                def evac_v(j):
                    return lambda ch, acc: nc.vector.tensor_copy(dst(j), acc)

                def evac_a(j):
                    return lambda ch, acc: nc.scalar.copy(dst(j), acc)
                return [(P, S, [(w[:, c, j * P:(j + 1) * P], hT[:, c, :]) for c in range(DC)],
                         (evac_v if j % 2 == 0 else evac_a)(j), "va"[j % 2]) for j in range(4)]
            return groups

        def token_major(evac_v, evac_a):
            def groups(w):
                return [(P, NB, [(hT[:, c, t * P:(t + 1) * P], w[:, c, :]) for c in range(DC)],
                         (lambda ch, acc, t=t: evac_v(t, acc)) if t % 2 == 0 else
                         (lambda ch, acc, t=t: evac_a(t, acc)), "va"[t % 2]) for t in range(ST)]
            return groups

        def v_dst(t):
            return v_ext[:, t, :, 0:M_DIM]

        def heads(acc):
            return acc.rearrange("p (h d) -> p h d", h=M_HEADS)

        def gate_groups(w):
            def evac(s_):
                at = slice(32 * s_, 32 * s_ + 4)
                return lambda ch, acc: nc.vector.tensor_scalar(gates[:, s_, :], acc[at, :], T["gate_b"][at, :], None,
                                                               ALU.add)

            def four(ch, acc):
                for s_ in range(3):
                    ch.after(evac(s_)(ch, acc))
                return evac(3)(ch, acc)
            return [(P, S, [(w[:, c, 0:P], hT[:, c, :]) for c in range(DC)], four, "v")]

        W = I["w_in"]
        blocks = [
            (W[l, 0], channel_major(lambda j: qkpad[:, j, 2:2 + S])),
            (W[l, 1], channel_major(lambda j: qkpad[:, 4 + j, 2:2 + S])),
            (I["w_gates"][l], gate_groups),
            (W[l, 2], token_major(lambda t, acc: nc.vector.tensor_copy(v_dst(t), heads(acc)),
                                  lambda t, acc: nc.scalar.copy(v_dst(t), heads(acc)))),
            (W[l, 3], token_major(lambda t, acc: nc.vector.tensor_copy(mo[:, t, :], acc),
                                  lambda t, acc: nc.scalar.copy(mo[:, t, :], acc))),
            (W[l, 4], channel_major(lambda j: aqk[:, j, :])),
            (W[l, 5], channel_major(lambda j: aqk[:, 4 + j, :])),
            (W[l, 6], token_major(lambda t, acc: nc.vector.tensor_copy(av[:, t, :], acc),
                                  lambda t, acc: nc.scalar.copy(av[:, t, :], acc))),
        ]
        gemm_phase(nc, psum, blocks, raw_ring=2)
        normed.close()
        T["conv_room"] = sb("conv_room", [P, 8, S])
        T["weighted"] = sb("weighted", [P, 2, ST, S])
        mlstm_phase(nc, T, qkpad, v_ext, mo, gates, y)
        attention_phase(nc, T, aqk, av, y)
    yT = sbuf_split(mixing, nc, "yT", [P, DC, S])
    transpose_phase(nc, psum, ident, y, yT)

    def out_groups(half, src, dst):
        def groups(w):
            return [(P, NB, [(src[:, c, t * P:(t + 1) * P], w[:, c, :]) for c in range(DC)],
                     lambda ch, acc, t=t: nc.vector.tensor_tensor(dst[:, t, half * NB:(half + 1) * NB], acc,
                                                                  dst[:, t, half * NB:(half + 1) * NB], ALU.add), "v")
                    for t in range(ST)]
        return groups

    gemm_phase(nc, psum, [(I["w_out"][l, n], out_groups(n, yT, x)) for n in range(2)])
    mixing.close()
    HB = FF // P // 2
    with ExitStack() as ctx:
        hT = sbuf_split(ctx, nc, "hT_mlp", [P, DC, S])
        normalise(8, hT)
        uT = sbuf_split(ctx, nc, "uT", [P, HB, S])
        relu = ctx.enter_context(nc.sbuf_tensor("relu", [P, S], F32))
        squares = ctx.enter_context(nc.sbuf_tensor("relu_squares", [P, 2, S], F32))
        for half in range(2):
            def up_groups(b):
                def groups(w):
                    def evac(j):
                        def f(ch, acc):
                            k = 4 * b + j
                            ch.after(nc.scalar.activation(relu[:], acc, ACT.Relu))
                            ch.after(nc.scalar.activation(squares[:, k % 2, :], relu[:], ACT.Square))
                            return nc.scalar.copy(uT.hi[:, k, :], squares[:, k % 2, :])
                        return f
                    return [(P, S, [(w[:, c, j * P:(j + 1) * P], hT[:, c, :]) for c in range(DC)], evac(j), "a")
                            for j in range(4)]
                return groups

            def low_part(k):
                return nc.gpsimd.tensor_tensor(uT.lo[:, k, :], squares[:, k % 2, :], uT.hi[:, k, :].bitcast(F32),
                                               ALU.subtract)
            gemm_phase(nc, psum, [(I["w_up"][l, HB // 4 * half + b], up_groups(b)) for b in range(HB // 4)],
                       tail=low_part)

            def down_groups(n, kb):
                def groups(w):
                    last = kb == HB // DC - 1

                    def evac(t):
                        dst = x[:, t, n * NB:(n + 1) * NB]
                        return lambda ch, acc: nc.vector.tensor_tensor(dst, acc, dst, ALU.add)
                    return [(P, NB, [(uT[:, kb * DC + c, t * P:(t + 1) * P], w[:, c, :]) for c in range(DC)],
                             evac(t) if last else None, "v", n * ST + t, kb == 0, last) for t in range(ST)]
                return groups
            gemm_phase(nc, psum, [(I["w_down"][l, n, HB // DC * half + kb], down_groups(n, kb))
                                  for n in range(2) for kb in range(HB // DC)])


def transpose_phase(nc, psum, ident, src, dst):
    with Phase(nc, ["chunk_transposed", "hi_ready"]) as (block, chunk_transposed, hi_ready):
        @block.tensor
        def _(pe):
            for c in range(DC):
                for t in range(ST):
                    last = nc.tensor.transpose(psum[:, c, t * P:(t + 1) * P], src[:, t, c * P:(c + 1) * P], ident[:])
                last.then_inc(chunk_transposed, 1)

        @block.scalar
        def _(act):
            for c in range(DC):
                act.wait_ge(chunk_transposed, c + 1)
                nc.scalar.copy(dst.hi[:, c, :], psum[:, c, :]).then_inc(hi_ready, 1)

        @block.vector
        def _(dve):
            for c in range(DC):
                dve.wait_ge(hi_ready, c + 1)
                nc.vector.tensor_tensor(dst.lo[:, c, :], psum[:, c, :], dst.hi[:, c, :].bitcast(F32), ALU.subtract)


def mlstm_phase(nc, T, qkpad, v_ext, mo, gates, y):
    psum, ident = T["psum"], T["ident"]
    taps, hng, maskF, maskB, selneg = T["taps"], T["hng"], T["maskF"], T["maskB"], T["selneg"]
    SCALE = M_DIM ** -0.5
    with ExitStack() as ctx:
        def sb(name, shape, dt=F32):
            return ctx.enter_context(nc.sbuf_tensor(name, shape, dt))
        qk = T["conv_room"]
        conv = sb("conv", [P, 2, S])
        lse = sb("lse", [4, 2, S])
        G = sb("G", [4, 2, S])
        F = sb("F", [4, 2, S])
        M = sb("M", [4, 2, S])
        E = sb("E", [4, 2, S])
        gcol = sb("gcol", [P, 2, 2, ST, 4])
        wt = sb("wt", [P, 2, S])
        we = sb("we", [P, 2, S])
        prod = T["weighted"]
        den = sb("den", [P, 2, ST])
        hm = sb("hm", [P, ST, M_DIM])
        junk = sb("junk", [P, M_DIM])
        ss = sb("ss", [P, 3, ST])
        names = ["pads_zero", "convolved", "activated", "logs_taken", "floor_taken", "gates_ready", "cols_transposed",
                 "cols_copied", "scores_ready", "scores_used", "maxima_ready", "exponents_ready", "weights_ready",
                 "prod_ready", "values_ready", "values_used", "squares_ready", "root_taken", "gate_opened",
                 "vec_step", "act_step"]
        with Phase(nc, names) as (block, pads_zero, convolved, activated, logs_taken, floor_taken, gates_ready,
                                  cols_transposed, cols_copied, scores_ready, scores_used, maxima_ready,
                                  exponents_ready, weights_ready, prod_ready, values_ready, values_used,
                                  squares_ready, root_taken, gate_opened, vec_step, act_step):

            @block.gpsimd
            def _(pool):
                nc.gpsimd.memset(qkpad[:, :, 0:2], 0.0).then_inc(pads_zero, 1)
                nc.gpsimd.memset(qkpad[:, :, S + 2:S + 4], 0.0).then_inc(pads_zero, 1)
                nc.gpsimd.memset(v_ext[:, :, :, M_DIM:M_DIM + 1], 1.0).then_inc(pads_zero, 1)

            @block.vector
            def _(dve):
                chain = Chain(dve, vec_step)
                dve.wait_ge(logs_taken, 1)
                chain.after(nc.vector.scalar_tensor_tensor(lse[:], gates[:, 2:4, :], 0.0, lse[:], ALU.min, ALU.subtract))
                ones = wt[0:4, 0, :]
                chain.after(nc.vector.memset(ones, 1.0))
                for d in range(2):
                    def run(ap):
                        return ap if d == 0 else ap[:, ::-1]
                    chain.after(nc.vector.tensor_tensor_scan(run(F[:, d, :]), ones, run(lse[:, d, :]), 0.0, ALU.mult,
                                                             ALU.add))
                    chain.after(nc.vector.tensor_tensor(G[:, d, :], gates[:, d, :], F[:, d, :], ALU.subtract))
                    chain.after(nc.vector.tensor_tensor_scan(run(M[:, d, :]), ones, run(G[:, d, :]), -3e38, ALU.mult,
                                                             ALU.max))
                    chain.after(nc.vector.tensor_tensor(E[:, d, :], F[:, d, :], M[:, d, :], ALU.add))
                dve.sem_inc(gates_ready, 1)
                dve.wait_ge(pads_zero, 3)
                for j in range(8):
                    c = conv[:, j % 2, :]
                    if j >= 2:
                        dve.wait_ge(activated, j - 1)
                    chain.after(nc.vector.tensor_scalar(c, qkpad[:, j, 0:S], taps[:, 8 * 0 + j:8 * 0 + j + 1], None,
                                                        ALU.mult))
                    for k in range(1, 5):
                        ins = nc.vector.scalar_tensor_tensor(c, qkpad[:, j, k:k + S], taps[:, 8 * k + j:8 * k + j + 1],
                                                             c, ALU.mult, ALU.add)
                        if k < 4:
                            chain.after(ins)
                    ins.then_inc(convolved, 1)
                dve.wait_ge(cols_transposed, 1)
                nc.vector.tensor_copy(gcol[:], psum[:, 7, 0:64].rearrange("p (a d t h) -> p a d t h", a=2, d=2, t=ST)
                                      ).then_inc(cols_copied, 1)
                dve.wait_ge(cols_copied, 1)
                dve.wait_ge(gate_opened, 1)
                for t in range(ST):
                    chain.after(nc.vector.tensor_tensor(mo[:, t, :], mo[:, t, :], hng[:], ALU.mult))
                u = 0
                for h in range(M_HEADS):
                    for d in range(2):
                        n = 2 * h + d
                        dve.wait_ge(maxima_ready, n + 1)
                        for j in range(ST):
                            lo, hi = (j * P, S) if d == 0 else (0, (j + 1) * P)
                            mask = maskF[:, 0:S - j * P] if d == 0 else maskB[:, S - (j + 1) * P:S]
                            if u >= 2:
                                dve.wait_ge(weights_ready, u - 1)
                            nc.vector.scalar_tensor_tensor(wt[:, u % 2, lo:hi], psum[:, 4, lo:hi],
                                                           gcol[:, 0, d, j, h:h + 1], mask, ALU.add, ALU.add
                                                           ).then_inc(exponents_ready, 1)
                            u += 1
                            dve.wait_ge(weights_ready, u)
                            if j == 0:
                                dve.wait_ge(scores_ready, h + 1)
                                if n >= 2:
                                    dve.wait_ge(values_ready, n - 1)
                            nc.vector.scalar_tensor_tensor(prod[:, n % 2, j, lo:hi], psum[:, j, lo:hi], SCALE,
                                                           we[:, (u - 1) % 2, lo:hi], ALU.mult, ALU.mult
                                                           ).then_inc(prod_ready, 1)
                        dve.wait_ge(values_ready, n + 1)
                        O = psum[:, 5:7, :].rearrange("p b (i c) -> p b i c", i=2)
                        dn = den[:, 0, :].rearrange("p (b i) -> p b i", b=2)
                        neg = den[:, 1, :].rearrange("p (b i) -> p b i", b=2)
                        chain.after(nc.vector.tensor_scalar(neg, O[:, :, :, M_DIM], -1.0, None, ALU.mult))
                        chain.after(nc.vector.tensor_tensor(dn, O[:, :, :, M_DIM], neg, ALU.max))
                        chain.after(nc.vector.tensor_tensor(den[:, 0, :], den[:, 0, :], gcol[:, 1, d, :, h], ALU.max))
                        chain.after(nc.vector.reciprocal(den[:, 1, :], den[:, 0, :]))
                        for t in range(ST):
                            o = O[:, t // 2, t % 2, 0:M_DIM]
                            if d == 0:
                                chain.after(nc.vector.tensor_scalar(hm[:, t, :], o, den[:, 1, t:t + 1], None, ALU.mult))
                            else:
                                chain.after(nc.vector.scalar_tensor_tensor(hm[:, t, :], o, den[:, 1, t:t + 1],
                                                                           hm[:, t, :], ALU.mult, ALU.add))
                        dve.sem_inc(values_used, 1)
                    for t in range(ST):
                        chain.after(nc.vector.tensor_tensor(junk[:], hm[:, t, :], hm[:, t, :], ALU.mult))
                        chain.after(nc.vector.reduce_sum(ss[:, 0, t:t + 1], junk[:], AX.X))
                    nc.vector.tensor_scalar(ss[:, 1, :], ss[:, 0, :], 1.0 / M_DIM, EPS, ALU.mult, ALU.add
                                            ).then_inc(squares_ready, 1)
                    dve.wait_ge(root_taken, h + 1)
                    chain.after(nc.vector.reciprocal(ss[:, 0, :], ss[:, 2, :]))
                    for t in range(ST):
                        ins = nc.vector.scalar_tensor_tensor(y[:, t, h * M_DIM:(h + 1) * M_DIM], hm[:, t, :],
                                                             ss[:, 0, t:t + 1], mo[:, t, h * M_DIM:(h + 1) * M_DIM],
                                                             ALU.mult, ALU.mult)
                    chain.after(ins)

            @block.scalar
            def _(act):
                chain = Chain(act, act_step)
                z = gates[:, 2:4, :]
                chain.after(nc.scalar.activation(lse[:], z, ACT.Abs))
                chain.after(nc.scalar.activation(lse[:], lse[:], ACT.Exp, scale=-1.0))
                nc.scalar.activation(lse[:], lse[:], ACT.Ln, bias=T["one"][0:4, :]).then_inc(logs_taken, 1)
                act.wait_ge(gates_ready, 1)
                nc.scalar.activation(E[:], E[:], ACT.Exp, scale=-1.0).then_inc(floor_taken, 1)
                nc.scalar.activation(mo[:], mo[:], ACT.Sigmoid).then_inc(gate_opened, 1)
                for j in range(8):
                    act.wait_ge(convolved, j + 1)
                    nc.scalar.activation(qk[:, j, :], conv[:, j % 2, :], ACT.Silu).then_inc(activated, 1)
                u = 0
                for h in range(M_HEADS):
                    for d in range(2):
                        for j in range(ST):
                            lo, hi = (j * P, S) if d == 0 else (0, (j + 1) * P)
                            act.wait_ge(exponents_ready, u + 1)
                            if u >= 2:
                                act.wait_ge(prod_ready, u - 1)
                            nc.scalar.activation(we[:, u % 2, lo:hi], wt[:, u % 2, lo:hi], ACT.Exp
                                                 ).then_inc(weights_ready, 1)
                            u += 1
                    act.wait_ge(squares_ready, h + 1)
                    nc.scalar.activation(ss[:, 2, :], ss[:, 1, :], ACT.Sqrt).then_inc(root_taken, 1)

            @block.tensor
            def _(pe):
                pe.wait_ge(floor_taken, 1)
                for a, src in enumerate((G, E)):
                    for d in range(2):
                        for t in range(ST):
                            k = ((a * 2 + d) * ST + t) * 4
                            last = nc.tensor.transpose(psum[:, 7, k:k + 4], src[:, d, t * P:(t + 1) * P],
                                                       ident[0:4, 0:4])
                last.then_inc(cols_transposed, 1)
                pe.wait_ge(activated, 8)
                for h in range(M_HEADS):
                    if h >= 1:
                        pe.wait_ge(prod_ready, 8 * h)
                    for j in range(ST):
                        last = nc.tensor.matmul(psum[:, j, :], qk[:, 4 + h, j * P:(j + 1) * P], qk[:, h, :],
                                                start=True, stop=True)
                    last.then_inc(scores_ready, 1)
                    for d in range(2):
                        n = 2 * h + d
                        if n >= 1:
                            pe.wait_ge(exponents_ready, 4 * n)
                        nc.tensor.matmul(psum[:, 4, :], selneg[:, h, :], M[:, d, :], start=True, stop=True
                                         ).then_inc(maxima_ready, 1)
                        pe.wait_ge(prod_ready, 4 * (n + 1))
                        if n >= 1:
                            pe.wait_ge(values_used, n)
                        for t in range(ST):
                            src = list(range(0, t + 1)) if d == 0 else list(range(t, ST))
                            for k, j in enumerate(src):
                                last = nc.tensor.matmul(psum[:, 5 + t // 2, (t % 2) * 256:(t % 2) * 256 + M_DIM + 1],
                                                        prod[:, n % 2, j, t * P:(t + 1) * P], v_ext[:, j, h, :],
                                                        start=(k == 0), stop=(k == len(src) - 1))
                        last.then_inc(values_ready, 1)


def attention_phase(nc, T, aqk, av, y):
    psum, ident, rot, cosT, sinT, amask = T["psum"], T["ident"], T["rot"], T["cosT"], T["sinT"], T["amask"]
    SCALE = A_DIM ** -0.5
    UNITS = A_HEADS * ST
    with ExitStack() as ctx:
        def sb(name, shape, dt=F32):
            return ctx.enter_context(nc.sbuf_tensor(name, shape, dt))
        turned = sb("turned", [P, 8, S])
        part = sb("part", [P, 2, S])
        sc = sb("sc", [P, 2, S])
        pr = sb("pr", [P, 2, S])
        pT = sb("pT", [P, 2, S])
        st = sb("st", [P, 4, UNITS])
        names = ["rotated", "turned_ready", "scores_ready", "scores_masked", "probs_ready", "probs_turned",
                 "turned_copied", "values_ready", "out_ready", "vec_step"]
        with Phase(nc, names) as (block, rotated, turned_ready, scores_ready, scores_masked, probs_ready,
                                  probs_turned, turned_copied, values_ready, out_ready, vec_step):
            @block.tensor
            def _(pe):
                for j in range(8):
                    nc.tensor.matmul(psum[:, j, :], rot[:], aqk[:, j, :], start=True, stop=True).then_inc(rotated, 1)
                pe.wait_ge(turned_ready, 8)

                def scores(u):
                    h, i = divmod(u, ST)
                    lo = 64 * (h % 2)
                    if u >= 2:
                        pe.wait_ge(scores_masked, u - 1)
                    nc.tensor.matmul(psum[:, u % 2, :], turned[lo:lo + 64, h // 2, i * P:(i + 1) * P],
                                     turned[lo:lo + 64, 4 + h // 2, :], start=True, stop=True).then_inc(scores_ready, 1)

                def turn(u):
                    pe.wait_ge(probs_ready, u + 1)
                    if u >= 2:
                        pe.wait_ge(turned_copied, u - 1)
                    for k in range(ST):
                        last = nc.tensor.transpose(psum[:, 2 + u % 2, k * P:(k + 1) * P],
                                                   pr[:, u % 2, k * P:(k + 1) * P], ident[:])
                    last.then_inc(probs_turned, 1)

                def values(u):
                    h, i = divmod(u, ST)
                    pe.wait_ge(turned_copied, u + 1)
                    if u >= 2:
                        pe.wait_ge(out_ready, u - 1)
                    for k in range(ST):
                        last = nc.tensor.matmul(psum[:, 4 + u % 2, 0:A_DIM], pT[:, u % 2, k * P:(k + 1) * P],
                                                av[:, k, h * A_DIM:(h + 1) * A_DIM], start=(k == 0), stop=(k == ST - 1))
                    last.then_inc(values_ready, 1)

                scores(0)
                for u in range(UNITS + 1):
                    if u + 1 < UNITS:
                        scores(u + 1)
                    if u < UNITS:
                        turn(u)
                    if u >= 1:
                        values(u - 1)

            @block.vector
            def _(dve):
                chain = Chain(dve, vec_step)
                for j in range(8):
                    dve.wait_ge(rotated, j + 1)
                    if j >= 1:
                        dve.wait_ge(turned_ready, j)
                    chain.after(nc.vector.tensor_tensor(part[:, 0, :], psum[:, j, :], sinT[:], ALU.mult))
                    chain.after(nc.vector.tensor_tensor(part[:, 1, :], aqk[:, j, :], cosT[:], ALU.mult))
                    nc.vector.tensor_tensor(turned[:, j, :], part[:, 0, :], part[:, 1, :], ALU.add
                                            ).then_inc(turned_ready, 1)

                def mask(u):
                    dve.wait_ge(scores_ready, u + 1)
                    if u >= 2:
                        dve.wait_ge(probs_ready, u - 1)
                    chain.after(nc.vector.scalar_tensor_tensor(sc[:, u % 2, :], psum[:, u % 2, :], SCALE,
                                                               amask[:, u % ST, :], ALU.mult, ALU.add))
                    nc.vector.tensor_reduce(st[:, 0, u:u + 1], sc[:, u % 2, :], AX.X, ALU.max, negate=True
                                            ).then_inc(scores_masked, 1)

                def out(u):
                    h, i = divmod(u, ST)
                    chain.after(nc.vector.reciprocal(st[:, 2, u:u + 1], st[:, 1, u:u + 1]))
                    dve.wait_ge(values_ready, u + 1)
                    nc.vector.tensor_scalar(y[:, i, 512 + h * A_DIM:512 + (h + 1) * A_DIM], psum[:, 4 + u % 2, 0:A_DIM],
                                            st[:, 2, u:u + 1], None, ALU.mult).then_inc(out_ready, 1)

                mask(0)
                for u in range(UNITS + 1):
                    if u + 1 < UNITS:
                        mask(u + 1)
                    if u >= 1:
                        out(u - 1)

            @block.scalar
            def _(act):
                def probs(u):
                    act.wait_ge(scores_masked, u + 1)
                    if u >= 2:
                        act.wait_ge(probs_turned, u - 1)
                    nc.scalar.activation(pr[:, u % 2, :], sc[:, u % 2, :], ACT.Exp, bias=st[:, 0, u:u + 1],
                                         accum_out=st[:, 1, u:u + 1]).then_inc(probs_ready, 1)

                def copy(u):
                    act.wait_ge(probs_turned, u + 1)
                    if u >= 2:
                        act.wait_ge(values_ready, u - 1)
                    nc.scalar.copy(pT[:, u % 2, :], psum[:, 2 + u % 2, :]).then_inc(turned_copied, 1)

                probs(0)
                for u in range(UNITS):
                    if u + 1 < UNITS:
                        probs(u + 1)
                    copy(u)


def constants():
    import numpy as np
    f = np.float32
    out = {"ident": np.eye(P, dtype=f)}
    p, q = np.arange(P)[:, None], np.arange(S)[None, :]
    out["maskF"] = np.where((q < P) & (q < p), NEG, 0.0).astype(f)
    out["maskB"] = np.where((q >= S - P) & (q - (S - P) > p), NEG, 0.0).astype(f)
    sel = np.zeros((4, 4, P), f)
    for h in range(4):
        sel[h, h, :] = -1.0
    out["selneg"] = sel
    rot = np.zeros((P, P), f)
    for m in range(P):
        if m % 64 < 32:
            rot[m + 32, m] = -1.0
        else:
            rot[m - 32, m] = 1.0
    out["rot"] = rot
    inv = (f(10000.0) ** (-np.arange(32, dtype=f) / f(32))).astype(f)
    ang = np.arange(S, dtype=f)[None, :] * inv[np.arange(P) % 32][:, None]
    out["cosT"], out["sinT"] = np.cos(ang).astype(f), np.sin(ang).astype(f)
    qq, kk = np.arange(S)[:, None], np.arange(S)[None, :]
    dd = np.abs(qq - kk)
    cnt = (dd <= 64).astype(int) + ((dd % 4 == 0) & (dd <= 256)) + (dd % 16 == 0)
    m = np.where(cnt > 0, np.log(np.maximum(cnt, 1)), NEG).astype(f)
    out["amask"] = np.ascontiguousarray(m.reshape(ST, P, S).transpose(1, 0, 2))
    return out


CTX = 256
CT = CTX // P
N_ALL = CTX + S
AT = N_ALL // P
DA_HEADS, DA_QK = 8, 64
L_CH = 64
NCH = N_ALL // L_CH
CCH = CTX // L_CH
XCH = NCH - CCH
LEVELS = 5
RW_LN_EPS = 64e-5
DECAY = 0.6065306597126334
LAM_INIT = 0.2
PEER_HEADS, N_KEYS, TOPK = 8, 128, 16
SLOTS = PEER_HEADS * TOPK
RING = 6


def modulation_phases(nc, T, wbuf):
    I, psum = T["in"], T["psum"]
    with nc.sbuf_tensor("csil", [P, DC, 2], F32) as csil, nc.sbuf_tensor("cwide", [P, DC, P], F32) as cwide, \
            nc.sbuf_tensor("bcol", [P, 6, DC], F32) as bcol, nc.sbuf_tensor("gn", [P, 2, DC], F32) as gn, \
            nc.sbuf_tensor("modc", [P, 6, DC, 2], F32) as modc:
        load_phase(nc, [(csil[:], I["c"]), (bcol[:], I["b_mod"]), (gn[:, 0, :], I["norm1_g_2"]),
                        (gn[:, 1, :], I["norm2_g_2"])] +
                   [(T["gate_rows"][:, k, :], I["b_mod_rows"][:, m * D:(m + 1) * D].to_broadcast([P, D]))
                    for k, m in enumerate((2, 5))])
        with Phase(nc, ["silu_taken", "widened"]) as (block, silu_taken, widened):
            @block.scalar
            def _(act):
                nc.scalar.activation(csil[:], csil[:], ACT.Silu).then_inc(silu_taken, 1)

            @block.vector
            def _(dve):
                dve.wait_ge(silu_taken, 1)
                nc.vector.tensor_copy(cwide[:], csil[:, :, 0:1].to_broadcast([P, DC, P])).then_inc(widened, 1)

        def column_groups(m, half):
            def groups(w):
                def evac(j):
                    k = half * 4 + j
                    return lambda ch, acc: nc.vector.tensor_scalar(modc[:, m, k, :], acc, bcol[:, m, k:k + 1], None,
                                                                   ALU.add)
                return [(P, 2, [(w[:, c, j * P:(j + 1) * P], csil[:, c, :]) for c in range(DC)], evac(j), "v")
                        for j in range(4)]
            return groups

        def row_groups(k, half):
            def groups(w):
                dst = T["gate_rows"][:, k, half * NB:(half + 1) * NB]
                return [(P, NB, [(cwide[:, c, :], w[:, c, :]) for c in range(DC)],
                         lambda ch, acc: nc.vector.tensor_tensor(dst, acc, dst, ALU.add), "v")]
            return groups
        blocks = []
        for m in range(6):
            for half in range(2):
                g = row_groups(m // 3, half) if m in (2, 5) else column_groups(m, half)
                blocks.append((I["w_mod"][2 * m + half], g))
        plain_gemm_phase(nc, psum, wbuf, blocks)
        with Phase(nc, ["vec_step"]) as (block, vec_step):
            @block.vector
            def _(dve):
                chain = Chain(dve, vec_step)
                for k, (m, col, g) in enumerate(((0, 0, 0), (0, 1, 0), (3, 0, 1))):
                    chain.after(nc.vector.scalar_tensor_tensor(T["affine"][:, k, 0, :], modc[:, m + 1, :, col], 1.0,
                                                               gn[:, g, :], ALU.add, ALU.mult))
                    chain.after(nc.vector.tensor_copy(T["affine"][:, k, 1, :], modc[:, m, :, col]))


def modulated_norm(nc, T, x, tiles, which, dst, at, scratch):
    A = T["affine"]

    def finish(chain, c, acc):
        return nc.vector.tensor_scalar(dst[:, c, at:at + tiles * P], acc, A[:, which, 0, c:c + 1],
                                       A[:, which, 1, c:c + 1], ALU.mult, ALU.add)
    norm_phase(nc, T["psum"], T["ident"], x, tiles, scratch, T["stats"], finish)


def head_norm_rope_phase(nc, T, q, k, ropeC, ropeS, gq, gk, qT, kT):
    psum, ident = T["psum"], T["ident"]
    with ExitStack() as ctx:
        def sb(name, shape, dt=F32):
            return ctx.enter_context(nc.sbuf_tensor(name, shape, dt))
        tabs = sb("tabs", [P, 2, 2, AT, 64])
        tmp = sb("hn_tmp", [P, 2, D])
        ss = sb("hn_ss", [P, 2, 16])
        jobs = [(q, t, t + CT, 0, qT) for t in range(ST)] + [(k, t, t, 1, kT) for t in range(AT)]
        n_banks = 2
        with Phase(nc, ["sums_ready", "root_taken", "rows_ready", "transposed", "copied", "vec_step"]) as (
                block, sums_ready, root_taken, rows_ready, transposed, copied, vec_step):
            @block.vector
            def _(dve):
                chain = Chain(dve, vec_step)
                for w, g in enumerate((gq, gk)):
                    chain.after(nc.vector.tensor_tensor(tabs[:, w, 0], ropeC, g[:, 0:1, :].to_broadcast([P, AT, 64]),
                                                        ALU.mult))
                    chain.after(nc.vector.tensor_tensor(tabs[:, w, 1], ropeS, g[:, 1:2, :].to_broadcast([P, AT, 64]),
                                                        ALU.mult))
                for n, (src, t, pos, w, dst) in enumerate(jobs):
                    row = src[:, t, :]
                    g3 = row.rearrange("p (g e) -> p g e", e=64)
                    t0 = tmp[:, 0, :].rearrange("p (g e) -> p g e", e=64)
                    t1 = tmp[:, 1, :].rearrange("p (g e) -> p g e", e=64)
                    chain.after(nc.vector.tensor_tensor(tmp[:, 0, :], row, row, ALU.mult))
                    chain.after(nc.vector.reduce_sum(ss[:, 0, :], t0, AX.X))
                    nc.vector.tensor_scalar(ss[:, 0, :], ss[:, 0, :], 1.0 / 64, EPS, ALU.mult, ALU.add
                                            ).then_inc(sums_ready, 1)
                    dve.wait_ge(root_taken, n + 1)
                    chain.after(nc.vector.reciprocal(ss[:, 0, :], ss[:, 1, :]))
                    chain.after(nc.vector.tensor_tensor(g3, g3, ss[:, 0, :].rearrange("p (g o) -> p g o", o=1)
                                                        .to_broadcast([P, 16, 64]), ALU.mult))
                    C = tabs[:, w, 0, pos:pos + 1, :].to_broadcast([P, 16, 64])
                    chain.after(nc.vector.tensor_tensor(t0, g3, C, ALU.mult))
                    for half in range(2):
                        o4 = tmp[:, 1, :].rearrange("p (g a h f) -> p g a h f", g=16, a=2, h=2)[:, :, :, half, :]
                        i4 = row.rearrange("p (g a h f) -> p g a h f", g=16, a=2, h=2)[:, :, :, 1 - half, :]
                        S4 = tabs[:, w, 1, pos, :].rearrange("p (o a h f) -> p o a h f", o=1, a=2, h=2)[
                            :, :, :, half, :].to_broadcast([P, 16, 2, 16])
                        chain.after(nc.vector.tensor_tensor(o4, i4, S4, ALU.mult))
                    nc.vector.tensor_tensor(row, tmp[:, 0, :], tmp[:, 1, :], ALU.add).then_inc(rows_ready, 1)
                    dve.wait_ge(rows_ready, n + 1)

            def copy_out(act, n):
                src, t, pos, w, dst = jobs[n]
                act.wait_ge(transposed, n + 1)
                nc.scalar.copy(dst[:, :, t * P:(t + 1) * P],
                               psum[:, 2 * (n % n_banks):2 * (n % n_banks) + 2, :].rearrange("p b (c t) -> p (b c) t", c=4)
                               ).then_inc(copied, 1)

            @block.scalar
            def _(act):
                for n, (src, t, pos, w, dst) in enumerate(jobs):
                    act.wait_ge(sums_ready, n + 1)
                    nc.scalar.activation(ss[:, 1, :], ss[:, 0, :], ACT.Sqrt).then_inc(root_taken, 1)
                    if n >= 1:
                        copy_out(act, n - 1)
                copy_out(act, len(jobs) - 1)

            @block.tensor
            def _(pe):
                for n, (src, t, pos, w, dst) in enumerate(jobs):
                    pe.wait_ge(rows_ready, n + 1)
                    if n >= n_banks:
                        pe.wait_ge(copied, n - n_banks + 1)
                    for c in range(DC):
                        last = nc.tensor.transpose(psum[:, 2 * (n % n_banks) + c // 4, (c % 4) * P:(c % 4 + 1) * P],
                                                   src[:, t, c * P:(c + 1) * P], ident[:])
                    last.then_inc(transposed, 1)


def diff_attention_phase(nc, T, qT, kT, v, lam, og, oaT, oa):
    psum, ident = T["psum"], T["ident"]
    SCALE = DA_QK ** -0.5
    UNITS = DA_HEADS * ST
    with ExitStack() as ctx:
        def sb(name, shape, dt=F32):
            return ctx.enter_context(nc.sbuf_tensor(name, shape, dt))
        pr = sb("da_pr", [P, 2, 2, N_ALL])
        pT = sb("da_pT", [P, 2, N_ALL])
        nm = sb("da_nm", [P, 2, UNITS])
        ls = sb("da_ls", [P, 2, UNITS])
        ri = sb("da_ri", [P, 3, 2])
        junk = sb("da_junk", [P, P])
        sq = sb("da_sq", [P, 3, UNITS])
        with Phase(nc, ["lam_sums", "lam_exps", "vec_step"]) as (block, lam_sums, lam_exps, vec_step):
            @block.vector
            def _(dve):
                chain = Chain(dve, vec_step)
                l4 = lam["rows"][:].rearrange("p (a b e) -> p a b e", a=2, b=2)
                pr4 = lam["prod"][:].rearrange("p (a e) -> p a e", a=2)
                chain.after(nc.vector.tensor_tensor(pr4, l4[:, :, 0, :], l4[:, :, 1, :], ALU.mult))
                nc.vector.reduce_sum(lam["two"][:, 0, :], pr4, AX.X).then_inc(lam_sums, 1)
                dve.wait_ge(lam_exps, 1)
                chain.after(nc.vector.tensor_tensor(lam["neg"][:], lam["two"][:, 1, 1:2], lam["two"][:, 1, 0:1],
                                                    ALU.subtract))
                chain.after(nc.vector.tensor_scalar(lam["neg"][:], lam["neg"][:], -LAM_INIT, None, ALU.add))

            @block.scalar
            def _(act):
                act.wait_ge(lam_sums, 1)
                nc.scalar.activation(lam["two"][:, 1, :], lam["two"][:, 0, :], ACT.Exp).then_inc(lam_exps, 1)

        names = ["scores_ready", "max_taken", "probs_ready", "diff_ready", "turned_ready", "turned_copied",
                 "values_ready", "out_taken", "vec_step"]
        with Phase(nc, names) as (block, scores_ready, max_taken, probs_ready, diff_ready, turned_ready,
                                  turned_copied, values_ready, out_taken, vec_step):
            def S_of(m):
                return psum[:, 2 * m:2 * m + 2, :].rearrange("p b n -> p (b n)")[:, 0:N_ALL]
            turned = psum[:, 4:6, :].rearrange("p b n -> p (b n)")[:, 0:N_ALL]

            @block.tensor
            def _(pe):
                def scores(u):
                    h, i = divmod(u, ST)
                    for m in range(2):
                        if u >= 1:
                            pe.wait_ge(probs_ready, 2 * (u - 1) + m + 1)
                        lo = 64 * m
                        for a, b in ((0, 512), (512, N_ALL)):
                            last = nc.tensor.matmul(S_of(m)[:, a:b], qT[lo:lo + 64, h, i * P:(i + 1) * P],
                                                    kT[lo:lo + 64, h, a:b], start=True, stop=True)
                        last.then_inc(scores_ready, 1)

                def turn(u):
                    pe.wait_ge(diff_ready, u + 1)
                    if u >= 1:
                        pe.wait_ge(turned_copied, u)
                    for k in range(AT):
                        last = nc.tensor.transpose(turned[:, k * P:(k + 1) * P], pr[:, u % 2, 0, k * P:(k + 1) * P],
                                                   ident[:])
                    last.then_inc(turned_ready, 1)

                def values(u):
                    h, i = divmod(u, ST)
                    pe.wait_ge(turned_copied, u + 1)
                    if u >= 2:
                        pe.wait_ge(out_taken, u - 1)
                    for k in range(AT):
                        last = nc.tensor.matmul(psum[:, 6 + u % 2, 0:P], pT[:, u % 2, k * P:(k + 1) * P],
                                                v[:, k, h * P:(h + 1) * P], start=(k == 0), stop=(k == AT - 1))
                    last.then_inc(values_ready, 1)

                scores(0)
                for u in range(UNITS + 1):
                    if u + 1 < UNITS:
                        scores(u + 1)
                    if u < UNITS:
                        turn(u)
                    if u >= 1:
                        values(u - 1)

            @block.vector
            def _(dve):
                chain = Chain(dve, vec_step)

                def maxima(u):
                    for m in range(2):
                        dve.wait_ge(scores_ready, 2 * u + m + 1)
                        chain.after(nc.vector.tensor_reduce(nm[:, m, u:u + 1], S_of(m), AX.X, ALU.max, negate=True))
                    nc.vector.tensor_scalar(nm[:, :, u:u + 1], nm[:, :, u:u + 1], SCALE, None, ALU.mult
                                            ).then_inc(max_taken, 1)

                def difference(u):
                    dve.wait_ge(probs_ready, 2 * u + 2)
                    chain.after(nc.vector.reciprocal(ri[:, 0:2, u % 2:u % 2 + 1], ls[:, :, u:u + 1]))
                    chain.after(nc.vector.tensor_tensor(ri[:, 2, u % 2:u % 2 + 1], ri[:, 1, u % 2:u % 2 + 1],
                                                        lam["neg"][:], ALU.mult))
                    p = pr[:, u % 2]
                    chain.after(nc.vector.tensor_scalar(p[:, 1, :], p[:, 1, :], ri[:, 2, u % 2:u % 2 + 1], None,
                                                        ALU.mult))
                    nc.vector.scalar_tensor_tensor(p[:, 0, :], p[:, 0, :], ri[:, 0, u % 2:u % 2 + 1], p[:, 1, :],
                                                   ALU.mult, ALU.add).then_inc(diff_ready, 1)

                def out(u):
                    h, i = divmod(u, ST)
                    dve.wait_ge(values_ready, u + 1)
                    o = oa[:, i, h * P:(h + 1) * P]
                    nc.vector.tensor_copy(o, psum[:, 6 + u % 2, 0:P]).then_inc(out_taken, 1)
                    dve.wait_ge(out_taken, u + 1)
                    chain.after(nc.vector.tensor_tensor(junk[:], o, o, ALU.mult))
                    chain.after(nc.vector.reduce_sum(sq[:, 0, u:u + 1], junk[:], AX.X))

                maxima(0)
                for u in range(UNITS + 1):
                    if u < UNITS:
                        difference(u)
                    if u + 1 < UNITS:
                        maxima(u + 1)
                    if u >= 1:
                        out(u - 1)

            @block.scalar
            def _(act):
                def probs(u):
                    act.wait_ge(max_taken, u + 1)
                    if u >= 2:
                        act.wait_ge(turned_ready, u - 1)
                    for m in range(2):
                        nc.scalar.activation(pr[:, u % 2, m, :], S_of(m), ACT.Exp, bias=nm[:, m, u:u + 1], scale=SCALE,
                                             accum_out=ls[:, m, u:u + 1]).then_inc(probs_ready, 1)

                def copy(u):
                    act.wait_ge(turned_ready, u + 1)
                    if u >= 2:
                        act.wait_ge(values_ready, u - 1)
                    nc.scalar.copy(pT[:, u % 2, :], turned).then_inc(turned_copied, 1)

                probs(0)
                for u in range(UNITS):
                    if u + 1 < UNITS:
                        probs(u + 1)
                    copy(u)

        with Phase(nc, ["mean_ready", "root_taken", "rows_ready", "transposed", "vec_step"]) as (
                block, mean_ready, root_taken, rows_ready, transposed, vec_step):
            @block.vector
            def _(dve):
                chain = Chain(dve, vec_step)
                nc.vector.tensor_scalar(sq[:, 1, :], sq[:, 0, :], 1.0 / P, EPS, ALU.mult, ALU.add
                                        ).then_inc(mean_ready, 1)
                dve.wait_ge(root_taken, 1)
                chain.after(nc.vector.reciprocal(sq[:, 0, :], sq[:, 2, :]))
                for u in range(UNITS):
                    h, i = divmod(u, ST)
                    o = oa[:, i, h * P:(h + 1) * P]
                    ins = nc.vector.tensor_scalar(o, o, sq[:, 0, u:u + 1], None, ALU.mult)
                    if i == ST - 1:
                        ins.then_inc(rows_ready, 1)
                for h in range(DA_HEADS):
                    dve.wait_ge(transposed, h + 1)
                    nc.vector.tensor_scalar(oaT[:, h, :], psum[:, h, :], og[:], 1.0 - LAM_INIT, ALU.mult, ALU.mult)

            @block.scalar
            def _(act):
                act.wait_ge(mean_ready, 1)
                nc.scalar.activation(sq[:, 2, :], sq[:, 1, :], ACT.Sqrt).then_inc(root_taken, 1)

            @block.tensor
            def _(pe):
                for h in range(DA_HEADS):
                    pe.wait_ge(rows_ready, h + 1)
                    for i in range(ST):
                        last = nc.tensor.transpose(psum[:, h, i * P:(i + 1) * P], oa[:, i, h * P:(h + 1) * P], ident[:])
                    last.then_inc(transposed, 1)


def rwkv_tile(nc, T, g, R, lora, obT):
    psum, ident, K = T["psum"], T["ident"], T["rwc"]
    z, area, cst = R["z"], R["area"], R["cst"]
    prm, up, gup = R["prm"], R["up"], R["gup"]
    C768 = N_ALL

    def cells(ap):
        return ap.rearrange("p (c t) -> p c t", t=L_CH)

    def wide(ap, n):
        return ap.rearrange("p c (o t) -> p c o t", o=1).to_broadcast([P, n, 2, L_CH])

    def bd(n):
        return cst["bd"][:].rearrange("p (c h t) -> p c h t", c=1, h=2).to_broadcast([P, n, 2, L_CH])

    def mask(ap, n):
        return ap.rearrange("p (c t) -> p c t", c=1).to_broadcast([P, n, L_CH])

    r, k, v = z[:, 0, 0:S], z[:, 1, :], z[:, 2, :]
    qr = R["qr"]
    bt, kt = R["bt"], R["kt"]
    wq, wb, wk, wv = R["wq"], R["wb"], R["wk"], R["wv"]
    wBT, wAT, wXT, wbt, wkt = R["wBT"], R["wAT"], R["wXT"], R["wbt"], R["wkt"]
    Cc, Dd, wV = R["C"], R["D"], R["wV"]
    tmp = R["tmp"]
    pl = R["pl"]

    names = ["tile_loaded", "lora_up", "opened", "kr_ready", "squares_ready", "norms_summed", "root_taken",
             "sums_ready", "exps_ready", "stacked_ready", "widened", "vec_step", "pool_step", "act_step"]
    with Phase(nc, names) as (block, tile_loaded, lora_up, opened, kr_ready, squares_ready, norms_summed, root_taken,
                              sums_ready, exps_ready, stacked_ready, widened, vec_step, pool_step, act_step):
        sig = [tmp[:, 0], tmp[:, 1]]
        a = [tmp[:, 2], tmp[:, 3]]
        kr, kk, Lc, Lm = tmp[:, 4], tmp[:, 5], tmp[:, 6], tmp[:, 7]
        eQ, eR, eK = R["eQ"], R["eR"], R["eK"]

        @block.sync
        def _(sp):
            sp.dma_start(z[:, 0, 0:S], R["zr_d"][g]).then_inc(tile_loaded, 16)
            sp.dma_start(z[:, 1, :], R["zk_d"][g]).then_inc(tile_loaded, 16)
            sp.dma_start(z[:, 2, :], R["zv_d"][g]).then_inc(tile_loaded, 16)
            sp.dma_start(prm[:, 0:9], T["in"]["rw_cols"][g]).then_inc(tile_loaded, 16)
            sp.dma_start(up[:], T["in"]["rw_up"][g]).then_inc(tile_loaded, 16)
            sp.dma_start(gup[:], T["in"]["rw_gup"][g]).then_inc(tile_loaded, 16)

        @block.tensor
        def _(pe):
            pe.wait_ge(tile_loaded, 96)
            for d in range(2):
                for w in range(2):
                    for lo, hi in ((0, 512), (512, C768)):
                        last = nc.tensor.matmul(psum[:, 4 * d + 2 * w + lo // 512, 0:hi - lo],
                                                up[64 * w:64 * w + 64, d, :], lora[64 * w:64 * w + 64, lo:hi],
                                                start=True, stop=True)
                    last.then_inc(lora_up, 1)
            pe.wait_ge(opened, 1)
            pe.wait_ge(squares_ready, 1)
            for lo, hi in ((0, 512), (512, C768)):
                last = nc.tensor.matmul(psum[:, lo // 512, 0:hi - lo], cst["ones"][:], kk[:, lo:hi],
                                        start=True, stop=True)
            last.then_inc(norms_summed, 1)

        def two_banks(b):
            return psum[:, b:b + 2, :].rearrange("p b n -> p (b n)")[:, 0:C768]

        @block.scalar
        def _(act):
            for d in range(2):
                for w, dst in ((0, sig[d]), (1, a[d])):
                    act.wait_ge(lora_up, 2 * d + w + 1)
                    nc.scalar.activation(dst, two_banks(4 * d + 2 * w), ACT.Sigmoid,
                                         bias=prm[:, 2 * w + d:2 * w + d + 1]).then_inc(opened, 1)
            act.wait_ge(kr_ready, 1)
            nc.scalar.activation(kk, kr, ACT.Square).then_inc(squares_ready, 1)
            act.wait_ge(norms_summed, 1)
            nc.scalar.activation(Lc, two_banks(0), ACT.Sqrt, bias=cst["tiny"][:]).then_inc(root_taken, 1)
            for d in range(2):
                act.wait_ge(sums_ready, d + 1)
                if d:
                    act.wait_ge(stacked_ready, 4)
                nc.scalar.activation(eQ, Lm, ACT.Exp, scale=-DECAY).then_inc(exps_ready, 1)
                nc.scalar.activation(eR, Lc, ACT.Exp, scale=-DECAY).then_inc(exps_ready, 1)
                nc.scalar.activation(eK, Lc, ACT.Exp, scale=DECAY).then_inc(exps_ready, 1)

        @block.vector
        def _(dve):
            chain = Chain(dve, vec_step)
            dve.wait_ge(tile_loaded, 96)
            nc.vector.tensor_scalar(kr, k, prm[:, 4:5], None, ALU.mult).then_inc(kr_ready, 1)
            chain.after(nc.vector.tensor_scalar(prm[:, 9:10], prm[:, 5:6], -1.0, 1.0, ALU.mult, ALU.add))
            dve.wait_ge(root_taken, 1)
            chain.after(nc.vector.reciprocal(Lc, Lc))
            chain.after(nc.vector.tensor_tensor(kk, kr, Lc, ALU.mult))
            dve.wait_ge(opened, 4)
            for d in range(2):
                if d:
                    dve.wait_ge(exps_ready, 3)

                def run(ap):
                    return ap if d == 0 else ap[:, ::-1]
                chain.after(nc.vector.tensor_tensor_scan(run(Lc), run(cst["reset"][:, d, :]), run(sig[d]), 0.0,
                                                         ALU.mult, ALU.add))
                nc.vector.tensor_tensor(Lm, Lc, sig[d], ALU.subtract).then_inc(sums_ready, 1)
                chain.after(nc.vector.tensor_tensor(bt[:, d], kk, a[d], ALU.mult))
                chain.after(nc.vector.tensor_scalar(a[d], a[d], prm[:, 5:6], prm[:, 9:10], ALU.mult, ALU.add))
                chain.after(nc.vector.tensor_tensor(kt[:, d], k, a[d], ALU.mult))
                dve.wait_ge(exps_ready, 3 * d + 3)
                nc.vector.tensor_tensor(qr[:, d, :, 0, :], cells(kk), cells(eQ), ALU.mult).then_inc(stacked_ready, 1)
                nc.vector.tensor_tensor(qr[:, d, CCH:, 1, :], cells(r), cells(eR)[:, CCH:, :], ALU.mult
                                        ).then_inc(stacked_ready, 1)
                nc.vector.tensor_tensor(bt[:, d], bt[:, d], eK, ALU.mult).then_inc(stacked_ready, 1)
                chain.after(nc.vector.tensor_copy(pl[:, d, :], cells(eR)[:, :, (L_CH - 1) * (1 - d)]))
                nc.vector.tensor_tensor(kt[:, d], kt[:, d], eK, ALU.mult).then_inc(stacked_ready, 1)
                dve.wait_ge(stacked_ready, 4 * d + 4)
                chain.after(nc.vector.tensor_tensor(wk[:, d], wide(cells(kt[:, d]), NCH), bd(NCH), ALU.mult))
            nc.vector.tensor_tensor(wv[:], wide(cells(v), NCH), bd(NCH), ALU.mult)

        @block.gpsimd
        def _(pool):
            for d in range(2):
                pool.wait_ge(stacked_ready, 4 * d + 3)
                nc.gpsimd.tensor_tensor(wq[:, d], wide(qr[:, d, :, 0, :], NCH), bd(NCH), ALU.mult)
                nc.gpsimd.tensor_tensor(wb[:, d], wide(cells(bt[:, d]), NCH), bd(NCH), ALU.mult)

    wX, wU, zt = R["wX"], R["wU"], R["zt"]

    def flat(ap):
        return ap.rearrange("p h t -> p (h t)")

    def flat4(ap):
        return ap.rearrange("p c h t -> p (c h t)")

    names = ["grams_ready", "grams_read", "turned_ready", "turned_read", "v_ready", "v_read", "vec_step"]
    with Phase(nc, names) as (block, grams_ready, grams_read, turned_ready, turned_read, v_ready, v_read, vec_step):
        batches = [(d, c0) for d in range(2) for c0 in range(0, NCH, 4)]

        @block.tensor
        def _(pe):
            for n, (d, c0) in enumerate(batches):
                if n >= 2:
                    pe.wait_ge(grams_read, n - 1)
                for i in range(4):
                    c = c0 + i
                    rhs = qr[:, d, c].rearrange("p a t -> p (a t)")
                    nc.tensor.matmul(psum[:, n % 2, i * P:(i + 1) * P], flat(wb[:, d, c]), rhs, start=True, stop=True)
                    nc.tensor.matmul(psum[:, 2 + n % 2, i * P:(i + 1) * P], flat(wk[:, d, c]), rhs,
                                     start=True, stop=True)
                    last = nc.tensor.matmul(psum[:, 4 + n % 2, i * P:(i + 1) * P], flat(wq[:, d, c]),
                                            flat(wb[:, d, c]), start=True, stop=True)
                last.then_inc(grams_ready, 1)
                if n >= 1:
                    pe.wait_ge(turned_read, 2 * n)
                for i in range(4):
                    c = c0 + i
                    nc.tensor.transpose(psum[:, 6, i * P:(i + 1) * P], flat(wb[:, d, c]), ident[:])
                    last = nc.tensor.transpose(psum[:, 7, i * P:(i + 1) * P], flat(wk[:, d, c]), ident[:])
                last.then_inc(turned_ready, 1)
            pe.wait_ge(turned_read, 2 * len(batches))
            for n in range(3):
                if n == 2:
                    pe.wait_ge(v_read, 1)
                for i in range(4):
                    last = nc.tensor.transpose(psum[:, 6 + n % 2, i * P:(i + 1) * P], flat(wv[:, 4 * n + i]), ident[:])
                last.then_inc(v_ready, 1)

        @block.vector
        def _(dve):
            chain = Chain(dve, vec_step)
            for n, (d, c0) in enumerate(batches):
                dve.wait_ge(grams_ready, n + 1)
                g1 = psum[:, n % 2, :].rearrange("p (c a t) -> p c a t", a=2, t=L_CH)
                g2 = psum[:, 2 + n % 2, :].rearrange("p (c a t) -> p c a t", a=2, t=L_CH)
                am = psum[:, 4 + n % 2, :].rearrange("p (c m) -> p c m", m=P)
                strict = cst["strict_wide"][:, d, :].rearrange("p (c h t) -> p c h t", c=1, h=2).to_broadcast(
                    [P, 4, 2, L_CH])
                x4 = wX[:, d, c0:c0 + 4].rearrange("p c h t -> p c (h t)")
                chain.after(nc.vector.tensor_tensor(x4, am, cst["level"][:, d, 0:1, :].to_broadcast([P, 4, P]),
                                                    ALU.mult))
                nc.vector.tensor_tensor(wAT[:, d, c0:c0 + 4], wide(g1[:, :, 0, :], 4), strict, ALU.mult)
                nc.vector.tensor_tensor(wBT[:, d, c0:c0 + 4], wide(g2[:, :, 0, :], 4), strict, ALU.mult)
                if c0 >= CCH:
                    incl = mask(cst["incl"][:, d, :], 4)
                    nc.vector.tensor_tensor(Dd[:, d, c0 - CCH:c0 - CCH + 4], g1[:, :, 1, :], incl, ALU.mult)
                    nc.vector.tensor_tensor(Cc[:, d, c0 - CCH:c0 - CCH + 4], g2[:, :, 1, :], incl, ALU.mult)
                nc.vector.tensor_tensor(x4, x4, ident[:].rearrange("p (c m) -> p c m", c=1).to_broadcast([P, 4, P]),
                                        ALU.add).then_inc(grams_read, 1)

        @block.scalar
        def _(act):
            for n, (d, c0) in enumerate(batches):
                act.wait_ge(turned_ready, n + 1)
                nc.scalar.copy(flat4(wbt[:, d, c0:c0 + 4]), psum[:, 6, :]).then_inc(turned_read, 1)
                nc.scalar.copy(flat4(wkt[:, d, c0:c0 + 4]), psum[:, 7, :]).then_inc(turned_read, 1)
            for n in range(3):
                act.wait_ge(v_ready, n + 1)
                nc.scalar.copy(flat4(wV[:, 4 * n:4 * n + 4]), psum[:, 6 + n % 2, :]).then_inc(v_read, 1)

    BQ = [(d, c0) for d in range(2) for c0 in range(0, NCH, 4)]
    NQ = len(BQ)
    names = ["x_turned", "xt_ready", "u_ready", "u_copied", "z_ready", "z_masked", "x_ready0", "x_ready1"]
    with Phase(nc, names) as (block, x_turned, xt_ready, u_ready, u_copied, z_ready, z_masked, x_ready0, x_ready1):
        x_ready = (x_ready0, x_ready1)

        @block.tensor
        def _(pe):
            for lv in range(LEVELS + 1):
                for q, (d, c0) in enumerate(BQ):
                    n = lv * NQ + q
                    if lv:
                        pe.wait_ge(x_ready[d], 3 * (lv - 1) + q % 3 + 1)
                    if n >= 2:
                        pe.wait_ge(xt_ready, n - 1)
                    for i in range(4):
                        last = nc.tensor.transpose(psum[:, 6 + q % 2, i * P:(i + 1) * P], flat(wX[:, d, c0 + i]),
                                                   ident[:])
                    last.then_inc(x_turned, 1)
                    if lv < LEVELS:
                        for i in range(4):
                            last = nc.tensor.matmul(psum[:, q, i * P:(i + 1) * P], flat(wAT[:, d, c0 + i]),
                                                    flat(wX[:, d, c0 + i]), start=True, stop=True)
                        last.then_inc(u_ready, 1)
                if lv < LEVELS:
                    for q, (d, c0) in enumerate(BQ):
                        n = lv * NQ + q
                        pe.wait_ge(u_copied, n + 1)
                        pe.wait_ge(xt_ready, n + 1)
                        for i in range(4):
                            last = nc.tensor.matmul(psum[:, q, i * P:(i + 1) * P], flat(wXT[:, d, c0 + i]),
                                                    flat(wU[:, d, c0 + i]), start=True, stop=True)
                        last.then_inc(z_ready, 1)

        @block.scalar
        def _(act):
            for lv in range(LEVELS + 1):
                for q, (d, c0) in enumerate(BQ):
                    n = lv * NQ + q
                    act.wait_ge(x_turned, n + 1)
                    if lv:
                        act.wait_ge(z_ready, n - NQ + 1)
                    nc.scalar.copy(flat4(wXT[:, d, c0:c0 + 4]), psum[:, 6 + q % 2, :]).then_inc(xt_ready, 1)
                    if lv < LEVELS:
                        act.wait_ge(u_ready, n + 1)
                        nc.scalar.copy(flat4(wU[:, d, c0:c0 + 4]), psum[:, q, :]).then_inc(u_copied, 1)

        @block.vector
        def _(dve):
            for lv in range(LEVELS):
                for q, (d, c0) in enumerate(BQ):
                    n = lv * NQ + q
                    t_ = zt[:, d, c0:c0 + 4].rearrange("p c h t -> p c (h t)")
                    dve.wait_ge(z_ready, n + 1)
                    if lv and d:
                        dve.wait_ge(x_ready1, 3 * (lv - 1) + q % 3 + 1)
                    nc.vector.tensor_tensor(t_, psum[:, q, :].rearrange("p (c m) -> p c m", m=P),
                                            cst["level"][:, d, lv + 1:lv + 2, :].to_broadcast([P, 4, P]), ALU.mult
                                            ).then_inc(z_masked, 1)
                    if d == 0:
                        dve.wait_ge(z_masked, n + 1)
                        x4 = flat4(wX[:, d, c0:c0 + 4])
                        nc.vector.tensor_tensor(x4, x4, flat4(zt[:, d, c0:c0 + 4]), ALU.add).then_inc(x_ready0, 1)

        @block.gpsimd
        def _(pool):
            for lv in range(LEVELS):
                for q, (d, c0) in enumerate(BQ):
                    if d:
                        pool.wait_ge(z_masked, lv * NQ + q + 1)
                        x4 = flat4(wX[:, d, c0:c0 + 4])
                        nc.gpsimd.tensor_tensor(x4, x4, flat4(zt[:, d, c0:c0 + 4]), ALU.add).then_inc(x_ready1, 1)

    orders = [list(range(NCH)), list(range(CCH - 1, -1, -1)) + list(range(NCH - 1, CCH - 1, -1))]
    wS, wW, wN = R["wS"], R["wW"], R["wN"]
    names = ["w_ready", "w_copied", "n_ready", "n_copied", "s_ready", "s_copied", "y_done"]
    with Phase(nc, [n + s for n in names for s in ("0", "1")] + ["state_zero"]) as (block, *sems):
        w_ready, w_copied, n_ready, n_copied, s_ready, s_copied, y_done = [
            (sems[2 * i], sems[2 * i + 1]) for i in range(7)]
        state_zero = sems[-1]

        def room(d, k):
            bank = 6 + d if k == 2 else 4 + d
            return psum[:, bank, k * P:(k + 1) * P]

        @block.tensor
        def _(pe):
            pe.wait_ge(state_zero, 1)

            def outputs(n, d):
                c = orders[d][n] - CCH
                yy = psum[0:L_CH, 2 * d + c // 4, (c % 4) * P:(c % 4 + 1) * P]
                nc.tensor.matmul(yy, qr[:, d, CCH + c, 1, :], wS[:, d], start=True, stop=False)
                nc.tensor.matmul(yy, Cc[:, d, c], flat(wV[:, CCH + c]), start=False, stop=False)
                nc.tensor.matmul(yy, Dd[:, d, c], wN[:, d], start=False, stop=True).then_inc(y_done[d], 1)

            for n in range(NCH):
                for d in range(2):
                    c = orders[d][n]
                    if n >= 1:
                        pe.wait_ge(s_copied[d], n)
                    nc.tensor.matmul(room(d, 0), flat(wq[:, d, c]), wS[:, d], start=True, stop=False)
                    nc.tensor.matmul(room(d, 0), flat(wBT[:, d, c]), flat(wV[:, c]), start=False, stop=True
                                     ).then_inc(w_ready[d], 1)
                for d in range(2):
                    c = orders[d][n]
                    pe.wait_ge(w_copied[d], n + 1)
                    nc.tensor.matmul(room(d, 1), flat(wXT[:, d, c]), wW[:, d], start=True, stop=True
                                     ).then_inc(n_ready[d], 1)
                for d in range(2):
                    c = orders[d][n]
                    if n < NCH - 1:
                        nc.tensor.matmul(room(d, 2), ident[:], wS[:, d], start=True, stop=False)
                        nc.tensor.matmul(room(d, 2), flat(wkt[:, d, c]), flat(wV[:, c]), start=False, stop=False)
                        pe.wait_ge(n_copied[d], n + 1)
                        nc.tensor.matmul(room(d, 2), flat(wbt[:, d, c]), wN[:, d], start=False, stop=True
                                         ).then_inc(s_ready[d], 1)
                    else:
                        pe.wait_ge(n_copied[d], n + 1)
                    if n >= CCH:
                        outputs(n, d)

        def copies(d, eng, copy_w, copy_n, copy_s):
            for n in range(NCH):
                c = orders[d][n]
                eng.wait_ge(w_ready[d], n + 1)
                copy_w(wW[:, d], room(d, 0)).then_inc(w_copied[d], 1)
                eng.wait_ge(n_ready[d], n + 1)
                if n >= 1:
                    if n > CCH:
                        eng.wait_ge(y_done[d], n - CCH)
                    else:
                        eng.wait_ge(s_ready[d], n)
                copy_n(wN[:, d], room(d, 1)).then_inc(n_copied[d], 1)
                if n < NCH - 1:
                    eng.wait_ge(s_ready[d], n + 1)
                    if n >= CCH:
                        eng.wait_ge(y_done[d], n - CCH + 1)
                    copy_s(wS[:, d], room(d, 2), pl[:, d, c:c + 1]).then_inc(s_copied[d], 1)

        @block.vector
        def _(dve):
            nc.vector.memset(wS[:], 0.0).then_inc(state_zero, 1)
            copies(0, dve, nc.vector.tensor_copy, lambda o, i: nc.vector.tensor_scalar(o, i, -1.0, None, ALU.mult),
                   lambda o, i, s: nc.vector.tensor_scalar(o, i, s, None, ALU.mult))

        @block.scalar
        def _(act):
            copies(1, act, nc.scalar.copy, lambda o, i: nc.scalar.activation(o, i, ACT.Copy, scale=-1.0),
                   lambda o, i, s: nc.scalar.activation(o, i, ACT.Copy, scale=s))

    names = ["y_added", "y_turned", "y_summed", "mean_ready", "squares_ready", "var_ready", "root_taken", "rk_ready",
             "bonus_ready", "gate_ready", "vec_step"]
    with Phase(nc, names) as (block, y_added, y_turned, y_summed, mean_ready, squares_ready, var_ready, root_taken,
                              rk_ready, bonus_ready, gate_ready, vec_step):
        yb, sqb, rk, rt = (R["fin"][:, i] for i in range(4))
        rows = R["y_rows"]

        @block.tensor
        def _(pe):
            nc.tensor.matmul(psum[:, 5, :], gup[:], R["gd"], start=True, stop=True).then_inc(gate_ready, 1)
            pe.wait_ge(rk_ready, 1)
            nc.tensor.matmul(psum[:, 6, :], cst["ones"][:], rk, start=True, stop=True).then_inc(bonus_ready, 1)
            pe.wait_ge(y_added, 1)
            for c in range(XCH):
                last = nc.tensor.transpose(psum[:, 4, c * L_CH:(c + 1) * L_CH], rows[:, c * P:(c + 1) * P],
                                           ident[0:L_CH, 0:L_CH])
            last.then_inc(y_turned, 1)
            pe.wait_ge(y_summed, 1)
            nc.tensor.matmul(psum[:, 7, :], cst["ones"][:], yb, start=True, stop=True).then_inc(mean_ready, 1)
            pe.wait_ge(squares_ready, 1)
            nc.tensor.matmul(psum[:, 4, :], cst["ones"][:], sqb, start=True, stop=True).then_inc(var_ready, 1)

        @block.scalar
        def _(act):
            act.wait_ge(var_ready, 1)
            nc.scalar.activation(rt, psum[:, 4, :], ACT.Sqrt, bias=cst["ln_eps"][:], scale=1.0 / 64
                                 ).then_inc(root_taken, 1)

        @block.vector
        def _(dve):
            chain = Chain(dve, vec_step)
            both = [psum[0:L_CH, 2 * d:2 * d + 2, :].rearrange("p b n -> p (b n)") for d in range(2)]
            chain.after(nc.vector.tensor_copy(rows, both[0]))
            nc.vector.tensor_tensor(rows, rows, both[1], ALU.add).then_inc(y_added, 1)
            nc.vector.scalar_tensor_tensor(rk, r, prm[:, 6:7], k[:, CTX:], ALU.mult, ALU.mult).then_inc(rk_ready, 1)
            dve.wait_ge(y_turned, 1)
            nc.vector.tensor_copy(yb, psum[:, 4, :]).then_inc(y_summed, 1)
            dve.wait_ge(mean_ready, 1)
            chain.after(nc.vector.scalar_tensor_tensor(yb, psum[:, 7, :], -1.0 / 64, yb, ALU.mult, ALU.add))
            nc.vector.tensor_tensor(sqb, yb, yb, ALU.mult).then_inc(squares_ready, 1)
            dve.wait_ge(bonus_ready, 1)
            chain.after(nc.vector.tensor_tensor(rk, psum[:, 6, :], v[:, CTX:], ALU.mult))
            dve.wait_ge(root_taken, 1)
            chain.after(nc.vector.reciprocal(rt, rt))
            chain.after(nc.vector.tensor_tensor(yb, yb, rt, ALU.mult))
            chain.after(nc.vector.tensor_scalar(yb, yb, prm[:, 7:8], prm[:, 8:9], ALU.mult, ALU.add))
            chain.after(nc.vector.tensor_tensor(yb, yb, rk, ALU.add))
            dve.wait_ge(gate_ready, 1)
            chain.after(nc.vector.tensor_tensor(obT[:, g, :], yb, psum[:, 5, :], ALU.mult))


def rwkv_constants():
    import numpy as np
    f = np.float32
    p = np.arange(P)
    t = np.arange(L_CH)
    out = {"ones": (p[:, None] // 64 == p[None, :] // 64).astype(f)}
    out["bd"] = out["ones"].copy()
    row, col = p[:, None] % 64, t[None, :]
    strict = [(row < col), (row > col)]
    incl = [(row <= col), (row >= col)]
    out["strict_wide"] = np.stack([np.tile(m, (1, 2)) * out["ones"] for m in strict], 1).astype(f)
    out["incl"] = np.stack(incl, 1).astype(f)
    lev = np.zeros((P, 2, LEVELS + 1, L_CH), f)
    for i in range(LEVELS + 1):
        m = 2 ** i
        same = row // (2 * m) == col // (2 * m)
        lev[:, 0, i] = -1.0 * (same & ((row // m) % 2 == 1) & ((col // m) % 2 == 0))
        lev[:, 1, i] = -1.0 * (same & ((row // m) % 2 == 0) & ((col // m) % 2 == 1))
    out["level"] = np.tile(lev, (1, 1, 1, 2)) * out["bd"][:, None, None, :]
    tt = np.arange(N_ALL)
    out["reset"] = np.broadcast_to(np.stack([tt % L_CH != 0, tt % L_CH != L_CH - 1]).astype(f), (P, 2, N_ALL)).copy()
    out["tiny"] = np.full((P, 1), 1e-12, f)
    out["ln_eps"] = np.full((P, 1), RW_LN_EPS, f)
    return out


def rope_constants():
    import numpy as np
    f = np.float32
    inv = (f(10000.0) ** (-np.arange(16, dtype=f) / f(16))).astype(f)
    tok = np.arange(S)
    C = np.ones((N_ALL, 2, 2, 16), f)
    Sn = np.zeros((N_ALL, 2, 2, 16), f)
    for a, pos in enumerate((tok // 64, tok % 64)):
        ang = pos.astype(f)[:, None] * inv
        C[CTX:, a, :, :] = np.cos(ang)[:, None, :]
        Sn[CTX:, a, 0, :] = -np.sin(ang)
        Sn[CTX:, a, 1, :] = np.sin(ang)
    lay = lambda x: np.ascontiguousarray(x.reshape(AT, P, 64).transpose(1, 0, 2))
    return {"ropeC": lay(C), "ropeS": lay(Sn)}


def peer_phases(nc, T, x, out):
    I, psum, ident = T["in"], T["psum"], T["ident"]
    with ExitStack() as ctx:
        def sb(name, shape, dt=F32):
            return ctx.enter_context(nc.sbuf_tensor(name, shape, dt))
        h = sb("h_rows", [P, ST, D])
        sel = sb("sel_idx", [P, ST, SLOTS], I32)
        gate = sb("sel_gate", [P, ST, SLOTS])
        qT = sb("qT_p", [P, 2 * PEER_HEADS, S])
        with ExitStack() as inner:
            def sbi(name, shape, dt=F32):
                return inner.enter_context(nc.sbuf_tensor(name, shape, dt))
            hT = sbi("hT_p", [P, DC, S])
            with nc.sbuf_tensor("p_scr", [P, 6 * D], F32) as scr:
                sc2 = scr[:].rearrange("p (t d) -> p t d", d=D)
                modulated_norm(nc, T, x, ST, 2, hT, 0, (sc2[:, 0:2], sc2[:, 2:6]))
            with Phase(nc, ["turned_back", "copied"]) as (block, turned_back, copied):
                @block.tensor
                def _(pe):
                    for t in range(ST):
                        for c in range(DC):
                            last = nc.tensor.transpose(psum[:, 2 * t + c // 4, (c % 4) * P:(c % 4 + 1) * P],
                                                       hT[:, c, t * P:(t + 1) * P], ident[:])
                        last.then_inc(turned_back, 1)

                @block.vector
                def _(dve):
                    for t in range(ST):
                        dve.wait_ge(turned_back, t + 1)
                        nc.vector.tensor_copy(h[:, t, :], psum[:, 2 * t:2 * t + 2, :].rearrange("p b n -> p (b n)"))
            with ExitStack() as queries:
                hs = sbuf_split(queries, nc, "hT_ps", [P, DC, S])
                split_phase(nc, hT, hs)

                def q_groups(b):
                    def groups(w):
                        res = []
                        for j in range(4):
                            dst = qT[:, 4 * b + j, :]
                            ev = (lambda ch, acc, dst=dst: nc.vector.tensor_copy(dst, acc)) if j % 2 == 0 else \
                                (lambda ch, acc, dst=dst: nc.scalar.copy(dst, acc))
                            res.append((P, S, [(w[:, c, j * P:(j + 1) * P], hs[:, c, :]) for c in range(DC)], ev,
                                        "va"[j % 2]))
                        return res
                    return groups
                gemm_phase(nc, psum, [(I["peer_wq"][b], q_groups(b)) for b in range(4)])
        expert_phase(nc, T, x, h, qT, sel, gate, out, sb)


class Search:
    SETS = 2 * PEER_HEADS
    STEPS = SETS + PEER_HEADS + 1

    def __init__(self, nc, T, qT, sel, gate, sb):
        self.nc, self.psum, self.qT, self.sel, self.gate = nc, T["psum"], qT, sel, gate
        self.keys = sb("keys", [P, self.SETS, N_KEYS])
        self.iota = sb("iota16", [P, TOPK])
        load_phase(nc, [(self.keys[:], T["in"]["peer_keys"]), (self.iota[:], T["in"]["iota16"])])
        self.sc = sb("key_scores", [P, self.SETS, N_KEYS])
        self.top = sb("top_val", [P, self.SETS, TOPK])
        self.topi = sb("top_pos", [P, self.SETS, TOPK], U32)
        self.topf = sb("top_posf", [P, self.SETS, TOPK])
        self.cand = sb("cand", [P, TOPK * TOPK])
        self.best = sb("best", [P, PEER_HEADS, TOPK])
        self.besti = sb("best_pos", [P, PEER_HEADS, TOPK], U32)
        self.hi = sb("pos_hi", [P, 2, PEER_HEADS * TOPK], U32)
        self.hif = sb("pos_hif", [P, 2, PEER_HEADS * TOPK])
        self.pick = sb("pick", [P, PEER_HEADS, TOPK, TOPK])
        self.found = sb("found", [P, 2, PEER_HEADS * TOPK])
        self.den = sb("gate_den", [P, 2, PEER_HEADS])

    def scores(self, t):
        for hp in range(self.SETS):
            last = self.nc.tensor.matmul(self.psum[:, 4 + hp // 4, (hp % 4) * P:(hp % 4 + 1) * P],
                                         self.qT[:, hp, t * P:(t + 1) * P], self.keys[:, hp, :], start=True, stop=True)
        return last

    def copy_scores(self):
        return self.nc.vector.tensor_copy(self.sc[:].rearrange("p h k -> p (h k)"),
                                          self.psum[:, 4:8, :].rearrange("p b n -> p (b n)"))

    def exps(self):
        return self.nc.scalar.activation(self.best[:], self.best[:], ACT.Exp)

    def top16(self, chain, vals, v16, i16):
        nc = self.nc
        chain.after(nc.vector.max(v16[:, 0:8], vals))
        chain.after(nc.vector.max_index(i16[:, 0:8], v16[:, 0:8], vals))
        chain.after(nc.vector.match_replace(vals, v16[:, 0:8], vals, -3e38))
        chain.after(nc.vector.max(v16[:, 8:16], vals))
        chain.after(nc.vector.max_index(i16[:, 8:16], v16[:, 8:16], vals))

    def top_of_set(self, chain, hp):
        self.top16(chain, self.sc[:, hp, :], self.top[:, hp, :], self.topi[:, hp, :])

    def top_of_head(self, chain, hd):
        first = self.top[:, 2 * hd, :].rearrange("p (a o) -> p a o", o=1).to_broadcast([P, TOPK, TOPK])
        second = self.top[:, 2 * hd + 1:2 * hd + 2, :].to_broadcast([P, TOPK, TOPK])
        chain.after(self.nc.vector.tensor_tensor(self.cand[:].rearrange("p (a b) -> p a b", a=TOPK), first, second,
                                                 ALU.add))
        self.top16(chain, self.cand[:], self.best[:, hd, :], self.besti[:, hd, :])

    def numbers(self, chain, t):
        nc, hi, hif, pick, found, den, best = (self.nc, self.hi, self.hif, self.pick, self.found, self.den,
                                               self.best)
        chain.after(nc.vector.tensor_copy(self.topf[:], self.topi[:]))
        flat = self.besti[:].rearrange("p h k -> p (h k)")
        chain.after(nc.vector.tensor_scalar(hi[:, 0, :], flat, 4, None, ALU.logical_shift_right))
        chain.after(nc.vector.tensor_scalar(hi[:, 1, :], flat, 15, None, ALU.bitwise_and))
        chain.after(nc.vector.tensor_copy(hif[:], hi[:]))
        for w in range(2):
            rank = hif[:, w, :].rearrange("p (n o) -> p n o", o=1).to_broadcast([P, SLOTS, TOPK])
            io = self.iota[:].rearrange("p (o a) -> p o a", o=1).to_broadcast([P, SLOTS, TOPK])
            pk = pick[:].rearrange("p h k a -> p (h k) a")
            chain.after(nc.vector.tensor_tensor(pk, rank, io, ALU.is_equal))
            places = self.topf[:, w::2, :].rearrange("p h (o a) -> p h o a", o=1).to_broadcast(
                [P, PEER_HEADS, TOPK, TOPK])
            chain.after(nc.vector.tensor_tensor(pick[:], pick[:], places, ALU.mult))
            chain.after(nc.vector.reduce_sum(found[:, w, :], pk, AX.X))
        chain.after(nc.vector.scalar_tensor_tensor(found[:, 0, :], found[:, 0, :], float(N_KEYS),
                                                   found[:, 1, :], ALU.mult, ALU.add))
        chain.after(nc.vector.tensor_copy(self.sel[:, t, :], found[:, 0, :]))
        chain.after(nc.vector.tensor_copy(den[:, 0, :], best[:, :, 0]))
        big = den[:, 0, :].rearrange("p (h o) -> p h o", o=1).to_broadcast([P, PEER_HEADS, TOPK])
        return nc.vector.tensor_tensor(best[:], best[:], big, ALU.subtract)

    def gates(self, chain, t):
        nc, den, best = self.nc, self.den, self.best
        chain.after(nc.vector.reduce_sum(den[:, 0, :], best[:], AX.X))
        chain.after(nc.vector.reciprocal(den[:, 1, :], den[:, 0, :]))
        inv = den[:, 1, :].rearrange("p (h o) -> p h o", o=1).to_broadcast([P, PEER_HEADS, TOPK])
        return nc.vector.tensor_tensor(self.gate[:, t, :].rearrange("p (h k) -> p h k", k=TOPK), best[:], inv,
                                       ALU.mult)


def expert_phase(nc, T, x, h, qT, sel, gate, out, sb):
    I, psum, ident = T["in"], T["psum"], T["ident"]
    BATCH = 4
    RB = 2 * BATCH + 2
    NBT = SLOTS // BATCH
    rows = sb("rows", [P, RB, 2 * D])
    prod = sb("uh", [P, D])
    dots = sb("dots", [P, 2, BATCH])
    g1 = sb("g1", [P, 2, BATCH])
    g2 = sb("g2", [P, 2, BATCH])
    diag = sb("diag", [P, 2 * BATCH, P])
    UN = ST * SLOTS
    search = Search(nc, T, qT, sel, gate, sb)
    assert search.STEPS <= NBT
    with Phase(nc, [f"row_landed{i}" for i in range(RB)] +
               ["dot_taken", "inner_ready", "tanh_ready", "weights_ready", "diag_ready", "row_used", "tile_ready",
                "tile_taken", "out_written", "scores_ready", "scores_copied", "shifted", "exps_ready", "chosen",
                "vec_step"]) as (block, *sems):
        row_landed = sems[:RB]
        (dot_taken, inner_ready, tanh_ready, weights_ready, diag_ready, row_used, tile_ready, tile_taken, out_written,
         scores_ready, scores_copied, shifted, exps_ready, chosen, vec_step) = sems[RB:]

        @block.gpsimd
        def _(pool):
            for n in range(UN):
                t, s = divmod(n, SLOTS)
                if s == 0:
                    pool.wait_ge(chosen, t + 1)
                if n >= RB:
                    pool.wait_ge(row_used, n - RB + 1)
                nc.gpsimd.indirect_dma_start(out=rows[:, n % RB, :], out_offset=None, in_=I["peer_uv"],
                                             in_offset=bass.IndirectOffsetOnAxis(ap=sel[:, t, s:s + 1], axis=0)
                                             ).then_inc(row_landed[n % RB], 16)

        @block.vector
        def _(dve):
            chain = Chain(dve, vec_step)

            def dot(n):
                t, s = divmod(n, SLOTS)
                dve.wait_ge(row_landed[n % RB], 16 * (n // RB + 1))
                if n >= 1:
                    dve.wait_ge(dot_taken, n)
                if s % BATCH == 0 and n >= 2 * BATCH:
                    dve.wait_ge(weights_ready, n // BATCH - 1)
                nc.vector.scalar_tensor_tensor(prod[:], rows[:, n % RB, 0:D], 1.0, h[:, t, :], ALU.mult, ALU.mult,
                                               accum_out=dots[:, (n // BATCH) % 2, s % BATCH:s % BATCH + 1]
                                               ).then_inc(dot_taken, 1)

            def gelu(b):
                zz, u1, u2 = dots[:, b % 2, :], g1[:, b % 2, :], g2[:, b % 2, :]
                t, s = divmod(b * BATCH, SLOTS)
                dve.wait_ge(dot_taken, (b + 1) * BATCH)
                chain.after(nc.vector.tensor_tensor(u1, zz, zz, ALU.mult))
                chain.after(nc.vector.tensor_scalar(u1, u1, 0.044715, 1.0, ALU.mult, ALU.add))
                nc.vector.tensor_tensor(u1, u1, zz, ALU.mult).then_inc(inner_ready, 1)
                chain.after(nc.vector.scalar_tensor_tensor(u2, zz, 0.5, gate[:, t, s:s + BATCH], ALU.mult, ALU.mult))
                dve.wait_ge(tanh_ready, b + 1)
                if b >= 2:
                    dve.wait_ge(diag_ready, (b - 1) * BATCH)
                nc.vector.scalar_tensor_tensor(u2, u1, 1.0, u2, ALU.add, ALU.mult).then_inc(weights_ready, 1)

            def search_step(t, k):
                if k == 0:
                    dve.wait_ge(scores_ready, t + 1)
                    search.copy_scores().then_inc(scores_copied, 1)
                    dve.wait_ge(scores_copied, t + 1)
                if k < search.SETS:
                    search.top_of_set(chain, k)
                elif k < search.STEPS - 1:
                    search.top_of_head(chain, k - search.SETS)
                elif k == search.STEPS - 1:
                    search.numbers(chain, t).then_inc(shifted, 1)
                    dve.wait_ge(exps_ready, t + 1)
                    search.gates(chain, t).then_inc(chosen, 1)
                    dve.wait_ge(chosen, t + 1)

            for k in range(search.STEPS):
                search_step(0, k)
            for b in range(ST * NBT):
                for i in range(BATCH):
                    dot(b * BATCH + i)
                gelu(b)
                if b // NBT + 1 < ST:
                    search_step(b // NBT + 1, b % NBT)
                if (b + 1) % NBT == 0:
                    t = b // NBT
                    dve.wait_ge(tile_ready, t + 1)
                    acc = psum[:, 2 * (t % 2):2 * (t % 2) + 2, :].rearrange("p b n -> p (b n)")
                    chain.after(nc.vector.tensor_tensor(prod[:], acc, T["gate_rows"][:, 1, :], ALU.mult))
                    nc.vector.tensor_tensor(x[:, t, :], x[:, t, :], prod[:], ALU.add).then_inc(tile_taken, 1)
                    dve.wait_ge(tile_taken, t + 1)

        @block.scalar
        def _(act):
            act.wait_ge(shifted, 1)
            search.exps().then_inc(exps_ready, 1)
            for b in range(ST * NBT):
                act.wait_ge(inner_ready, b + 1)
                nc.scalar.activation(g1[:, b % 2, :], g1[:, b % 2, :], ACT.Tanh, scale=0.7978845608028654
                                     ).then_inc(tanh_ready, 1)
                act.wait_ge(weights_ready, b + 1)
                for i in range(BATCH):
                    n = b * BATCH + i
                    if n >= 2 * BATCH:
                        act.wait_ge(row_used, n - 2 * BATCH + 1)
                    nc.scalar.activation(diag[:, n % (2 * BATCH), :], ident[:], ACT.Copy,
                                         scale=g2[:, b % 2, i:i + 1]).then_inc(diag_ready, 1)
                t = b // NBT + 1
                if t < ST and b % NBT == search.STEPS - 1:
                    act.wait_ge(shifted, t + 1)
                    search.exps().then_inc(exps_ready, 1)

        @block.tensor
        def _(pe):
            search.scores(0).then_inc(scores_ready, 1)
            for n in range(UN):
                t, s = divmod(n, SLOTS)
                if s == 0 and t + 1 < ST:
                    pe.wait_ge(scores_copied, t + 1)
                    search.scores(t + 1).then_inc(scores_ready, 1)
                pe.wait_ge(row_landed[n % RB], 16 * (n // RB + 1))
                pe.wait_ge(diag_ready, n + 1)
                if s == 0 and t >= 2:
                    pe.wait_ge(tile_taken, t - 1)
                for half in range(2):
                    last = nc.tensor.matmul(psum[:, 2 * (t % 2) + half, :], diag[:, n % (2 * BATCH), :],
                                            rows[:, n % RB, D + half * NB:D + (half + 1) * NB],
                                            start=(s == 0), stop=(s == SLOTS - 1))
                last.then_inc(row_used, 1)
                if s == SLOTS - 1:
                    pe.wait_ge(row_used, n + 1)
                    pe.sem_inc(tile_ready, 1)

        @block.sync
        def _(sp):
            for t in range(ST):
                sp.wait_ge(tile_taken, t + 1)
                sp.dma_start(out[:, t, :], x[:, t, :]).then_inc(out_written, 16)
            sp.wait_ge(out_written, 16 * ST)


def second_block_program(nc, T, out):
    I, psum, ident, x = T["in"], T["psum"], T["ident"], T["x"]
    hT_d, oaT_d = (nc.dram_tensor(n, [P, DC, S], F32, kind="Internal").ap() for n in ("hT_spill", "oaT_spill"))
    z_d = {n: nc.dram_tensor(f"z{n}_spill", [DC, P, w], F32, kind="Internal").ap()
           for n, w in (("r", S), ("k", N_ALL), ("v", N_ALL))}

    def scope():
        s = ExitStack()

        def sb(name, shape, dt=F32):
            return s.enter_context(nc.sbuf_tensor(name, shape, dt))
        return s, sb

    def move_phase(moves):
        with Phase(nc, ["moved"]) as (block, moved):
            @block.sync
            def _(sp):
                for dst, src in moves:
                    sp.dma_start(dst, src).then_inc(moved, 16)
                sp.wait_ge(moved, 16 * len(moves))

    with nc.sbuf_tensor("wbuf_mod", [P, 2, DC * NB], F32) as wbuf:
        modulation_phases(nc, T, wbuf)

    top, sbt = scope()
    lora = sbt("lora", [P, N_ALL])
    gd = sbt("gd", [P, S])
    with ExitStack() as stage:
        def sb(name, shape, dt=F32):
            return stage.enter_context(nc.sbuf_tensor(name, shape, dt))
        hT = sbuf_split(stage, nc, "hT_all", [P, DC, N_ALL])
        with nc.sbuf_tensor("ctx_rows", [P, CT, D], F32) as ctx_rows, nc.sbuf_tensor("nscr", [P, 6 * D], F32) as scr, \
                nc.sbuf_tensor("hT_whole", [P, DC, N_ALL], F32) as whole:
            load_phase(nc, [(ctx_rows[:], I["ctx"])])
            sc2 = scr[:].rearrange("p (t d) -> p t d", d=D)
            modulated_norm(nc, T, ctx_rows, CT, 1, whole, 0, (sc2[:, 0:2], sc2[:, 2:6]))
            modulated_norm(nc, T, x, ST, 0, whole, CTX, (sc2[:, 0:2], sc2[:, 2:6]))
            split_phase(nc, whole, hT, spill=(hT_d, whole[:, :, CTX:]))

        def rows_of(dst, half, first_tile, tiles):
            def groups(w):
                res = []
                for t in range(tiles):
                    o = dst[:, t, half * NB:(half + 1) * NB]
                    ev = (lambda ch, acc, o=o: nc.vector.tensor_copy(o, acc)) if t % 2 == 0 else \
                        (lambda ch, acc, o=o: nc.scalar.copy(o, acc))
                    at = (first_tile + t) * P
                    res.append((P, NB, [(hT[:, c, at:at + P], w[:, c, :]) for c in range(DC)], ev, "va"[t % 2]))
                return res
            return groups

        W = I["w_in_2"]
        with ExitStack() as att:
            def sba(name, shape, dt=F32):
                return att.enter_context(nc.sbuf_tensor(name, shape, dt))
            v = sba("v_all", [P, AT, D])
            q = sba("q_rows", [P, ST, D])
            k = sba("k_rows", [P, AT, D])
            gemm_phase(nc, psum, [(W[0], rows_of(q, 0, CT, ST)), (W[1], rows_of(q, 1, CT, ST)),
                                  (W[2], rows_of(k, 0, 0, AT)), (W[3], rows_of(k, 1, 0, AT)),
                                  (W[4], rows_of(v, 0, 0, AT)), (W[5], rows_of(v, 1, 0, AT))])
            qT = sba("qT", [P, DC, S])
            kT = sba("kT", [P, DC, N_ALL])
            with nc.sbuf_tensor("ropeC_sb", [P, AT, 64], F32) as rc, nc.sbuf_tensor("ropeS_sb", [P, AT, 64], F32) \
                    as rs, nc.sbuf_tensor("gq", [P, 2, 64], F32) as gq, nc.sbuf_tensor("gk", [P, 2, 64], F32) as gk:
                load_phase(nc, [(rc[:], I["ropeC"]), (rs[:], I["ropeS"]),
                                (gq[:], I["q_gain"].to_broadcast([P, 2, 64])),
                                (gk[:], I["k_gain"].to_broadcast([P, 2, 64]))])
                head_norm_rope_phase(nc, T, q, k, rc[:], rs[:], gq, gk, qT, kT)
            oaT = q[:].rearrange("p t (h s) -> p (t h) s", s=S)
            with nc.sbuf_tensor("lam_rows", [P, 256], F32) as lr, nc.sbuf_tensor("lam_prod", [P, 128], F32) as lp, \
                    nc.sbuf_tensor("lam_two", [P, 2, 2], F32) as l2, nc.sbuf_tensor("lam_neg", [P, 1], F32) as ln, \
                    nc.sbuf_tensor("og", [P, 1], F32) as og:
                load_phase(nc, [(lr[:], I["diff_lambda"].to_broadcast([P, 256])), (og[:], I["diff_out_g"])])
                diff_attention_phase(nc, T, qT, kT, v, {"rows": lr, "prod": lp, "two": l2, "neg": ln}, og, oaT,
                                     k[:, 0:ST, :])
            move_phase([(oaT_d, oaT)])

        with ExitStack() as proj:
            def sbp(name, shape, dt=F32):
                return proj.enter_context(nc.sbuf_tensor(name, shape, dt))
            zr, zk, zv = sbp("zr", [P, DC, S]), sbp("zk", [P, DC, N_ALL]), sbp("zv", [P, DC, N_ALL])
            shift = sbp("shift", [P, 26, 3])
            lo2 = sbp("lo2", [P, 2, N_ALL])
            load_phase(nc, [(shift[:], I["rw_shift"])])

            def shifted(j, dst):
                def evac(ch, acc):
                    n = dst.shape[1]
                    ch.after(nc.vector.tensor_scalar(dst, acc, shift[:, j, 1:2], None, ALU.mult))
                    ch.after(nc.vector.scalar_tensor_tensor(dst[:, 1:n], acc[:, 0:n - 1], shift[:, j, 0:1], dst[:, 1:n],
                                                            ALU.mult, ALU.add))
                    return nc.vector.scalar_tensor_tensor(dst[:, 0:n - 1], acc[:, 1:n], shift[:, j, 2:3],
                                                          dst[:, 0:n - 1], ALU.mult, ALU.add)
                return evac

            def channels(first, dst, tiles, with_ctx):
                def groups(w):
                    res = []
                    for i in range(tiles):
                        j = first + i
                        o = dst(i)
                        spans = ([(0, CTX)] if with_ctx else []) + [(CTX, N_ALL)]
                        for lo, hi in spans:
                            at = lo if with_ctx else lo - CTX
                            res.append((P, hi - lo, [(w[:, c, i * P:(i + 1) * P], hT[:, c, lo:hi]) for c in range(DC)],
                                        shifted(j, o[:, at:at + hi - lo]), "v"))
                    return res
                return groups
            blocks = [(W[6 + b], channels(4 * b, lambda i, b=b: zr[:, 4 * b + i], 4, False)) for b in range(2)]
            blocks += [(W[8 + b], channels(8 + 4 * b, lambda i, b=b: zk[:, 4 * b + i], 4, True)) for b in range(2)]
            blocks += [(W[10 + b], channels(16 + 4 * b, lambda i, b=b: zv[:, 4 * b + i], 4, True)) for b in range(2)]
            blocks += [(I["w_lora"], channels(24, lambda i: lo2[:, i], 2, True))]
            gemm_phase(nc, psum, blocks, raw_ring=2)
            with Phase(nc, ["spilled"]) as (block, spilled):
                @block.sync
                def _(sp):
                    for dst, src in ((z_d["r"], zr), (z_d["k"], zk), (z_d["v"], zv)):
                        sp.dma_start(dst.rearrange("c p n -> p c n"), src[:]).then_inc(spilled, 16)
                    sp.wait_ge(spilled, 48)

                @block.scalar
                def _(act):
                    nc.scalar.activation(lora[0:64, :], lo2[0:64, 0, :], ACT.Tanh)
                    nc.scalar.copy(lora[64:P, :], lo2[64:P, 0, :])
                    nc.scalar.activation(gd[:], lo2[:, 1, CTX:], ACT.Sigmoid)

    obT = sbt("obT", [P, DC, S])
    with ExitStack() as rw:
        def sb(name, shape, dt=F32):
            return rw.enter_context(nc.sbuf_tensor(name, shape, dt))
        cst = {n: sb("rwc_" + n, list(I["rwc_" + n].shape)) for n in T["rwc_names"]}
        load_phase(nc, [(cst[n][:], I["rwc_" + n]) for n in cst])
        wide_shape = [P, 2, NCH, 2, L_CH]
        R = {"cst": cst, "z": sb("z", [P, 3, N_ALL]), "prm": sb("prm", [P, 10]), "up": sb("up", [P, 2, P]),
             "gup": sb("gup", [P, P]), "gd": gd[:], "area": None, "pl": sb("pl", [P, 2, NCH]),
             "zr_d": z_d["r"], "zk_d": z_d["k"], "zv_d": z_d["v"]}
        R["qr"] = sb("qr", [P, 2, NCH, 2, L_CH])[:]
        A1 = sb("room_bk", [P, 4 * N_ALL])
        R["bt"] = A1[:, 0:2 * N_ALL].rearrange("p (d n) -> p d n", d=2)
        R["kt"] = A1[:, 2 * N_ALL:].rearrange("p (d n) -> p d n", d=2)
        R["wXT"] = A1[:, :].rearrange("p (d c h t) -> p d c h t", d=2, c=NCH, h=2)
        A2 = sb("room_ab", [P, 8 * N_ALL])
        R["tmp"] = A2[:, :].rearrange("p (i n) -> p i n", i=8)
        R["wAT"] = A2[:, 0:4 * N_ALL].rearrange("p (d c h t) -> p d c h t", d=2, c=NCH, h=2)
        R["wBT"] = A2[:, 4 * N_ALL:].rearrange("p (d c h t) -> p d c h t", d=2, c=NCH, h=2)
        A3 = sb("room_turned", [P, 4 * N_ALL])
        R["eQ"], R["eR"], R["eK"] = (A3[:, i * N_ALL:(i + 1) * N_ALL] for i in range(3))
        R["wbt"] = A3[:, :].rearrange("p (d c h t) -> p d c h t", d=2, c=NCH, h=2)
        R["wkt"] = sb("wkt", wide_shape)[:]
        R["wq"] = sb("wq", wide_shape)[:]
        A4 = sb("room_wb", [P, 4 * N_ALL])
        R["wb"] = A4[:, :].rearrange("p (d c h t) -> p d c h t", d=2, c=NCH, h=2)
        R["wU"] = R["wb"]
        A5 = sb("room_wk", [P, 4 * N_ALL])
        R["wk"] = A5[:, :].rearrange("p (d c h t) -> p d c h t", d=2, c=NCH, h=2)
        R["zt"] = R["wk"]
        R["fin"] = A5[:, 0:4 * S].rearrange("p (i n) -> p i n", i=4)
        R["y_rows"] = A5[0:L_CH, 4 * S:6 * S]
        R["wX"] = sb("wX", wide_shape)[:]
        R["wv"] = A1[:, 2 * N_ALL:].rearrange("p (c h t) -> p c h t", c=NCH, h=2)
        R["C"], R["D"] = sb("Cc", [P, 2, XCH, L_CH])[:], sb("Dd", [P, 2, XCH, L_CH])[:]
        R["wV"] = sb("wV", [P, NCH, 2, L_CH])[:]
        R["wS"], R["wW"], R["wN"] = sb("wS", [P, 2, P])[:], *(
            A4[:, i * 2 * P:(i + 1) * 2 * P].rearrange("p (d m) -> p d m", d=2) for i in range(2))
        with Phase(nc, ["zeroed"]) as (block, zeroed):
            @block.vector
            def _(dve):
                nc.vector.memset(R["qr"][:, :, 0:CCH, 1, :], 0.0).then_inc(zeroed, 1)
        with nc.Fori(0, DC) as g:
            rwkv_tile(nc, T, g, R, lora, obT)

    with ExitStack() as mg:
        def sb(name, shape, dt=F32):
            return mg.enter_context(nc.sbuf_tensor(name, shape, dt))
        operand = sbuf_split(mg, nc, "merge_operand", [P, DC, S])
        zg = sb("zg", [P, 2 * DC, S])
        m = sb("merged", [P, DC, S])
        mt = sb("merge_tmp", [P, 2, S])
        split_phase(nc, m, operand, source=hT_d)

        def open_gate(b):
            def groups(w):
                return [(P, S, [(w[:, c, j * P:(j + 1) * P], operand[:, c, :]) for c in range(DC)],
                         lambda ch, acc, j=j: nc.scalar.activation(zg[:, 4 * b + j, :], acc, ACT.Sigmoid), "a")
                        for j in range(4)]
            return groups

        def branch(b, which):
            def groups(w):
                def evac(j):
                    k = 4 * b + j

                    def first(ch, acc):
                        return nc.vector.tensor_tensor(m[:, k, :], acc, zg[:, k, :], ALU.mult)

                    def second(ch, acc):
                        ch.after(nc.vector.tensor_tensor(mt[:, 0, :], acc, zg[:, DC + k, :], ALU.mult))
                        return nc.vector.tensor_tensor(m[:, k, :], m[:, k, :], mt[:, 0, :], ALU.add)
                    return second if which else first
                return [(P, S, [(w[:, c, j * P:(j + 1) * P], operand[:, c, :]) for c in range(DC)], evac(j), "v")
                        for j in range(4)]
            return groups

        def project(half):
            def groups(w):
                def evac(t):
                    def f(ch, acc):
                        o = x[:, t, half * NB:(half + 1) * NB]
                        ch.after(nc.vector.tensor_tensor(mt[:, 1, :], acc,
                                                         T["gate_rows"][:, 0, half * NB:(half + 1) * NB], ALU.mult))
                        return nc.vector.tensor_tensor(o, o, mt[:, 1, :], ALU.add)
                    return f
                return [(P, NB, [(operand[:, c, t * P:(t + 1) * P], w[:, c, :]) for c in range(DC)], evac(t), "v")
                        for t in range(ST)]
            return groups
        gemm_phase(nc, psum, [(I["w_in_2"][12 + b], open_gate(b)) for b in range(4)])
        split_phase(nc, m, operand, source=oaT_d)
        gemm_phase(nc, psum, [(I["w_branch_a"][b], branch(b, 0)) for b in range(2)])
        split_phase(nc, obT, operand)
        gemm_phase(nc, psum, [(I["w_branch_b"][b], branch(b, 1)) for b in range(2)])
        split_phase(nc, m, operand)
        gemm_phase(nc, psum, [(I["w_out_2"][b], project(b)) for b in range(2)])
    top.close()
    peer_phases(nc, T, x, out)


def program(nc, I, consts, out):
    with ExitStack() as ctx:
        def sb(name, shape, dt=F32):
            return ctx.enter_context(nc.sbuf_tensor(name, shape, dt))
        T = {"in": I, "psum": ctx.enter_context(nc.psum_tensor("psum", [P, BANKS, 512], F32)),
             "rwc_names": [n[4:] for n in I if n.startswith("rwc_")]}
        T["x"] = sb("x", [P, ST, D])
        T["ident"] = sb("ident_sb", [P, P])
        T["stats"] = sb("stats", [P, 4, ST])
        T["one"] = sb("one", [P, 1])
        with ExitStack() as first:
            def sbf(name, shape, dt=F32):
                return first.enter_context(nc.sbuf_tensor(name, shape, dt))
            for name, a in consts.items():
                if name != "ident":
                    T[name] = sbf(name + "_sb", list(a.shape))
            T["cols"] = sbf("cols", [P, 16])
            T["taps"] = sbf("taps", [P, 40])
            T["gate_b"] = sbf("gate_b", [P, 1])
            T["hng"] = sbf("hng", [P, 512])
            load_phase(nc, [(T[n][:], a) for n, a in consts.items()] + [(T["x"][:], I["x"])])
            with Phase(nc, ["ones_set"]) as (block, ones_set):
                @block.vector
                def _(dve):
                    nc.vector.memset(T["one"][:], 1.0).then_inc(ones_set, 1)
            with nc.Fori(0, DEPTH) as l:
                hybrid_layer(nc, l, T)
            with nc.sbuf_tensor("fg", [P, D], F32) as fg, nc.sbuf_tensor("final_scr", [P, 2, D], F32) as fscr:
                load_phase(nc, [(fg[:], I["final_g"].to_broadcast([P, D]))])
                norm_phase(nc, T["psum"], T["ident"], T["x"], ST,
                           (fscr[:], None), T["stats"], None,
                           write_back=fg[:])
        T["gate_rows"] = sb("gate_rows", [P, 2, D])
        T["affine"] = sb("affine", [P, 3, 2, DC])
        T["rwc"] = None
        second_block_program(nc, T, out)


def lay_out(v):
    import numpy as np
    A = {k: np.asarray(a) for k, a in v.items()}
    c = np.ascontiguousarray
    L = DEPTH

    def blocks(w, nb):
        K, N = w.shape[1:]
        return c(w.reshape(w.shape[0], K // P, P, N // nb, nb).transpose(0, 3, 2, 1, 4))

    def cols(g):
        return c(g.reshape(g.shape[0], -1, P).transpose(0, 2, 1))
    w = A["w_in"]
    gates, gate_b = np.zeros((L, D, P), w.dtype), np.zeros((L, 4, 32), w.dtype)
    gates.reshape(L, D, 4, 32)[..., 0:4] = w[:, :, 2048:2064].reshape(L, D, 4, 4)
    gate_b[:, 0:2, 0:4] = A["gate_i_b"].reshape(L, 2, 4)
    gate_b[:, 2:4, 0:4] = A["gate_f_b"].reshape(L, 2, 4)
    out = {
        "x": c(A["x"][0].reshape(ST, P, D).transpose(1, 0, 2)),
        "norm1_g": cols(A["norm1_g"]), "norm2_g": cols(A["norm2_g"]),
        "w_in": blocks(np.concatenate([w[:, :, 0:2048], w[:, :, 2064:]], axis=2), NB),
        "w_gates": blocks(gates, P)[:, 0],
        "conv_w": c(A["conv_w"].reshape(L, 5, 8, P).transpose(0, 3, 1, 2).reshape(L, P, 40)),
        "gate_b": gate_b.reshape(L, P, 1),
        "head_norm_g": A["head_norm_g"].reshape(L, 1, 512),
        "w_out": blocks(A["w_out"], NB),
        "w_up": blocks(A["w_up"], NB),
        "w_down": c(A["w_down"].reshape(L, 4, DC, P, 2, NB).transpose(0, 4, 1, 3, 2, 5)),
        "final_g": A["final_g"].reshape(1, D),
    }
    W = A["w_in_2"]
    order = np.concatenate([W[:, :, 0:6144], W[:, :, 6400:8448]], axis=2)
    out.update({
        "c": c(np.stack([A["c_2"][0], A["c_ctx_2"]], 1).reshape(DC, P, 2).transpose(1, 0, 2)),
        "ctx": c(A["ctx_2"][0].reshape(CT, P, D).transpose(1, 0, 2)),
        "w_mod": blocks(A["w_mod_2"], NB)[0],
        "b_mod": c(A["b_mod_2"][0].reshape(6, DC, P).transpose(2, 0, 1)),
        "b_mod_rows": A["b_mod_2"],
        "norm1_g_2": cols(A["norm1_g_2"])[0], "norm2_g_2": cols(A["norm2_g_2"])[0],
        "w_in_2": blocks(order, NB)[0],
        "w_lora": blocks(W[:, :, 6144:6400], 256)[0, 0],
        "diff_lambda": A["diff_lambda_2"].reshape(1, 256),
        "diff_out_g": A["diff_out_g_2"].reshape(P, 1),
        "rw_shift": c(A["rw_shift_2"][0].reshape(3, 26, P).transpose(2, 1, 0)),
        "rw_cols": c(np.stack([A["rw_w0_2"][0, 0], A["rw_w0_2"][0, 1], A["rw_a0_2"][0, 0], A["rw_a0_2"][0, 1],
                               A["rw_k_k_2"][0], A["rw_k_a_2"][0], A["rw_r_k_2"][0].reshape(-1), A["rw_ln_g_2"][0],
                               A["rw_ln_b_2"][0]], 1).reshape(DC, P, 9)),
        "rw_up": c(np.concatenate([A["rw_w_up_2"][0].transpose(1, 0, 2), A["rw_a_up_2"][0].transpose(1, 0, 2)], 0)
                   .reshape(P, 2, DC, P).transpose(2, 0, 1, 3)),
        "rw_gup": c(A["rw_g_up_2"][0].reshape(P, DC, P).transpose(1, 0, 2)),
        "w_branch_a": blocks(A["w_branch_a_2"], NB)[0], "w_branch_b": blocks(A["w_branch_b_2"], NB)[0],
        "w_out_2": blocks(A["w_out_2"], NB)[0],
        "peer_wq": blocks(A["peer_wq_2"], NB)[0],
        "peer_keys": c(A["peer_keys_2"][0].reshape(2 * PEER_HEADS, N_KEYS, P).transpose(2, 0, 1)),
        "peer_uv": c(np.concatenate([A["peer_u_2"][0], A["peer_v_2"][0]], axis=1)),
        "iota16": np.broadcast_to(np.arange(TOPK, dtype=np.float32), (P, TOPK)).copy(),
    })
    for n in ("q", "k"):
        g = A[f"{n}_norm_g_2"][0]
        swapped = g.reshape(2, 2, 16)[:, ::-1].reshape(64)
        out[n + "_gain"] = c(np.stack([g, swapped])[None])
    out.update(rope_constants())
    out.update({"rwc_" + n: a for n, a in rwkv_constants().items()})
    return out


def kernel(**v):
    import numpy as np
    import concourse.bacc as bacc
    from concourse import mybir as mb
    from concourse.bass_utils import run_bass_kernel_spmd as run
    nc = bacc.Bacc("TRN2", target_bir_lowering=False, num_devices=1)
    arrays, I, C = {}, {}, {}
    for group, dst in ((lay_out(v), I), (constants(), C)):
        for name, a in group.items():
            arrays["in_" + name] = np.ascontiguousarray(a)
            dst[name] = nc.dram_tensor("in_" + name, a.shape, mb.dt.from_np(a.dtype), kind="ExternalInput").ap()
    o = nc.dram_tensor("out_0", (P, ST, D), F32, kind="ExternalOutput").ap()
    program(nc, I, C, o)
    r = run(nc, [arrays], core_ids=[0]).results[0]["out_0"]
    return r.transpose(1, 0, 2).reshape(1, S, D)
```
